# Optimizing a Trainium2 kernel written in Bass

```python
import math
import jax, jax.numpy as jnp
from jax import lax
import numpy as np

D_MODEL = 1024
BATCH = 1
SEQ = 1024
DEPTH = 1
DEC_BATCH = 8
DEC_SEQ = 8
PAST_LEN = 4096
PAGE_SIZE = 128

HEAD_DIM = 64
A_HEADS = 8
B_HEADS = 8
A_WIDTH = A_HEADS * HEAD_DIM
B_WIDTH = B_HEADS * HEAD_DIM
MIX_WIDTH = A_WIDTH + B_WIDTH
CHUNK = 128
IDX_HEADS = 8
IDX_DIM = 64
TOPK_MAX = 256
D_FF = 2816
CONV_W = 3
N_BUCKETS = 32
MAX_DISTANCE = 128
RMS_EPS = 1e-6
Q_BLOCK = 128
NEG = -1e30
IN_SIZES = (A_WIDTH, A_WIDTH, B_WIDTH, B_WIDTH, B_WIDTH, IDX_HEADS * IDX_DIM, IDX_HEADS, IDX_DIM)
IN_WIDTH = 2 * A_WIDTH + 3 * B_WIDTH + IDX_HEADS * IDX_DIM + IDX_HEADS + IDX_DIM

kernel_name = "hybrid_chunkmlp_dsa_convffn_step"

def rmsnorm(x, g):
    xf = x.astype(jnp.float32)
    y = xf * lax.rsqrt(jnp.mean(xf * xf, axis=-1, keepdims=True) + RMS_EPS)
    return (y * g.astype(jnp.float32)).astype(x.dtype)

def split_projection(xn, w_in):
    z = jnp.einsum('btd,de->bte', xn, w_in)
    offs = [int(o) for o in np.cumsum(IN_SIZES)[:-1]]
    ua, va, q, k, v, iq, iw, ik = jnp.split(z, offs, axis=-1)
    b, t = z.shape[0], z.shape[1]
    return (ua.reshape(b, t, A_HEADS, HEAD_DIM), va.reshape(b, t, A_HEADS, HEAD_DIM),
            q.reshape(b, t, B_HEADS, HEAD_DIM), k.reshape(b, t, B_HEADS, HEAD_DIM),
            v.reshape(b, t, B_HEADS, HEAD_DIM), iq.reshape(b, t, IDX_HEADS, IDX_DIM), iw, ik)

def chunk_mlp_mix(ua, va, w_s, b_s):
    b, t = ua.shape[0], ua.shape[1]
    u = jax.nn.gelu(ua)
    vg = jax.nn.gelu(va).astype(jnp.float32)
    vn = (vg * lax.rsqrt(jnp.mean(vg * vg, axis=-1, keepdims=True) + RMS_EPS)).astype(ua.dtype)
    pad = (-t) % CHUNK
    vp = jnp.pad(vn, ((0, 0), (0, pad), (0, 0), (0, 0)))
    n_c = (t + pad) // CHUNK
    vc = vp.reshape(b, n_c, CHUNK, A_HEADS, HEAD_DIM)
    w = w_s * jnp.tril(jnp.ones((CHUNK, CHUNK), w_s.dtype))[None]
    s = jnp.einsum('hts,bcshd->bcthd', w, vc) + jnp.transpose(b_s)[None, None, :, :, None]
    s = s.reshape(b, n_c * CHUNK, A_HEADS, HEAD_DIM)[:, :t]
    return (u * s).reshape(b, t, A_WIDTH), vn

def rel_bucket(dist):
    n = jnp.maximum(dist, 0)
    max_exact = N_BUCKETS // 2
    nf = jnp.maximum(n, 1).astype(jnp.float32)
    large = max_exact + (jnp.log(nf / max_exact) / math.log(MAX_DISTANCE / max_exact)
                         * (N_BUCKETS - max_exact)).astype(jnp.int32)
    large = jnp.minimum(large, N_BUCKETS - 1)
    return jnp.where(n < max_exact, n, large)

def indexer_scores(iq, iw, ik):
    dots = jnp.einsum('bthd,bsd->bths', iq.astype(jnp.float32), ik.astype(jnp.float32)) * (IDX_DIM ** -0.5)
    return jnp.einsum('bths,bth->bts', jax.nn.relu(dots), iw.astype(jnp.float32) * (IDX_HEADS ** -0.5))

def select_keys(scores, q_pos, n_keys, k_sel):
    adm = jnp.arange(n_keys)[None, None, :] <= q_pos[None, :, None]
    _, idx = lax.top_k(jnp.where(adm, scores, NEG), k_sel)
    return idx

def sparse_attend(q, kg, vg, sel_pos, q_pos, rel_bias):
    logits = jnp.einsum('bthd,btkhd->bthk', q.astype(jnp.float32), kg.astype(jnp.float32)) * (HEAD_DIM ** -0.5)
    dist = q_pos[None, :, None] - sel_pos
    bias = rel_bias[rel_bucket(dist)].astype(jnp.float32)
    logits = logits + jnp.transpose(bias, (0, 1, 3, 2))
    logits = jnp.where((dist >= 0)[:, :, None, :], logits, NEG)
    p = jax.nn.softmax(logits, axis=-1)
    return jnp.einsum('bthk,btkhd->bthd', p.astype(vg.dtype), vg)

def sparse_attn_prompt(q, k, v, iq, iw, ik, rel_bias):
    b, s = q.shape[0], q.shape[1]
    k_sel = min(TOPK_MAX, s // 4)
    bidx = jnp.arange(b)[:, None, None]

    def block(i):
        start = i * Q_BLOCK
        qb = lax.dynamic_slice_in_dim(q, start, Q_BLOCK, axis=1)
        iqb = lax.dynamic_slice_in_dim(iq, start, Q_BLOCK, axis=1)
        iwb = lax.dynamic_slice_in_dim(iw, start, Q_BLOCK, axis=1)
        q_pos = start + jnp.arange(Q_BLOCK)
        idx = select_keys(indexer_scores(iqb, iwb, ik), q_pos, s, k_sel)
        kg = k[bidx, idx]
        vg = v[bidx, idx]
        return sparse_attend(qb, kg, vg, idx, q_pos, rel_bias)

    out = lax.map(block, jnp.arange(s // Q_BLOCK))
    return jnp.transpose(out, (1, 0, 2, 3, 4)).reshape(b, s, B_WIDTH)

def sparse_attn_sample(q, k_new, v_new, iq, iw, ik_new, cache_k, cache_v, cache_idx_k, layer, page_table, rel_bias):
    db, t = q.shape[0], q.shape[1]
    page_size = cache_k.shape[2]
    past = page_table.shape[1] * page_size
    n_keys = past + t
    k_sel = min(TOPK_MAX, n_keys // 4)
    ik_past = cache_idx_k[layer, page_table].reshape(db, past, IDX_DIM)
    ik_all = jnp.concatenate([ik_past, ik_new.astype(ik_past.dtype)], axis=1)
    q_pos = past + jnp.arange(t)
    idx = select_keys(indexer_scores(iq, iw, ik_all), q_pos, n_keys, k_sel)
    bidx = jnp.arange(db)[:, None, None]
    pidx = jnp.minimum(idx, past - 1)
    phys = page_table[bidx, pidx // page_size]
    row = pidx % page_size
    nidx = jnp.clip(idx - past, 0, t - 1)
    in_past = (idx < past)[..., None, None]
    kg = jnp.where(in_past, cache_k[layer, phys, row].astype(k_new.dtype), k_new[bidx, nidx])
    vg = jnp.where(in_past, cache_v[layer, phys, row].astype(v_new.dtype), v_new[bidx, nidx])
    return sparse_attend(q, kg, vg, idx, q_pos, rel_bias).reshape(db, t, B_WIDTH)

def conv_ffn(h, w_gate, w_up, conv_w, conv_b, w_down, conv_state):
    t = h.shape[1]
    g = jnp.einsum('btd,df->btf', h, w_gate)
    u = jnp.einsum('btd,df->btf', h, w_up)
    gp = jnp.concatenate([conv_state.astype(g.dtype), g], axis=1)
    gc = conv_b + sum(conv_w[j] * gp[:, j:j + t] for j in range(CONV_W))
    y = jnp.einsum('btf,fd->btd', jax.nn.silu(gc) * u, w_down)
    return y, gp[:, -(CONV_W - 1):]

def setup_inputs(seed: int = 0) -> dict:
    key = jax.random.key(seed)
    ks = jax.random.split(key, 24)
    f32 = jnp.float32
    n_pages = PAST_LEN // PAGE_SIZE
    n_used = DEC_BATCH * n_pages
    n_pool = n_used + max(1, n_used // 4)
    nrm = lambda k, shp, sc: jax.random.normal(k, shp, f32) * sc
    page_table = jax.random.permutation(ks[0], n_pool)[:n_used].reshape(DEC_BATCH, n_pages).astype(jnp.int32)
    return {
        "x_prompt": nrm(ks[1], (BATCH, SEQ, D_MODEL), 1.0),
        "x_sample": nrm(ks[2], (DEC_BATCH, DEC_SEQ, D_MODEL), 1.0),
        "cache_k": nrm(ks[3], (DEPTH, n_pool, PAGE_SIZE, B_HEADS, HEAD_DIM), 1.0),
        "cache_v": nrm(ks[4], (DEPTH, n_pool, PAGE_SIZE, B_HEADS, HEAD_DIM), 1.0),
        "cache_idx_k": nrm(ks[5], (DEPTH, n_pool, PAGE_SIZE, IDX_DIM), 1.0),
        "state_ffn_conv": nrm(ks[6], (DEPTH, DEC_BATCH, CONV_W - 1, D_FF), 1.0),
        "page_table": page_table,
        "norm1_g": 1.0 + nrm(ks[7], (DEPTH, D_MODEL), 0.05),
        "w_in": nrm(ks[8], (DEPTH, D_MODEL, IN_WIDTH), D_MODEL ** -0.5),
        "w_s": nrm(ks[9], (DEPTH, A_HEADS, CHUNK, CHUNK), CHUNK ** -0.5),
        "b_s": 1.0 + nrm(ks[10], (DEPTH, A_HEADS, CHUNK), 0.1),
        "rel_bias": nrm(ks[11], (N_BUCKETS, B_HEADS), 0.5),
        "w_o": nrm(ks[12], (DEPTH, MIX_WIDTH, D_MODEL), MIX_WIDTH ** -0.5),
        "norm2_g": 1.0 + nrm(ks[13], (DEPTH, D_MODEL), 0.05),
        "w_gate": nrm(ks[14], (DEPTH, D_MODEL, D_FF), D_MODEL ** -0.5),
        "w_up": nrm(ks[15], (DEPTH, D_MODEL, D_FF), D_MODEL ** -0.5),
        "conv_w": nrm(ks[16], (DEPTH, CONV_W, D_FF), CONV_W ** -0.5),
        "conv_b": nrm(ks[17], (DEPTH, D_FF), 0.02),
        "w_down": nrm(ks[18], (DEPTH, D_FF, D_MODEL), D_FF ** -0.5),
        "final_g": 1.0 + nrm(ks[19], (D_MODEL,), 0.05),
    }

def reference(x_prompt, x_sample, cache_k, cache_v, cache_idx_k, state_ffn_conv, page_table,
              norm1_g, w_in, w_s, b_s, rel_bias, w_o, norm2_g, w_gate, w_up, conv_w, conv_b,
              w_down, final_g):
    hp, hs = x_prompt, x_sample
    kp_l, vp_l, ikp_l, cp_l = [], [], [], []
    ks_l, vs_l, iks_l, cs_l, avs_l = [], [], [], [], []
    for l in range(DEPTH):
        ua, va, q, k, v, iq, iw, ik = split_projection(rmsnorm(hp, norm1_g[l]), w_in[l])
        a_out, _ = chunk_mlp_mix(ua, va, w_s[l], b_s[l])
        b_out = sparse_attn_prompt(q, k, v, iq, iw, ik, rel_bias)
        hp = hp + jnp.einsum('bte,ed->btd', jnp.concatenate([a_out, b_out], axis=-1), w_o[l])
        zero_state = jnp.zeros((hp.shape[0], CONV_W - 1, D_FF), hp.dtype)
        f, conv_p = conv_ffn(rmsnorm(hp, norm2_g[l]), w_gate[l], w_up[l], conv_w[l], conv_b[l], w_down[l], zero_state)
        hp = hp + f
        kp_l.append(k); vp_l.append(v); ikp_l.append(ik); cp_l.append(conv_p)
        ua, va, q, k, v, iq, iw, ik = split_projection(rmsnorm(hs, norm1_g[l]), w_in[l])
        a_out, v_chunk = chunk_mlp_mix(ua, va, w_s[l], b_s[l])
        b_out = sparse_attn_sample(q, k, v, iq, iw, ik, cache_k, cache_v, cache_idx_k, l, page_table, rel_bias)
        hs = hs + jnp.einsum('bte,ed->btd', jnp.concatenate([a_out, b_out], axis=-1), w_o[l])
        f, conv_s = conv_ffn(rmsnorm(hs, norm2_g[l]), w_gate[l], w_up[l], conv_w[l], conv_b[l], w_down[l], state_ffn_conv[l])
        hs = hs + f
        ks_l.append(k); vs_l.append(v); iks_l.append(ik); cs_l.append(conv_s); avs_l.append(v_chunk)
    y_prompt = rmsnorm(hp, final_g)
    y_sample = rmsnorm(hs, final_g)
    return (y_prompt, y_sample,
            jnp.stack(kp_l), jnp.stack(vp_l), jnp.stack(ikp_l), jnp.stack(cp_l),
            jnp.stack(ks_l), jnp.stack(vs_l), jnp.stack(iks_l), jnp.stack(cs_l), jnp.stack(avs_l))


_drawn_inputs = setup_inputs


def setup_inputs(seed=0):
    import zlib

    import numpy as np

    out = dict(_drawn_inputs(seed))
    spreads = {}
    factors = {'conv_b': 5.9}
    for name, (base, spread) in spreads.items():
        noise = np.random.default_rng([zlib.crc32(name.encode()), seed]).standard_normal(out[name].shape)
        drawn = base * np.exp(spread * noise) if base else spread * noise
        out[name] = __import__('jax').numpy.asarray(drawn.astype(out[name].dtype))
    for name, factor in factors.items():
        out[name] = (out[name] * factor).astype(out[name].dtype)
    return out
```

```python
from contextlib import ExitStack

import numpy as np
import concourse.bass as bass
from concourse import mybir

F32 = mybir.dt.float32
I32 = mybir.dt.int32
U32 = mybir.dt.uint32
ALU = mybir.AluOpType
ACT = mybir.ActivationFunctionType
AX_X = mybir.AxisListType.X

P = 128
D = 1024
KD = D // P
SEQ = 1024
NT = SEQ // P
SB, ST = 8, 8
SROWS = SB * ST
TILES = NT + 1
TOK = SEQ + SROWS
H, HD = 8, 64
W = H * HD
PAIRS = H // 2
PAGE = 128
NPAGES = 32
PAST = PAGE * NPAGES
TOPK = 256
DFF = 2816
NF = DFF // P
BUCKETS = 32
EPS = 1e-6
NEG = -1e30
TAKEN = -3e38
HALF = PAST // 2
SCORES = HALF + SROWS
GROUPS = ((0, 363), (363, 726), (726, TOK))
DSLOTS = 15
NEAR = 3 * P

CHUNKS = [("small", 6 * W, H + HD), ("iq", 5 * W, W), ("q", 2 * W, W), ("k", 3 * W, W), ("v", 4 * W, W),
          ("ua", 0, W), ("va", W, W)]
VEC_ROWS = [("g1", KD), ("g2", KD), ("cw", 3 * NF), ("cb", NF), ("bs", H)]


_DIST = np.arange(1, 4 * P, dtype=np.float32)
_LARGE = BUCKETS // 2 + (np.log(_DIST / np.float32(BUCKETS // 2)) / np.float32(np.log(128 / (BUCKETS // 2)))
                         * np.float32(BUCKETS // 2)).astype(np.int32)
BUCKET_OF = np.concatenate([[0], np.where(_DIST < BUCKETS // 2, _DIST.astype(np.int32), np.minimum(_LARGE, BUCKETS - 1))])
FIRST_OF = [int(np.argmax(BUCKET_OF == k)) for k in range(BUCKETS)]


def reverse(x):
    (step, rows), (_, n) = x.ap
    return bass.AP(tensor=x.tensor, offset=x.offset + n - 1, ap=[[step, rows], [-1, n]])


def rows_of(t):
    return P if t < NT else SROWS


def program(nc, io):
    ctx = ExitStack()
    with ctx:
        arena = ctx.enter_context(nc.sbuf_tensor("arena", [P, 52900], F32))
        ps = ctx.enter_context(nc.psum_tensor("ps", [P, 8, 512], F32))
        ptab = ctx.enter_context(nc.sbuf_tensor("ptab", [1, SB * NPAGES], I32))

        def sem(name):
            return ctx.enter_context(nc.semaphore(name))

        at = {}
        top = [0]

        def region(name, cols):
            at[name] = top[0]
            top[0] += cols
            assert top[0] <= 52900, (name, top[0])

        def view(name, cols, off=0):
            return arena[:, at[name] + off:at[name] + off + cols]

        region("xT", KD * TOK)
        region("wring", 2 * KD * W)
        region("scd", SCORES)
        region("lists", 2560)
        region("rbuf", 2048)
        region("wd", 1088)
        region("iqd", 512)
        region("qbd", 512)
        region("qT", PAIRS * TOK)
        region("kT", PAIRS * TOK)
        region("iqT", TILES * W)
        region("ikc", 5120)
        region("score", 4224)
        region("z", 3 * W)
        region("ikT", TOK)
        region("ident", P)
        region("cols", 112)
        region("stats", 512)
        region("causal", 2 * P)
        region("own", SROWS)
        region("iw", TILES * H)
        region("scn", SROWS)
        region("bias31", H)
        region("idx", P)
        region("small", 256)

        xT = view("xT", KD * TOK).rearrange("p (c t) -> p c t", c=KD)
        wring = view("wring", 2 * KD * W).rearrange("p (s n) -> p s n", s=2)
        qT = view("qT", PAIRS * TOK).rearrange("p (c t) -> p c t", c=PAIRS)
        kT = view("kT", PAIRS * TOK).rearrange("p (c t) -> p c t", c=PAIRS)
        iqT = view("iqT", PAIRS * TOK).rearrange("p (c t) -> p c t", c=PAIRS)
        ikT = view("ikT", TOK)
        u = view("iqT", TILES * W).rearrange("p (t n) -> p t n", t=TILES)
        vn = view("ikc", TILES * W).rearrange("p (t n) -> p t n", t=TILES)
        xring = view("ikc", 3 * D).rearrange("p (s n) -> p s n", s=3)
        ikc = view("ikc", 2048).rearrange("p (s j e d) -> p s j e d", s=2, e=2, d=HD)
        ikcT = view("ikc", 2048, 2048).rearrange("p (s n) -> p s n", s=2)
        zr = view("z", 3 * W).rearrange("p (s n) -> p s n", s=3)
        rb = view("rbuf", 2048).rearrange("p (s n) -> p s n", s=2)
        twice = view("rbuf", 1024, 1024)
        wd = view("wd", 1024).rearrange("p (b n) -> p b n", b=SB)
        iqd = view("iqd", 512).rearrange("p (b n) -> p b n", b=SB)
        qbd = view("qbd", 512).rearrange("p (b c n) -> p b c n", b=SB, c=PAIRS)
        scd = view("scd", SCORES)
        sc_off = {}
        o = 0
        for i in range(2, NT):
            sc_off[i] = o
            o += (i + 1) * P
        ident = view("ident", P)
        near_mask = view("causal", 2 * P)
        causal = view("causal", P, P)
        own = view("own", SROWS)
        cols = view("cols", 112)
        col_at, o = {}, 0
        for name, n in VEC_ROWS:
            col_at[name] = o
            o += n
        g1 = cols[:, col_at["g1"]:col_at["g1"] + KD]
        iw = view("iw", TILES * H).rearrange("p (t h) -> p t h", t=TILES)
        stats = view("stats", 512)
        ssq, std, rstd = stats[:, 0:9], stats[:, 16:25], stats[:, 32:41]
        epsc = stats[:, 48:49]
        m8 = stats[:, 64:72]
        bsd = stats[0:SROWS, 80:88]
        vss = stats[:, 96:168].rearrange("p (t h) -> p t h", t=TILES)
        minus_half = stats[:, 49:50]
        bs = cols[:, col_at["bs"]:col_at["bs"] + H]
        rb4 = view("rbuf", 2048).rearrange("p (s n) -> p s n", s=4)
        ws_in = view("rbuf", 1024).rearrange("p (h s) -> p h s", h=H)
        wsT = view("wd", 1024).rearrange("p (h t) -> p h t", h=H)
        wsd = view("iqd", 512).rearrange("p (h t) -> p h t", h=H)
        mixT = view("xT", KD * TOK).rearrange("p (c t) -> p c t", c=KD)
        scn = view("scn", SROWS)
        b31 = view("bias31", H)
        val, pos = view("lists", TOPK), view("lists", TOPK, TOPK)
        val_b, pos_b = view("lists", TOPK, 2 * TOPK), view("lists", TOPK, 3 * TOPK)
        low, page_of, rows_f, turn_f = (view("lists", TOPK, (4 + i) * TOPK) for i in range(4))
        int_a = view("lists", TOPK, 8 * TOPK)
        int_b = view("lists", TOPK, 9 * TOPK)
        idx4 = view("small", 8).bitcast(I32).rearrange("p (s c) -> p s c", s=4)
        sel_new = view("small", ST, 8)
        row_t, row_new = view("small", 1, 16), view("small", 1, 17)
        neg_max = view("small", 2, 18)
        top_col = view("small", 4, 20)
        i8 = view("small", 8, 24).bitcast(U32)
        ptab_f = view("small", NPAGES, 32)
        ptab_i = view("small", NPAGES, 64).bitcast(I32)
        sel_new2 = view("small", ST, 160)
        new_bias = view("small", SROWS, 168)
        new_mask = view("small", SROWS, 96)
        idxT = view("idx", P).bitcast(I32).rearrange("p (c r) -> p c r", c=2)
        distT = view("ikT", P, 4 * P)
        new_maskT = view("ikT", SROWS, 5 * P)
        steps = view("ikT", BUCKETS * H, 5 * P + SROWS).rearrange("p (k h) -> p k h", k=BUCKETS)
        reach = view("ikT", P, 5 * P + SROWS + BUCKETS * H)
        kv = view("wring", 4 * 2 * W).rearrange("p (s n) -> p s n", s=4)
        qrow = view("wring", 4 * W, 8 * W).rearrange("p (s n) -> p s n", s=4)
        prod = view("wring", 2 * W, 12 * W)
        ones = view("wring", P, 14 * W)
        diag = view("wring", 4 * P, 15 * W)
        lg = view("scd", 2 * W).rearrange("p (c n) -> p c n", c=2)
        ln = view("scd", W, 2 * W)
        mx = view("scd", W, 3 * W)
        pT = view("iqT", NT * SEQ).rearrange("p (k q) -> p k q", k=NT)
        rl = view("iqT", SEQ, NT * SEQ)
        vone = arena[:, at["z"]:at["z"] + 2 * NT * P].rearrange("p (s k n) -> p s k n", s=2, k=NT)
        bn = view("wd", 2 * P * H).rearrange("p (h u) -> p h u", h=H)
        toep_row = view("lists", NEAR)
        hot = view("lists", NEAR, NEAR)
        relb = view("lists", H, 2 * NEAR)
        def free(first, cols):
            return arena[:, first:first + cols]

        wo = view("wring", KD * D).rearrange("p (k n) -> p k n", k=KD)
        hx = free(at["qT"], TILES * D).rearrange("p (t n) -> p t n", t=TILES)
        tail = at["qT"] + TILES * D
        x2 = free(tail, 2 * D).rearrange("p (s n) -> p s n", s=2)
        hn = view("rbuf", 2 * D).rearrange("p (s n) -> p s n", s=2)
        hT = free(at["ikc"], KD * TOK).rearrange("p (c t) -> p c t", c=KD)
        after = at["ikc"] + KD * TOK
        wf = [free(o, 2 * KD * P).rearrange("p (w k n) -> p w k n", w=2, k=KD) for o in (after, tail + 2 * D)]
        st = free(after + 2 * D, NF * 2 * SB).rearrange("p (f s) -> p f s", f=NF)
        cs = free(after + 2 * D + NF * 2 * SB, NF * (2 + 2 * SB)).rearrange("p (f s) -> p f s", f=NF)
        aT = arena[:, 0:NF * TOK]
        gb = free(NF * TOK, 2 + SEQ + SB * (2 + ST))
        gb_p = gb[:, 0:2 + SEQ]
        gb_s = gb[:, 2 + SEQ:].rearrange("p (b t) -> p b t", b=SB)
        state_rows = view("scd", DFF)
        g2 = cols[:, col_at["g2"]:col_at["g2"] + KD]
        cw = cols[:, col_at["cw"]:col_at["cw"] + 3 * NF]
        cb = cols[:, col_at["cb"]:col_at["cb"] + NF]
        cs_rows = (free(NF * TOK, 14 * P), free(tail + 3 * D, 8 * P))
        final_g = free(NF * TOK, D)
        d_at = [tail, tail + D, tail + 2 * D] + [at["ikc"] + i * D for i in range(11)] + [tail + 3 * D]
        wdn = [free(o, D).rearrange("p (f n) -> p f n", f=2) for o in d_at]
        squares = free(NF * TOK + D, 512)
        hq, hr, yq, yr = stats[:, 200:209], stats[:, 216:225], stats[:, 232:250], stats[:, 256:265]
        q_dram = nc.dram_tensor("sampled_queries", (SROWS, W), F32, kind="Internal").ap()
        toep_dram = nc.dram_tensor("bias_by_distance", (H, P, NEAR), F32, kind="Internal").ap()
        o_dram = nc.dram_tensor("sampled_heads", (SROWS, H, H, HD), F32, kind="Internal").ap()
        rows_in = view("rbuf", P)
        wrep = view("scd", P)
        wsel = view("scd", ST, P)
        iwT = view("scd", SROWS, 2 * P)

        s_const = sem("consts_loaded")
        s_pt = sem("page_table_loaded")
        s_x = [sem(f"x_loaded{i}") for i in range(3)]
        s_w = [sem(f"w_loaded{i}") for i in range(2)]
        s_pool = sem("pool_step")
        s_built = sem("masks_built")
        s_ssq = sem("squares_summed")
        s_root = sem("root_mean_square_ready")
        s_dve = sem("dve_step")
        s_xn = sem("x_normed")
        s_xTp = sem("xT_in_psum")
        s_xT = sem("xT_ready")
        s_mm = sem("projection_done")
        s_z = sem("projection_evacuated")
        s_tz = sem("z_transposed")
        s_tev = sem("transposed_evacuated")
        s_zs = [sem(f"z_stored{i}") for i in range(3)]
        s_cps = sem("columns_in_psum")
        s_col = sem("columns_ready")
        s_twice = sem("index_queries_twice")
        s_dot = sem("index_dots_done")
        s_relu = sem("index_relu_done")
        s_sc = sem("index_relu_used")
        s_scm = sem("index_scores_masked")
        s_topk = sem("topk_done")
        s_iwp = sem("index_weights_in_psum")
        s_iwT = sem("index_weights_turned")
        s_wd = sem("head_sum_weights_ready")
        s_ikc = [sem(f"index_pages_loaded{i}") for i in range(2)]
        s_ct = sem("index_pages_turned")
        s_cT = sem("index_pages_evacuated")
        s_cd = sem("page_dots_done")
        s_cr = sem("page_relu_done")
        s_ch = sem("page_heads_summed")
        s_cs = sem("page_scores_evacuated")
        s_ws = sem("w_s_loaded")
        s_wsp = sem("w_s_turned")
        s_wse = sem("w_s_evacuated")
        s_wsc = sem("w_s_causal")
        s_wsd = sem("w_s_blocks_placed")
        s_vss = sem("gate_squares_summed")
        s_vn = sem("gate_normed")
        s_cv = sem("chunk_v_stored")
        s_sg = sem("spatial_gate_done")
        s_sb = sem("spatial_bias_added")
        s_au = sem("chunk_mlp_done")
        s_at = sem("chunk_mlp_turned")
        s_am = sem("chunk_mlp_evacuated")
        s_qbd = sem("query_blocks_ready")
        s_kn = sem("new_key_logits_done")
        s_ln = sem("new_key_logits_evacuated")
        s_rel = sem("bias_table_loaded")
        s_toep = sem("bias_by_distance_done")
        s_toev = sem("bias_by_distance_evacuated")
        s_tod = sem("bias_by_distance_stored")
        s_bn = sem("near_bias_loaded")
        s_b31 = sem("far_bias_loaded")
        s_rows = sem("row_numbers_loaded")
        s_scn = sem("own_scores_moved")
        s_list = sem("lists_ready")
        s_move = sem("second_list_moved")
        s_pick = sem("picked_rows_ready")
        s_pickT = sem("picked_rows_turned")
        s_idx = sem("gather_rows_ready")
        s_nmT = sem("new_mask_turned")
        s_kg = [sem(f"rows_gathered{i}") for i in range(4)]
        s_qr = [sem(f"query_row_loaded{i}") for i in range(4)]
        s_kd = sem("key_dots_done")
        s_S = sem("prompt_logits_done")
        s_L = sem("prompt_logits_masked")
        s_nbs = sem("own_bias_spread")
        s_nbT = sem("own_bias_turned")
        s_E = sem("prompt_exp_done")
        s_T = sem("prompt_probs_turned")
        s_Te = sem("prompt_probs_evacuated")
        s_vo = [sem(f"head_values_loaded{i}") for i in range(2)]
        s_pv = sem("prompt_heads_done")
        s_po = sem("prompt_heads_normalised")
        s_mxT = sem("sampled_max_turned")
        s_dg = sem("sampled_max_diagonal")
        s_mb = sem("sampled_max_spread")
        s_lm = sem("sampled_logits_shifted")
        s_le = sem("sampled_exp_done")
        s_ls = sem("sampled_sums_ready")
        s_lb = sem("sampled_sums_spread")
        s_pn = sem("sampled_probs_ready")
        s_vd = sem("sampled_heads_done")
        s_ve = sem("sampled_heads_evacuated")
        s_vs = [sem(f"sampled_heads_stored{i}") for i in range(2)]
        s_vnl = sem("new_values_loaded")
        s_nd = sem("new_key_heads_done")
        s_oh = sem("sampled_heads_loaded")
        s_os = sem("sampled_heads_summed")
        s_oT = sem("sampled_heads_turned")
        s_oTe = sem("sampled_heads_placed")

        s_wo = [sem(f"w_o_loaded{i}") for i in range(2)]
        s_x2 = [sem(f"residual_loaded{i}") for i in range(2)]
        s_mo = sem("w_o_products_done")
        s_h = sem("residual_added")
        s_hq = sem("residual_squares_summed")
        s_hn = sem("residual_normed")
        s_hp = sem("residual_turned")
        s_hT = sem("hT_ready")
        s_st = sem("conv_state_loaded")
        s_stp = sem("conv_state_turned")
        s_ste = sem("conv_state_evacuated")
        s_wf = [sem(f"ffn_weights_loaded{i}") for i in range(2)]
        s_gst = sem("conv_state_placed")
        s_gm = sem("gate_products_done")
        s_gc = sem("gate_evacuated")
        s_um = sem("up_products_done")
        s_cd2 = sem("conv_done")
        s_si = sem("silu_done")
        s_ag = sem("gated")
        s_cst = sem("new_conv_state_turned")
        s_cse = sem("new_conv_state_evacuated")
        s_cso = sem("new_conv_state_stored")
        s_fg = sem("final_gain_loaded")
        s_wdn = [sem(f"w_down_loaded{i}") for i in range(DSLOTS)]
        s_du = sem("w_down_used")
        s_dm = sem("down_products_done")
        s_y = sem("output_added")
        s_yq = sem("output_squares_summed")
        s_yn = sem("output_normed")
        s_yo = sem("output_stored")

        n_of = lambda c, t: c * TILES + t
        tjob = [(c, t) for c in range(4) for t in range(TILES)]
        tjob.insert(tjob.index((1, NT)) + 1, ("dup", NT))
        tjob_at = {job: i for i, job in enumerate(tjob)}
        zstores = {}
        for c, t in [(c, t) for c in (0, 2, 3, 4) for t in range(TILES) if c != 2 or t == NT]:
            slot = n_of(c, t) % 3
            zstores[(c, t)] = sum(1 for k in zstores if n_of(*k) % 3 == slot) + 1

        def page_numbers(eng, first, n):
            return nc.values_load_multi_w_load_instructions(ptab[0:1, bass.ds(first, n)], engines=(eng.engine,), min_val=0,
                                                            max_val=io["pool"] - 1)[1]

        out8 = view("rbuf", 2 * W)[0:H, :].rearrange("p (s n) -> p s n", s=2)

        def own_near(h):
            return view("rbuf", SROWS * H).rearrange("p (h n) -> p h n", h=H)[0:ST, h, :]

        def probs_groups(i):
            return [range(a, min(a + 4, i + 1)) for a in range(0, i + 1, 4)]

        def turned_after(m):
            h, i = divmod(m, NT)
            return h * sum(len(probs_groups(j)) for j in range(NT)) + sum(len(probs_groups(j)) for j in range(i + 1))

        def evacuate_probs(act, h, i, g):
            if h and i == 0:
                act.wait_ge(s_pv, h)
            for blocks in probs_groups(i):
                act.wait_ge(s_T, g + 1)
                n, a = len(blocks), blocks[0]
                nc.scalar.activation(pT[:, a:a + n, i * P:(i + 1) * P], ps[:, 4 + g % 2, 0:n * P].rearrange("p (k q) -> p k q", k=n),
                                     ACT.Copy).then_inc(s_Te, 1)
                g += 1
            return g

        block = ctx.enter_context(nc.Block())

        @block.sync
        def _(sp):
            sp.dma_start(ptab[:, :], io["page_table"].rearrange("(a b) n -> a (b n)", a=1)).then_inc(s_pt, 16)

            def load_x(t):
                if t >= 3:
                    sp.wait_ge(s_xTp, t - 2)
                src = io["x_prompt"][0, t * P:(t + 1) * P, :] if t < NT else io["x_sample"].rearrange("b t d -> (b t) d")
                sp.dma_start(xring[0:rows_of(t), t % 3, :], src).then_inc(s_x[t % 3], 16)

            def load_w(c):
                _, c0, width = CHUNKS[c]
                if c >= 2:
                    sp.wait_ge(s_mm, n_of(c - 1, 0))
                sp.dma_start(wring[:, c % 2, 0:KD * width].rearrange("p (k n) -> p k n", k=KD),
                             io["w_in"][0, :, c0:c0 + width].rearrange("(k p) n -> p k n", p=P)).then_inc(s_w[c % 2], 16)

            load_x(0)
            r = 0
            for name, n in VEC_ROWS:
                src = {"g1": io["norm1_g"], "g2": io["norm2_g"], "cw": io["conv_w"][0], "cb": io["conv_b"], "bs": io["b_s"][0]}[name]
                src = src if name == "bs" else src.rearrange("a (c p) -> (a c) p", p=P)
                sp.dma_start(rows_in[r:r + n, :], src).then_inc(s_const, 16)
                r += n
            sp.dma_start(wrep[0:H, :], io["c_rep"]).then_inc(s_const, 16)
            sp.dma_start(wsel[:, :], io["c_sel"]).then_inc(s_const, 16)
            load_x(1)
            load_x(2)
            for dst, src in ((relb[0:BUCKETS, :], io["rel_bias"]), (hot[0:BUCKETS, :], io["c_hot"])):
                sp.dma_start(dst, src).then_inc(s_rel, 16)
            sp.dma_start(b31, io["rel_bias"][BUCKETS - 1:BUCKETS, :].partition_broadcast(P)).then_inc(s_rows, 16)
            sp.dma_start(view("small", 2, 16)[0:SROWS, :], io["c_rows"]).then_inc(s_rows, 16)
            for b in range(SB):
                sp.dma_start(ptab_i[b * ST:(b + 1) * ST, :], io["page_table"][b:b + 1, :].partition_broadcast(ST)).then_inc(s_rows, 16)
            load_w(0)
            load_w(1)
            for t in range(3, TILES):
                load_x(t)
            load_w(2)
            sp.wait_ge(s_pt, 16)
            sp.wait_ge(s_xTp, TILES)

            def load_index_pages(b, first):
                for half in range(2):
                    for e in range(2):
                        for j, page in enumerate(page_numbers(sp, b * NPAGES + (e * 16 + half * 8), 8)):
                            if not first and (e, j) == (0, 0):
                                sp.wait_ge(s_ct, b * 2 + (half - 1))
                            sp.dma_start(ikc[:, half, j, e, :],
                                         io["cache_idx_k"][0, bass.ds(page, 1), :, :].rearrange("a p d -> (a p) d")).then_inc(s_ikc[half], 16)

            load_index_pages(0, True)
            load_w(3)
            with sp.Fori(1, SB) as b:
                load_index_pages(b, False)
            sp.wait_ge(s_scm, NT - 1)
            sp.dma_start(scd[SROWS:P, HALF:SCORES], scn[0:SROWS, :]).then_inc(s_scn, 16)
            sp.wait_ge(s_ch, 4 * SB)
            sp.dma_start(ws_in, io["w_s"][0].rearrange("h t s -> t h s")).then_inc(s_ws, 16)
            for c in range(4, 7):
                load_w(c)
            sp.wait_ge(s_wsc, 1)
            for b in range(SB):
                r = slice(b * ST, (b + 1) * ST)
                sp.dma_start(wsd[r, :, r], wsT[0:ST, :, 0:ST]).then_inc(s_wsd, 16)
                sp.dma_start(bsd[r, :], bs[0:ST, :]).then_inc(s_wsd, 16)

            sp.wait_ge(s_toev, 1)
            sp.dma_start(toep_dram, toep_row[0:H, :].unsqueeze(1).to_broadcast([H, P, NEAR])).then_inc(s_tod, 16)
            sp.wait_ge(s_tod, 16)
            sp.wait_ge(s_ln, 1)
            sp.dma_start(bn, bass.AP(tensor=toep_dram.tensor, offset=P - 1, ap=[[NEAR - 1, P], [P * NEAR, H], [1, 2 * P]])).then_inc(s_bn, 16)

            sp.wait_ge(s_list, 1)
            sp.dma_start(val_b[0:SROWS, :], val[SROWS:P, :]).then_inc(s_move, 16)
            sp.dma_start(pos_b[0:SROWS, :], pos[SROWS:P, :]).then_inc(s_move, 16)

            def load_head(h):
                if h >= 2:
                    sp.wait_ge(s_pv, h - 1)
                sp.dma_start(vone[:, h % 2, :, 0:HD],
                             io["v_p"][0, 0, :, h, :].rearrange("(k p) d -> p k d", p=P)).then_inc(s_vo[h % 2], 16)

            for s in range(3):
                sp.wait_ge(s_zs[s], 16 * sum(1 for k in zstores if n_of(*k) % 3 == s))
            load_head(0)
            load_head(1)
            sp.dma_start(steps.rearrange("p k h -> p (k h)"), io["rel_bias"].rearrange("(a k) h -> a (k h)", a=1).partition_broadcast(P)).then_inc(s_b31, 16)
            for h in range(H):
                for r in range(h * 8, h * 8 + 8):
                    if r >= 4:
                        sp.wait_ge(s_kd, r - 3)
                    sp.dma_start(qrow[:, r % 4, :], q_dram[r:r + 1, :].partition_broadcast(P)).then_inc(s_qr[r % 4], 16)
                if h + 2 < H:
                    load_head(h + 2)
            sp.wait_ge(s_kd, SROWS)
            sp.dma_start(qrow[0:SROWS, 0, :], io["v_s"][0].rearrange("b t h d -> (b t) (h d)")).then_inc(s_vnl, 16)
            for s in range(2):
                sp.wait_ge(s_vs[s], 16 * SROWS // 2)
            sp.dma_start(qrow[0:SROWS, 1, :].rearrange("p (h d) -> p h d", h=H),
                         bass.AP(tensor=o_dram.tensor, offset=0, ap=[[H * W, SROWS], [W + HD, H], [1, HD]])).then_inc(s_oh, 16)

            sp.wait_ge(s_oT, 1)
            for half in range(2):
                sp.dma_start(wo[:, :, half * 512:(half + 1) * 512],
                             io["w_o"][0, :, half * 512:(half + 1) * 512].rearrange("(k p) n -> p k n", p=P)).then_inc(s_wo[half], 16)
            sp.wait_ge(s_po, H)

            def load_residual(t):
                if t >= 2:
                    sp.wait_ge(s_h, t - 1)
                src = io["x_prompt"][0, t * P:(t + 1) * P, :] if t < NT else io["x_sample"].rearrange("b t d -> (b t) d")
                sp.dma_start(x2[0:rows_of(t), t % 2, :], src).then_inc(s_x2[t % 2], 16)

            load_residual(0)
            load_residual(1)
            sp.dma_start(state_rows[0:2 * SB, :], io["state_ffn_conv"][0].rearrange("b j f -> (b j) f")).then_inc(s_st, 16)

            def load_ffn(f, s):
                for w, name in enumerate(("w_gate", "w_up")):
                    sp.dma_start(wf[s][:, w], io[name][0, :, bass.ds(f * P, P)].rearrange("(k p) n -> p k n", p=P)).then_inc(s_wf[s], 16)

            load_ffn(0, 0)
            load_ffn(1, 1)
            for t in range(2, TILES):
                load_residual(t)
            sp.wait_ge(s_h, TILES)

            def load_down(j):
                half, fp = divmod(j, NF // 2)
                sp.dma_start(wdn[j % DSLOTS], io["w_down"][0, fp * 2 * P:(fp + 1) * 2 * P, half * 512:(half + 1) * 512]
                             .rearrange("(f p) n -> p f n", p=P)).then_inc(s_wdn[j % DSLOTS], 16)

            load_down(0)
            load_down(1)
            with sp.Fori(1, NF // 2) as it:
                for s in range(2):
                    sp.wait_ge(s_um, it * 6 + (3 * s - 3))
                    load_ffn(it * 2 + s, s)
            sp.wait_ge(s_um, 3 * NF)
            for j in range(2, DSLOTS - 2):
                load_down(j)
            sp.wait_ge(s_cst, 1)
            load_down(DSLOTS - 2)
            sp.wait_ge(s_cse, 2)
            for (first, n), rows in zip(((0, 14), (14, 8)), cs_rows):
                c = slice(first * P, (first + n) * P)
                sp.dma_start(io["conv_p"][0, 0, :, c], rows[0:2, :]).then_inc(s_cso, 16)
                sp.dma_start(io["conv_s"][0].rearrange("b j f -> (b j) f")[:, c], rows[2:2 + 2 * SB, :]).then_inc(s_cso, 16)
            sp.wait_ge(s_cso, 64)
            load_down(DSLOTS - 1)
            sp.dma_start(final_g, io["final_g"].rearrange("(a n) -> a n", a=1).partition_broadcast(P)).then_inc(s_fg, 16)
            for j in range(DSLOTS, NF):
                sp.wait_ge(s_du, j - DSLOTS + 1)
                load_down(j)
            for t in range(TILES):
                sp.wait_ge(s_yn, t + 1)
                dst = io["y_p"][0, t * P:(t + 1) * P, :] if t < NT else io["y_s"].rearrange("b t d -> (b t) d")
                sp.dma_start(dst, hx[0:rows_of(t), t, :]).then_inc(s_yo, 16)
            sp.wait_ge(s_yo, 16 * TILES)

        @block.gpsimd
        def _(pool):
            step = [0]

            def link(ins):
                step[0] += 1
                ins.then_inc(s_pool, 1)
                pool.wait_ge(s_pool, step[0])

            link(nc.gpsimd.memset(ident, 0.0))
            link(nc.gpsimd.affine_select(out=ident, in_=ident, compare_op=ALU.not_equal, fill=1.0, base=0,
                                         pattern=[[-1, P]], channel_multiplier=1))
            nc.gpsimd.memset(minus_half, -0.5)
            nc.gpsimd.memset(epsc, EPS).then_inc(s_built, 1)

            def root(squares, out, t):
                r = rows_of(t)
                link(nc.gpsimd.tensor_scalar(out[0:r, t:t + 1], squares[0:r, t:t + 1], 1.0 / D, EPS, ALU.mult, ALU.add))
                link(nc.gpsimd.tensor_tensor(out[0:r, t:t + 1], out[0:r, t:t + 1], minus_half[0:r, :], ALU.pow))
                nc.gpsimd.drain().then_inc(s_root, 1)

            link(nc.gpsimd.memset(near_mask, 0.0))
            nc.gpsimd.affine_select(out=causal, in_=causal, compare_op=ALU.is_ge, fill=NEG, base=0,
                                    pattern=[[-1, P]], channel_multiplier=1).then_inc(s_built, 1)
            link(nc.gpsimd.memset(own[0:SROWS, :], 0.0))
            for base, pattern, mult in ((0, [[-8, SB], [-1, ST]], 1), (0, [[-8, SB], [0, ST]], 1), (7, [[8, SB], [0, ST]], -1)):
                o3 = own[0:SROWS, :].rearrange("p (b t) -> p b t", b=SB)
                link(nc.gpsimd.affine_select(out=o3, in_=o3, compare_op=ALU.is_ge, fill=NEG, base=base,
                                             pattern=pattern, channel_multiplier=mult))
            nc.gpsimd.memset(stats[:, 500:501], 0.0).then_inc(s_built, 1)

            link(nc.gpsimd.memset(wd, 0.0))
            nc.gpsimd.memset(scd[0:SROWS, HALF:SCORES], NEG).then_inc(s_built, 1)
            link(nc.gpsimd.memset(qbd, 0.0))
            for t in range(TILES):
                pool.wait_ge(s_ssq, t + 1)
                root(ssq, rstd, t)

            for c, t in zstores:
                name, r = CHUNKS[c][0], rows_of(t)
                z = zr[0:r, n_of(c, t) % 3, 0:(HD if name == "small" else W)]
                pool.wait_ge(s_z, n_of(c, t) + 1)
                if name == "q":
                    pool.dma_start(q_dram, z).then_inc(s_zs[n_of(c, t) % 3], 16)
                    continue
                out = {"small": ("idx_k_p", "idx_k_s"), "k": ("k_p", "k_s"), "v": ("v_p", "v_s")}[name]
                if t < NT:
                    dst = io[out[0]][0, 0, t * P:(t + 1) * P]
                    dst = dst if name == "small" else dst.rearrange("t h d -> t (h d)")
                else:
                    dst = io[out[1]][0].rearrange("b t d -> (b t) d" if name == "small" else "b t h d -> (b t) (h d)")
                pool.dma_start(dst, z).then_inc(s_zs[n_of(c, t) % 3], 16)
                if (c, t) == (3, 0):
                    pool.wait_ge(s_tev, tjob_at[(2, NT)] + 1)
                    for j in range(2):
                        r = slice(j * HD, (j + 1) * HD)
                        nc.gpsimd.tensor_copy(qbd[r, :, :, j * ST:(j + 1) * ST],
                                              qT[r, :, SEQ:TOK].rearrange("p c (b q) -> p b c q", b=SB)).then_inc(s_qbd, 1)
                        pool.wait_ge(s_qbd, j + 1)
                if (c, t) == (3, 1):
                    pool.wait_ge(s_wse, 1)
                    link(nc.gpsimd.affine_select(out=wsT, in_=wsT, compare_op=ALU.is_ge, fill=0.0, base=0,
                                                 pattern=[[0, H], [1, P]], channel_multiplier=-1))
                    nc.gpsimd.memset(wsd, 0.0).then_inc(s_wsc, 1)
            for t in range(TILES):
                r = rows_of(t)
                pool.wait_ge(s_z, n_of(6, t) + 1)
                sq = rb4[0:r, 3, :]
                link(nc.gpsimd.tensor_tensor(sq, vn[0:r, t, :], vn[0:r, t, :], ALU.mult))
                sq = sq.rearrange("p (h d) -> p h d", h=H)
                half = HD // 2
                while half > 1:
                    link(nc.gpsimd.tensor_tensor(sq[:, :, 0:half], sq[:, :, 0:half], sq[:, :, half:2 * half], ALU.add))
                    half //= 2
                nc.gpsimd.tensor_tensor(vss[0:r, t, :], sq[:, :, 0], sq[:, :, 1], ALU.add).then_inc(s_vss, 1)
                pool.wait_ge(s_vss, t + 1)
                link(nc.gpsimd.tensor_scalar(vss[0:r, t, :], vss[0:r, t, :], 1.0 / HD, EPS, ALU.mult, ALU.add))
                link(nc.gpsimd.tensor_tensor(vss[0:r, t, :], vss[0:r, t, :], minus_half[0:r, :].to_broadcast([r, H]), ALU.pow))
                v = vn[0:r, t, :].rearrange("p (h d) -> p h d", h=H)
                nc.gpsimd.tensor_tensor(v, v, vss[0:r, t, :].unsqueeze(2).to_broadcast([r, H, HD]), ALU.mult).then_inc(s_vn, 1)
                pool.wait_ge(s_vn, t + 1)
            pool.wait_ge(s_vn, TILES)
            pool.dma_start(io["chunk_v_s"][0].rearrange("b t h d -> (b t) (h d)"), vn[0:SROWS, NT, :]).then_inc(s_cv, 16)
            for h in range(H):
                c = slice(h * HD, (h + 1) * HD)
                pool.wait_ge(s_sb, h + 1)
                link(nc.gpsimd.tensor_tensor(u[:, 0:NT, c], u[:, 0:NT, c], rb4[:, h % 2, :].rearrange("p (t d) -> p t d", t=NT), ALU.mult))
                nc.gpsimd.tensor_tensor(u[0:SROWS, NT, c], u[0:SROWS, NT, c], rb4[0:SROWS, 2, (h % 2) * HD:(h % 2 + 1) * HD],
                                        ALU.mult).then_inc(s_au, 1)
                pool.wait_ge(s_au, h + 1)
            pool.wait_ge(s_cv, 16)
            for s in range(3):
                pool.wait_ge(s_zs[s], 16 * sum(1 for k in zstores if n_of(*k) % 3 == s))
            for s in range(2):
                link(nc.gpsimd.memset(vone[:, s, :, HD:P], 1.0))
            nc.gpsimd.memset(ones, 1.0).then_inc(s_built, 1)

            def gather(cache, done, used):
                def body(it, first):
                    for s in range(4):
                        if not first:
                            pool.wait_ge(used, it * 4 + (s - 3))
                        nc.gpsimd.tensor_copy(idx4[:, s, :], idxT[:, :, bass.ds(it * 4 + s, 1)].rearrange("p c a -> p (c a)"))
                        nc.gpsimd.drain()
                        for c in range(2):
                            pool.indirect_dma_start(out=kv[:, s, c * W:(c + 1) * W], out_offset=None,
                                                    in_=cache[0].rearrange("n p h d -> (n p) (h d)"),
                                                    in_offset=bass.IndirectOffsetOnAxis(ap=idx4[:, s, c:c + 1], axis=0)).then_inc(done[s], 16)

                body(0, True)
                with pool.Fori(1, SROWS // 4) as it:
                    body(it, False)

            pool.wait_ge(s_idx, 1)
            pool.wait_ge(s_mm, 7 * TILES)
            gather(io["cache_k"], s_kg, s_kd)
            pool.wait_ge(s_kd, SROWS)
            gather(io["cache_v"], s_kg, s_vd)

            for t in range(TILES):
                pool.wait_ge(s_hq, t + 1)
                root(hq, hr, t)

            pool.wait_ge(s_ste, 1)
            pool.wait_ge(s_h, TILES)
            link(nc.gpsimd.memset(gb_p[:, 0:2], 0.0))
            nc.gpsimd.tensor_copy(gb_s[:, :, 0:2], st[:, 0, :].rearrange("p (b j) -> p b j", b=SB)).then_inc(s_gst, 1)

            def keep_state(f):
                nc.gpsimd.tensor_copy(cs[:, bass.ds(f, 1), 0:2].rearrange("p a s -> p (a s)"), gb_p[:, SEQ:])
                nc.gpsimd.drain()
                nc.gpsimd.tensor_copy(cs[:, bass.ds(f, 1), 2:].rearrange("p a (b j) -> p (a b) j", b=SB), gb_s[:, :, ST:])
                nc.gpsimd.drain()

            with pool.Fori(0, NF - 1) as f:
                pool.wait_ge(s_cd2, f + 1)
                keep_state(f)
                nc.gpsimd.tensor_copy(gb_s[:, :, 0:2], st[:, bass.ds(f + 1, 1), :].rearrange("p a (b j) -> p (a b) j", b=SB)).then_inc(s_gst, 1)
                pool.wait_ge(s_gst, f + 2)
            pool.wait_ge(s_cd2, NF)
            keep_state(NF - 1)
            nc.gpsimd.drain().then_inc(s_gst, 1)
            for t in range(TILES):
                r = rows_of(t)
                pool.wait_ge(s_yq, TILES + t + 1)
                link(nc.gpsimd.tensor_tensor(yq[0:r, t:t + 1], yq[0:r, t:t + 1], yq[0:r, TILES + t:TILES + t + 1], ALU.add))
                root(yq, yr, t)

        @block.scalar
        def _(act):
            act.wait_ge(s_built, 1)
            for t in range(TILES):
                r = rows_of(t)
                act.wait_ge(s_x[t % 3], 16 * (t // 3 + 1))
                if t:
                    act.wait_ge(s_ssq, t)
                nc.scalar.activation(rb[0:r, 1, :], xring[0:r, t % 3, :], ACT.Square, accum_out=ssq[0:r, t:t + 1]).then_inc(s_ssq, 1)

            def evacuate(c, t):
                name, n, r = CHUNKS[c][0], n_of(c, t), rows_of(t)
                act.wait_ge(s_mm, n + 1)
                src = ps[0:r, 4 + n % 2, :]
                slot = n % 3
                if c < 5 and n >= 3:
                    pc, pt = divmod(n - 3, TILES)
                    if pc < 4:
                        act.wait_ge(s_tz, tjob_at[("dup", NT) if (pc, pt) == (1, NT) else (pc, pt)] + 1)
                    if (pc, pt) in zstores:
                        act.wait_ge(s_zs[slot], 16 * zstores[(pc, pt)])
                if name == "small":
                    nc.scalar.activation(iw[0:r, t, :], src[:, 0:H], ACT.Copy, scale=H ** -0.5)
                    nc.scalar.activation(zr[0:r, slot, 0:HD], src[:, H:H + HD], ACT.Copy)
                    nc.scalar.activation(zr[0:r, slot, HD:2 * HD], src[:, H:H + HD], ACT.Copy).then_inc(s_z, 1)
                elif c < 5:
                    nc.scalar.activation(zr[0:r, slot, :], src, ACT.Copy).then_inc(s_z, 1)
                    if (c, t) == (1, NT):
                        act.wait_ge(s_z, n + 1)
                        nc.scalar.activation(twice[0:r, :].rearrange("p (h e d) -> p h e d", h=H, e=2),
                                             zr[0:r, slot, :].rearrange("p (h d) -> p h d", h=H).unsqueeze(2).to_broadcast([r, H, 2, HD]),
                                             ACT.Copy).then_inc(s_twice, 1)
                elif name == "ua":
                    nc.scalar.activation(u[0:r, t, :], src, ACT.Gelu_apprx_tanh).then_inc(s_z, 1)
                else:
                    nc.scalar.activation(vn[0:r, t, :], src, ACT.Gelu_apprx_tanh).then_inc(s_z, 1)

            def evacuate_t(job):
                c, t = job
                i = tjob_at[job]
                r = rows_of(t)
                tok = slice(t * P, t * P + r)
                act.wait_ge(s_tz, i + 1)
                src = ps[:, 6 + i % 2, :]
                if c == "dup":
                    out = iqd.rearrange("p b (h q) -> p b h q", h=H)
                    nc.scalar.activation(out, src.rearrange("p (h b q) -> p b h q", h=H, b=SB), ACT.Copy,
                                         scale=HD ** -0.5).then_inc(s_tev, 1)
                elif c == 0:
                    nc.scalar.activation(ikT[:, tok], src[:, 0:r], ACT.Copy).then_inc(s_tev, 1)
                else:
                    dst = {1: iqT, 2: qT, 3: kT}[c]
                    nc.scalar.activation(dst[:, :, tok], src.rearrange("p (c t) -> p c t", c=PAIRS)[:, :, 0:r], ACT.Copy,
                                         scale=1.0 if c == 3 else HD ** -0.5).then_inc(s_tev, 1)

            def project(chunks):
                last = None
                for c in chunks:
                    for t in range(TILES):
                        evacuate(c, t)
                        if last and last[0] < 4:
                            evacuate_t(last)
                        if last == (1, NT):
                            evacuate_t(("dup", NT))
                        last = (c, t)
                if last[0] < 4:
                    evacuate_t(last)
                if last == (1, NT):
                    evacuate_t(("dup", NT))

            project([0, 1])
            m = 0
            for i in list(range(2, NT)) + [NT]:
                n, r = ((i + 1) * P, P) if i < NT else (SROWS, SROWS)
                for h in range(H):
                    act.wait_ge(s_dot, m + 1)
                    if m >= 2:
                        act.wait_ge(s_sc, m - 1)
                    src = ps[0:r, 2 * (m % 2):2 * (m % 2) + 2, :].rearrange("p a n -> p (a n)")[:, 0:n]
                    nc.scalar.activation(rb[0:r, m % 2, 0:n], src, ACT.Relu).then_inc(s_relu, 1)
                    m += 1
            act.wait_ge(s_sc, m)

            def evacuate_index_pages(un):
                act.wait_ge(s_ct, un + 1)
                if un >= 2:
                    act.wait_ge(s_cd, 2 * (un - 1))
                nc.scalar.activation(ikcT[:, un % 2, :], ps[:, 0:2, :].rearrange("p a n -> p (a n)"), ACT.Copy).then_inc(s_cT, 1)

            evacuate_index_pages(0)
            for un in range(2 * SB):
                if un + 1 < 2 * SB:
                    evacuate_index_pages(un + 1)
                for r2 in range(2):
                    act.wait_ge(s_cd, 2 * un + r2 + 1)
                    if un:
                        act.wait_ge(s_ch, 2 * (un - 1) + r2 + 1)
                    nc.scalar.activation(rb4[:, r2, :], ps[:, 2 + r2, :], ACT.Relu).then_inc(s_cr, 1)
            act.wait_ge(s_ch, 4 * SB)
            nc.scalar.activation(scd[:, 0:HALF], ps[:, 4:8, :].rearrange("p a n -> p (a n)"), ACT.Copy).then_inc(s_cs, 1)
            project([2])
            act.wait_ge(s_wsp, 1)
            nc.scalar.activation(wsT.rearrange("p h t -> p (h t)"), ps[:, 0:2, :].rearrange("p a n -> p (a n)"), ACT.Copy).then_inc(s_wse, 1)
            project([3, 4, 5, 6])

            act.wait_ge(s_wsd, 16 * 2 * SB)
            for h in range(H):
                act.wait_ge(s_sg, h + 1)
                if h >= 2:
                    act.wait_ge(s_au, h - 1)
                nc.scalar.activation(rb4[:, h % 2, :], ps[:, h % 2, :], ACT.Identity, bias=bs[:, h:h + 1])
                nc.scalar.activation(rb4[0:SROWS, 2, (h % 2) * HD:(h % 2 + 1) * HD], ps[0:SROWS, 2 + h % 2, 0:HD], ACT.Identity,
                                     bias=bsd[:, h:h + 1]).then_inc(s_sb, 1)
            for t in range(TILES):
                r = rows_of(t)
                act.wait_ge(s_at, t + 1)
                nc.scalar.activation(mixT[:, 0:PAIRS, t * P:t * P + r],
                                     ps[:, 6 + t % 2, :].rearrange("p (c t) -> p c t", c=PAIRS)[:, :, 0:r], ACT.Copy).then_inc(s_am, 1)
            act.wait_ge(s_kn, 1)
            act.wait_ge(s_list, 1)
            nc.scalar.activation(ln[0:SROWS, :].rearrange("p (b q h) -> p b h q", b=SB, q=ST),
                                 ps[0:SROWS, 5, :].rearrange("p (b h q) -> p b h q", b=SB, h=H), ACT.Copy).then_inc(s_ln, 1)

            m = g = 0
            for h in range(H):
                for i in range(NT):
                    act.wait_ge(s_L, m + 1)
                    l = rb[:, m % 2, 0:(i + 1) * P]
                    nc.scalar.activation(l, l, ACT.Exp, bias=neg_max[:, m % 2:m % 2 + 1]).then_inc(s_E, 1)
                    m += 1
                    if i:
                        g = evacuate_probs(act, h, i - 1, g)
                g = evacuate_probs(act, h, NT - 1, g)

            nc.scalar.activation(view("rbuf", SROWS * H).rearrange("p (h b t) -> p h b t", h=H, b=SB)[0:ST],
                                 bn[0:ST, :, P:P + ST].unsqueeze(2).to_broadcast([ST, H, SB, ST]), ACT.Copy).then_inc(s_nbs, 1)

            act.wait_ge(s_lm, 3)
            nc.scalar.activation(lg, lg, ACT.Exp)
            nc.scalar.activation(ln[0:SROWS, :], ln[0:SROWS, :], ACT.Exp).then_inc(s_le, 1)
            for r in range(SROWS):
                act.wait_ge(s_vd, r + 1)
                if r >= 2:
                    act.wait_ge(s_vs[r % 2], 16 * (r // 2))
                nc.scalar.activation(out8[:, r % 2, :], ps[0:H, 2 * (r % 2), :], ACT.Copy).then_inc(s_ve, 1)
                act.wait_ge(s_ve, r + 1)
                act.dma_start(o_dram[r].rearrange("g h d -> g (h d)"), out8[:, r % 2, :]).then_inc(s_vs[r % 2], 16)


            for t in range(TILES):
                r = rows_of(t)
                act.wait_ge(s_h, t + 1)
                if t >= 2:
                    act.wait_ge(s_hp, t - 1)
                nc.scalar.activation(hn[0:r, t % 2, :], hx[0:r, t, :], ACT.Square, accum_out=hq[0:r, t:t + 1]).then_inc(s_hq, 1)

            def gate(f):
                act.wait_ge(s_gst, f + 1)
                for g, (a, e) in enumerate(GROUPS):
                    act.wait_ge(s_gm, f * 3 + (g + 1))
                    if e <= SEQ:
                        nc.scalar.activation(gb_p[:, 2 + a:2 + e], ps[:, g, 0:e - a], ACT.Copy).then_inc(s_gc, 1)
                    else:
                        nc.scalar.activation(gb_p[:, 2 + a:2 + SEQ], ps[:, g, 0:SEQ - a], ACT.Copy)
                        nc.scalar.activation(gb_s[:, :, 2:], ps[:, g, SEQ - a:e - a].rearrange("p (b t) -> p b t", b=SB), ACT.Copy).then_inc(s_gc, 1)
                act.wait_ge(s_cd2, f + 1)
                a = aT[:, bass.ds(f * TOK, TOK)]
                nc.scalar.activation(a, a, ACT.Silu).then_inc(s_si, 1)

            with act.Fori(0, NF) as f:
                gate(f)
            for half, blocks in enumerate(cs_rows):
                n = 2 + 2 * SB
                act.wait_ge(s_cst, 1)
                src = ps[0:n, 0:4, :] if half == 0 else ps[0:n, 4:6, :]
                nc.scalar.activation(blocks[0:n, :], src.rearrange("p a n -> p (a n)")[:, 0:(14, 8)[half] * P], ACT.Copy).then_inc(s_cse, 1)
            act.wait_ge(s_cso, 64)
            for unit in range(2 * TILES):
                half, t = divmod(unit, TILES)
                r = rows_of(t)
                act.wait_ge(s_y, unit + 1)
                nc.scalar.activation(squares[0:r, :], hx[0:r, t, half * 512:(half + 1) * 512], ACT.Square,
                                     accum_out=yq[0:r, unit:unit + 1]).then_inc(s_yq, 1)
                act.wait_ge(s_yq, unit + 1)

        @block.vector
        def _(dve):
            step = [0]

            def link(ins):
                step[0] += 1
                ins.then_inc(s_dve, 1)
                dve.wait_ge(s_dve, step[0])

            dve.wait_ge(s_cps, 1)
            nc.vector.tensor_copy(cols, ps[:, 4, 0:112]).then_inc(s_col, 1)
            dve.wait_ge(s_col, 1)

            def scale(t):
                r = rows_of(t)
                dve.wait_ge(s_root, t + 1)
                nc.vector.tensor_scalar(xring[0:r, t % 3, :], xring[0:r, t % 3, :], rstd[0:r, t:t + 1], None, ALU.mult).then_inc(s_xn, 1)

            def gain(t):
                r = rows_of(t)
                dve.wait_ge(s_xTp, t + 1)
                src = ps[:, 2 * (t % 2):2 * (t % 2) + 2, :].rearrange("p a (c t) -> p (a c) t", c=4)[:, :, 0:r]
                nc.vector.tensor_tensor(xT[:, :, t * P:t * P + r], src, g1.unsqueeze(2).to_broadcast([P, KD, r]), ALU.mult).then_inc(s_xT, 1)

            for t in range(TILES):
                scale(t)
                if t:
                    gain(t - 1)
            gain(TILES - 1)
            dve.wait_ge(s_iwp, 1)
            nc.vector.tensor_copy(iwT[0:H, :], ps[0:H, 2, 0:SROWS]).then_inc(s_iwT, 1)
            dve.wait_ge(s_iwp, 2)
            dve.wait_ge(s_built, 4)
            for b in range(SB):
                for e in range(2):
                    r = slice(e * SROWS, (e + 1) * SROWS)
                    c = e * SROWS + b * ST
                    ins = nc.vector.tensor_tensor(wd[r, b, c:c + ST], ps[r, 2, SROWS + b * ST:SROWS + (b + 1) * ST], wsel[r, :], ALU.mult)
            ins.then_inc(s_wd, 1)
            dve.wait_ge(s_toep, 1)
            link(nc.vector.tensor_copy(toep_row[0:H, :], ps[0:H, 3, 0:NEAR]))
            nc.vector.tensor_scalar(toep_row[0:H, :], toep_row[0:H, :], toep_row[0:H, 0:1], None, ALU.subtract).then_inc(s_toev, 1)

            m = 0
            for i in list(range(2, NT)) + [NT]:
                n, r = ((i + 1) * P, P) if i < NT else (SROWS, SROWS)
                sc = view("score", n, sc_off[i]) if i < NT else scn[0:r, :]
                for h in range(H):
                    dve.wait_ge(s_relu, m + 1)
                    w = iw[0:r, i, h:h + 1]
                    if h == 0:
                        ins = nc.vector.tensor_scalar(sc, rb[0:r, m % 2, 0:n], w, None, ALU.mult)
                    else:
                        ins = nc.vector.scalar_tensor_tensor(out=sc, in0=rb[0:r, m % 2, 0:n], scalar=w, in1=sc, op0=ALU.mult, op1=ALU.add)
                    m += 1
                    ins.then_inc(s_sc, 1)
                    dve.wait_ge(s_sc, m)
                dve.wait_ge(s_built, 3)
                if i < NT:
                    nc.vector.tensor_tensor(sc[:, i * P:n], sc[:, i * P:n], causal, ALU.add).then_inc(s_scm, 1)
                else:
                    nc.vector.tensor_tensor(sc, sc, own[0:r, :], ALU.add).then_inc(s_scm, 1)

            dve.wait_ge(s_scm, NT - 1)

            for i in range(2, NT):
                sc = view("score", (i + 1) * P, sc_off[i])
                with dve.Fori(0, TOPK // 8):
                    nc.vector.max(m8, sc)
                    nc.vector.drain()
                    nc.vector.match_replace(sc, m8, sc, TAKEN)
                    nc.vector.drain()
                nc.vector.tensor_scalar(sc, sc, -2e38, NEG, ALU.is_gt, ALU.mult).then_inc(s_topk, 1)

            dve.wait_ge(s_tod, 16)
            dve.wait_ge(s_scn, 16)
            dve.wait_ge(s_cs, 1)
            sc = scd[:, 0:SCORES]
            with dve.Fori(0, TOPK // 8) as it:
                nc.vector.max(m8, sc)
                nc.vector.drain()
                nc.vector.max_index(i8, m8, sc)
                nc.vector.tensor_copy(val[:, bass.ds(it * 8, 8)], m8)
                nc.vector.drain()
                nc.vector.match_replace(sc, m8, sc, TAKEN)
                nc.vector.tensor_copy(pos[:, bass.ds(it * 8, 8)], i8)
                nc.vector.drain()
            nc.vector.drain().then_inc(s_list, 1)

            rows = slice(0, SROWS)
            a_v, a_p, b_v, b_p = val[rows], pos[rows], reverse(val_b[rows]), reverse(pos_b[rows])
            lo_, pg, rf, tf = low[rows], page_of[rows], rows_f[rows], turn_f[rows]
            ia, ib = int_a[rows].bitcast(I32), int_b[rows].bitcast(I32)
            dve.wait_ge(s_move, 32)
            dve.wait_ge(s_rows, 16 * (2 + SB))
            link(nc.vector.tensor_tensor(lo_, a_v, b_v, ALU.is_ge))
            link(nc.vector.tensor_scalar(pg, b_p, float(HALF), None, ALU.add))
            link(nc.vector.tensor_tensor(a_p, a_p, pg, ALU.subtract))
            link(nc.vector.tensor_tensor(a_p, a_p, lo_, ALU.mult))
            link(nc.vector.tensor_tensor(a_p, a_p, pg, ALU.add))
            link(nc.vector.tensor_copy(ia, a_p))
            link(nc.vector.tensor_scalar(ib, ia, 7, None, ALU.logical_shift_right))
            link(nc.vector.tensor_copy(pg, ib))
            link(nc.vector.tensor_scalar(ib, ia, PAGE - 1, None, ALU.bitwise_and))
            link(nc.vector.tensor_copy(rf, ib))
            link(nc.vector.tensor_copy(ptab_f[rows], ptab_i[rows]))
            link(nc.vector.tensor_scalar(ptab_f[rows], ptab_f[rows], float(PAGE), None, ALU.mult))
            for j in range(NPAGES):
                link(nc.vector.tensor_scalar(lo_, pg, float(j), ptab_f[rows, j:j + 1], ALU.is_equal, ALU.mult))
                link(nc.vector.tensor_tensor(rf, rf, lo_, ALU.add))
            link(nc.vector.tensor_scalar(tf, a_p, -1.0, row_t[rows], ALU.mult, ALU.add))
            link(nc.vector.tensor_scalar(lo_, a_p, float(PAST), -1000.0, ALU.is_ge, ALU.mult))
            nc.vector.tensor_tensor(tf, tf, lo_, ALU.add).then_inc(s_pick, 1)
            own_hits = prod[rows, 0:ST * P].rearrange("p (t n) -> p t n", t=ST)
            dve.wait_ge(s_mm, 7 * TILES)
            link(nc.vector.tensor_scalar(a_p, a_p, row_new[rows], None, ALU.subtract))
            for c in range(2):
                for t in range(ST):
                    link(nc.vector.tensor_scalar(own_hits[:, t, :], a_p[:, c * P:(c + 1) * P], float(t), None, ALU.is_equal))
                link(nc.vector.tensor_reduce(sel_new[rows] if c == 0 else sel_new2[rows], own_hits, AX_X, ALU.add))
            link(nc.vector.tensor_tensor(sel_new[rows], sel_new[rows], sel_new2[rows], ALU.add))
            nm = new_mask[rows]
            nm3 = nm.rearrange("p (b t) -> p b t", b=SB)
            link(nc.vector.tensor_scalar(nm, own[rows, :], -1.0, None, ALU.is_ge))
            link(nc.vector.tensor_tensor(nm3, nm3, sel_new[rows].unsqueeze(1).to_broadcast([SROWS, SB, ST]), ALU.mult))
            nc.vector.tensor_scalar(nm, nm, -1.0, -NEG, ALU.add, ALU.mult).then_inc(s_pick, 1)
            dve.wait_ge(s_pickT, 1)
            nc.vector.tensor_copy(idxT, ps[:, 0, 0:P].rearrange("p (c r) -> p c r", c=2)).then_inc(s_idx, 1)
            link(nc.vector.tensor_copy(distT, ps[:, 0, P:2 * P]))
            link(nc.vector.tensor_copy(new_maskT[rows], ps[rows, 0, 2 * P:2 * P + SROWS]))
            dve.wait_ge(s_b31, 16)
            link(nc.vector.tensor_tensor(mx[:, 0:(BUCKETS - 1) * H], steps[:, 1:, :].rearrange("p k h -> p (k h)"),
                                         steps[:, :-1, :].rearrange("p k h -> p (k h)"), ALU.subtract))
            link(nc.vector.tensor_copy(steps[:, 1:, :].rearrange("p k h -> p (k h)"), mx[:, 0:(BUCKETS - 1) * H]))
            nc.vector.drain().then_inc(s_nmT, 1)

            dve.wait_ge(s_topk, NT - 2)
            m = 0
            for h in range(H):
                for i in range(NT):
                    n = (i + 1) * P
                    dve.wait_ge(s_S, m + 1)
                    if m >= 2:
                        dve.wait_ge(s_T, turned_after(m - 2))
                    l = rb[:, m % 2, 0:n]
                    mask = causal if i == 0 else near_mask if i == 1 else view("score", n, sc_off[i])
                    src = ps[:, 2 * (m % 2):2 * (m % 2) + 2, :].rearrange("p a n -> p (a n)")[:, 0:n]
                    link(nc.vector.scalar_tensor_tensor(out=l, in0=src, scalar=b31[:, h:h + 1], in1=mask, op0=ALU.add, op1=ALU.add))
                    if m == 0:
                        dve.wait_ge(s_bn, 16)
                    lo = P if i == 0 else 0
                    near = rb[:, m % 2, n - 2 * P + lo:n]
                    link(nc.vector.tensor_tensor(near, near, bn[:, h, lo:], ALU.add))
                    nc.vector.tensor_reduce(neg_max[:, m % 2:m % 2 + 1], l, AX_X, ALU.max, negate=True).then_inc(s_L, 1)
                    m += 1
                    r = h * 8 + i
                    dve.wait_ge(s_kg[r % 4], 32 * (r // 4 + 1))
                    dve.wait_ge(s_qr[r % 4], 16 * (r // 4 + 1))
                    link(nc.vector.scalar_tensor_tensor(out=prod.rearrange("p (c n) -> p c n", c=2), in0=kv[:, r % 4, :].rearrange("p (c n) -> p c n", c=2),
                                                        scalar=HD ** -0.5, in1=qrow[:, r % 4, :].unsqueeze(1).to_broadcast([P, 2, W]),
                                                        op0=ALU.mult, op1=ALU.mult))
                    nc.vector.tensor_reduce(lg[:, :, r * H:(r + 1) * H], prod.rearrange("p (c h d) -> p c h d", c=2, h=H),
                                            AX_X, ALU.add).then_inc(s_kd, 1)
                dve.wait_ge(s_pv, h + 1)
                if h:
                    dve.wait_ge(s_po, h)
                up, dn = ps[HD:P, 6:8, :].rearrange("p a n -> p (a n)"), ps[0:HD, 6:8, :].rearrange("p a n -> p (a n)")
                link(nc.vector.reciprocal(rl[0:HD, :], up))
                nc.vector.tensor_tensor(mixT[(h % 2) * HD:(h % 2 + 1) * HD, PAIRS + h // 2, 0:SEQ], dn, rl[0:HD, :], ALU.mult).then_inc(s_po, 1)

            dve.wait_ge(s_kd, SROWS)
            lg4 = lg.rearrange("p c (r h) -> p (c r) h", h=H)
            link(nc.vector.tensor_scalar(reach, distT, 0.0, NEG, ALU.is_lt, ALU.mult))
            link(nc.vector.tensor_tensor(lg4, lg4, reach.unsqueeze(2).to_broadcast([P, P, H]), ALU.add))
            link(nc.vector.tensor_tensor(lg4, lg4, steps[:, 0, :].unsqueeze(1).to_broadcast([P, P, H]), ALU.add))
            for k in range(1, BUCKETS):
                link(nc.vector.tensor_scalar(reach, distT, float(FIRST_OF[k]), None, ALU.is_ge))
                for h in range(H):
                    ins = nc.vector.scalar_tensor_tensor(out=lg4[:, :, h], in0=reach, scalar=steps[:, k, h:h + 1], in1=lg4[:, :, h],
                                                         op0=ALU.mult, op1=ALU.add)
                link(ins)
            l3 = ln[rows].rearrange("p (r h) -> p r h", h=H)
            dve.wait_ge(s_ln, 1)
            link(nc.vector.tensor_tensor(l3, l3, new_maskT[rows].unsqueeze(2).to_broadcast([SROWS, SROWS, H]), ALU.add))
            link(nc.vector.tensor_tensor(l3, l3, b31[rows].unsqueeze(1).to_broadcast([SROWS, SROWS, H]), ALU.add))
            dve.wait_ge(s_nbT, 1)
            l4 = ln[rows].rearrange("p (b q h) -> p b q h", b=SB, q=ST)
            nb = new_bias[rows].rearrange("p (h q) -> p q h", h=H)
            link(nc.vector.tensor_copy(new_bias[rows], ps[rows, 1, 0:SROWS]))
            link(nc.vector.tensor_tensor(l4, l4, nb.unsqueeze(1).to_broadcast([SROWS, SB, ST, H]), ALU.add))
            link(nc.vector.tensor_tensor(mx, lg[:, 0, :], lg[:, 1, :], ALU.max))
            nc.vector.tensor_tensor(mx[rows], mx[rows], ln[rows], ALU.max).then_inc(s_dg, 1)
            dve.wait_ge(s_mxT, 1)
            link(nc.vector.tensor_reduce(top_col, ps[:, 2, :].rearrange("p (k n) -> p k n", k=4), AX_X, ALU.max))
            for k in range(4):
                ins = nc.vector.tensor_scalar(diag[:, k * P:(k + 1) * P], ident, top_col[:, k:k + 1], None, ALU.mult)
            ins.then_inc(s_dg, 1)
            dve.wait_ge(s_mb, 1)
            for c in range(2):
                nc.vector.tensor_tensor(lg[:, c, :], lg[:, c, :], ps[:, 3, :], ALU.subtract).then_inc(s_lm, 1)
            nc.vector.tensor_tensor(ln[rows], ln[rows], ps[rows, 3, :], ALU.subtract).then_inc(s_lm, 1)
            dve.wait_ge(s_le, 1)
            link(nc.vector.tensor_tensor(mx, lg[:, 0, :], lg[:, 1, :], ALU.add))
            nc.vector.tensor_tensor(mx[rows], mx[rows], ln[rows], ALU.add).then_inc(s_ls, 1)
            dve.wait_ge(s_lb, 1)
            link(nc.vector.reciprocal(mx, ps[:, 2, :]))
            for c in range(2):
                nc.vector.tensor_tensor(lg[:, c, :], lg[:, c, :], mx, ALU.mult)
            nc.vector.tensor_tensor(ln[rows], ln[rows], mx[rows], ALU.mult).then_inc(s_pn, 1)
            dve.wait_ge(s_oh, 16)
            dve.wait_ge(s_nd, 1)
            nc.vector.tensor_tensor(qrow[rows, 1, :], qrow[rows, 1, :], ps[rows, 1, :], ALU.add).then_inc(s_os, 1)
            dve.wait_ge(s_oT, 1)
            nc.vector.tensor_copy(mixT[:, PAIRS:, SEQ:TOK], ps[:, 3, :].rearrange("p (c t) -> p c t", c=PAIRS)[:, :, 0:SROWS]).then_inc(s_oTe, 1)


            dve.wait_ge(s_stp, 1)
            nc.vector.tensor_copy(st, ps[:, 4, 0:NF * 2 * SB].rearrange("p (f s) -> p f s", f=NF)).then_inc(s_ste, 1)

            def gain2(t):
                r = rows_of(t)
                dve.wait_ge(s_hp, t + 1)
                src = ps[:, 4 + 2 * (t % 2):6 + 2 * (t % 2), :].rearrange("p a (c t) -> p (a c) t", c=4)[:, :, 0:r]
                nc.vector.tensor_tensor(hT[:, :, t * P:t * P + r], src, g2.unsqueeze(2).to_broadcast([P, KD, r]), ALU.mult).then_inc(s_hT, 1)

            for t in range(TILES):
                r = rows_of(t)
                dve.wait_ge(s_mo, t + 1)
                dve.wait_ge(s_x2[t % 2], 16 * (t // 2 + 1))
                src = ps[0:r, 2 * (t % 2):2 * (t % 2) + 2, :].rearrange("p a n -> p (a n)")
                nc.vector.tensor_tensor(hx[0:r, t, :], src, x2[0:r, t % 2, :], ALU.add).then_inc(s_h, 1)
                if t:
                    gain2(t - 1)
                dve.wait_ge(s_root, TILES + t + 1)
                nc.vector.tensor_scalar(hn[0:r, t % 2, :], hx[0:r, t, :], hr[0:r, t:t + 1], None, ALU.mult).then_inc(s_hn, 1)
            gain2(NT)

            def conv(f):
                dve.wait_ge(s_gc, f * 3 + 3)
                a = aT[:, bass.ds(f * TOK, SEQ)]
                a_s = aT[:, bass.ds(f * TOK + SEQ, SROWS)].rearrange("p (b t) -> p b t", b=SB)
                for j in (2, 1, 0):
                    w = cw[:, bass.ds(f + j * NF, 1)]
                    for out, src in ((a, gb_p[:, j:j + SEQ]), (a_s, gb_s[:, :, j:j + ST])):
                        if j == 2:
                            nc.vector.tensor_scalar(out, src, w, cb[:, bass.ds(f, 1)], ALU.mult, ALU.add)
                        else:
                            nc.vector.scalar_tensor_tensor(out=out, in0=src, scalar=w, in1=out, op0=ALU.mult, op1=ALU.add)
                    if j:
                        nc.vector.drain()
                nc.vector.drain().then_inc(s_cd2, 1)
                dve.wait_ge(s_si, f + 1)
                for g, (b, e) in enumerate(GROUPS):
                    dve.wait_ge(s_um, f * 3 + (g + 1))
                    o = aT[:, bass.ds(f * TOK + b, e - b)]
                    nc.vector.tensor_tensor(o, o, ps[:, 3 + g, 0:e - b], ALU.mult).then_inc(s_ag, 1)

            with dve.Fori(0, NF) as f:
                conv(f)

            for unit in range(2 * TILES):
                half, t = divmod(unit, TILES)
                r = rows_of(t)
                dve.wait_ge(s_dm, unit + 1)
                o = hx[0:r, t, half * 512:(half + 1) * 512]
                nc.vector.tensor_tensor(o, o, ps[0:r, (unit + 6) % 8, :], ALU.add).then_inc(s_y, 1)
                if half:
                    dve.wait_ge(s_root, TILES + unit + 1)
                    if t == 0:
                        dve.wait_ge(s_fg, 16)
                    nc.vector.scalar_tensor_tensor(out=hx[0:r, t, :], in0=hx[0:r, t, :], scalar=yr[0:r, t:t + 1], in1=final_g[0:r, :],
                                                   op0=ALU.mult, op1=ALU.mult).then_inc(s_yn, 1)

        @block.tensor
        def _(pe):
            pe.wait_ge(s_built, 1)
            pe.wait_ge(s_const, 16 * 7)
            nc.tensor.transpose(ps[:, 4, 0:112], rows_in[0:112, :], ident[0:112, 0:112]).then_inc(s_cps, 1)
            for t in range(TILES):
                r = rows_of(t)
                pe.wait_ge(s_xn, t + 1)
                if t >= 2:
                    pe.wait_ge(s_xT, t - 1)
                for c in range(KD):
                    o = ps[:, 2 * (t % 2) + c // 4, (c % 4) * P:(c % 4) * P + r]
                    ins = nc.tensor.transpose(o, xring[0:r, t % 3, c * P:(c + 1) * P], ident[0:r, 0:r])
                ins.then_inc(s_xTp, 1)

            def project_tile(c, t):
                n, r, width = n_of(c, t), rows_of(t), CHUNKS[c][2]
                pe.wait_ge(s_w[c % 2], 16 * (c // 2 + 1))
                pe.wait_ge(s_xT, t + 1)
                if n >= 2:
                    pe.wait_ge(s_z, n - 1)
                if n == 0:
                    pe.wait_ge(s_col, 1)
                w = wring[:, c % 2, 0:KD * width].rearrange("p (k n) -> p k n", k=KD)
                for k in range(KD):
                    ins = nc.tensor.matmul(ps[0:r, 4 + n % 2, 0:width], xT[:, k, t * P:t * P + r], w[:, k, :],
                                           start=(k == 0), stop=(k == KD - 1))
                ins.then_inc(s_mm, 1)

            def transpose_z(job):
                c, t = job
                i = tjob_at[job]
                cc = 1 if c == "dup" else c
                n, r = n_of(cc, t), rows_of(t)
                pe.wait_ge(*((s_twice, 1) if c == "dup" else (s_z, n + 1)))
                if i >= 2:
                    pe.wait_ge(s_tev, i - 1)
                for b in range({0: 1, "dup": H}.get(c, PAIRS)):
                    if c == "dup":
                        src = twice[0:r, b * P:(b + 1) * P]
                        o = ps[:, 6 + i % 2, b * SROWS:(b + 1) * SROWS]
                    else:
                        src = zr[0:r, n % 3, b * P:(b + 1) * P]
                        o = ps[:, 6 + i % 2, b * P:b * P + r]
                    ins = nc.tensor.transpose(o, src, ident[0:r, 0:r])
                ins.then_inc(s_tz, 1)

            def project(chunks):
                last = None
                for c in chunks:
                    for t in range(TILES):
                        project_tile(c, t)
                        if last and last[0] < 4:
                            transpose_z(last)
                        if last == (1, NT):
                            transpose_z(("dup", NT))
                        last = (c, t)
                if last[0] < 4:
                    transpose_z(last)
                if last == (1, NT):
                    transpose_z(("dup", NT))

            project([0, 1])
            nc.tensor.transpose(ps[0:H, 2, 0:SROWS], iw[0:SROWS, NT, :], ident[0:SROWS, 0:SROWS]).then_inc(s_iwp, 1)
            pe.wait_ge(s_iwT, 1)
            nc.tensor.matmul(ps[:, 2, SROWS:2 * SROWS], wrep[0:H, :], iwT[0:H, :], start=True, stop=True).then_inc(s_iwp, 1)
            pe.wait_ge(s_rel, 32)
            nc.tensor.matmul(ps[0:H, 3, 0:NEAR], relb[0:BUCKETS, :], hot[0:BUCKETS, :], start=True, stop=True).then_inc(s_toep, 1)
            pe.wait_ge(s_wd, 1)
            pe.wait_ge(s_toev, 1)
            m = 0
            pe.wait_ge(s_tev, 2 * TILES + 1)
            for i in list(range(2, NT)) + [NT]:
                n, r, k0 = ((i + 1) * P, P, 0) if i < NT else (SROWS, SROWS, SEQ)
                for h in range(H):
                    lo = (h % 2) * HD
                    if m >= 2:
                        pe.wait_ge(s_relu, m - 1)
                    for a in range(0, n, 512):
                        e = min(n, a + 512)
                        ins = nc.tensor.matmul(ps[0:r, 2 * (m % 2) + a // 512, 0:e - a],
                                               iqT[lo:lo + HD, h // 2, i * P:i * P + r],
                                               ikT[lo:lo + HD, k0 + a:k0 + e], start=True, stop=True)
                    ins.then_inc(s_dot, 1)
                    m += 1
            def turn_index_pages(un):
                b, half = divmod(un, 2)
                pe.wait_ge(s_ikc[half], 16 * 16 * (b + 1))
                pe.wait_ge(*((s_cT, un) if un else (s_relu, m)))
                for j in range(8):
                    ins = nc.tensor.transpose(ps[:, j // 4, (j % 4) * P:(j % 4 + 1) * P],
                                              ikc[:, half, j, :, :].rearrange("p e d -> p (e d)"), ident)
                ins.then_inc(s_ct, 1)

            turn_index_pages(0)
            for un in range(2 * SB):
                b, half = divmod(un, 2)
                if un + 1 < 2 * SB:
                    turn_index_pages(un + 1)
                pe.wait_ge(s_cT, un + 1)
                for r2 in range(2):
                    if un:
                        pe.wait_ge(s_cr, 2 * (un - 1) + r2 + 1)
                    for e in range(2):
                        r = slice(e * SROWS, (e + 1) * SROWS)
                        ins = nc.tensor.matmul(ps[r, 2 + r2, :], iqd[r, b, :], ikcT[r, half, r2 * 512:(r2 + 1) * 512], start=True, stop=True)
                    ins.then_inc(s_cd, 1)
                for r2 in range(2):
                    pe.wait_ge(s_cr, 2 * un + r2 + 1)
                    nc.tensor.matmul(ps[:, 4 + 2 * half + r2, :], wd[:, b, :], rb4[:, r2, :], start=(b == 0), stop=(b == SB - 1),
                                     skip_group_check=True).then_inc(s_ch, 1)
            pe.wait_ge(s_cs, 1)
            project([2])
            pe.wait_ge(s_ws, 16)
            for h in range(H):
                ins = nc.tensor.transpose(ps[:, h // 4, (h % 4) * P:(h % 4 + 1) * P], ws_in[:, h, :], ident)
            ins.then_inc(s_wsp, 1)
            project([3, 4, 5, 6])

            pe.wait_ge(s_vn, TILES)
            pe.wait_ge(s_wsd, 16 * 2 * SB)
            for h in range(H):
                c = slice(h * HD, (h + 1) * HD)
                pe.wait_ge(*((s_sb, h - 1) if h >= 2 else (s_wse, 1)))
                nc.tensor.matmul(ps[:, h % 2, :], wsT[:, h, :], vn[:, 0:NT, c], start=True, stop=True)
                nc.tensor.matmul(ps[0:SROWS, 2 + h % 2, 0:HD], wsd[0:SROWS, h, :], vn[0:SROWS, NT, c], start=True, stop=True).then_inc(s_sg, 1)
            pe.wait_ge(s_qbd, 2)
            for c in range(PAIRS):
                ins = nc.tensor.matmul(ps[0:SROWS, 5, :].rearrange("p (b c n) -> p b c n", b=SB, c=PAIRS)[:, :, c, :],
                                       kT[:, c, SEQ:TOK], qbd[:, :, c, :], start=True, stop=True)
            ins.then_inc(s_kn, 1)
            pe.wait_ge(s_au, H)
            for t in range(TILES):
                r = rows_of(t)
                if t >= 2:
                    pe.wait_ge(s_am, t - 1)
                for c in range(PAIRS):
                    ins = nc.tensor.transpose(ps[:, 6 + t % 2, c * P:c * P + r], u[0:r, t, c * P:(c + 1) * P], ident[0:r, 0:r])
                ins.then_inc(s_at, 1)

            pe.wait_ge(s_pick, 2)
            pe.wait_ge(s_am, TILES)
            for k, src in enumerate((rows_f, turn_f)):
                for c in range(2):
                    nc.tensor.transpose(ps[:, 0, k * P + c * SROWS:k * P + (c + 1) * SROWS], src[0:SROWS, c * P:(c + 1) * P],
                                        ident[0:SROWS, 0:SROWS])
            nc.tensor.transpose(ps[0:SROWS, 0, 2 * P:2 * P + SROWS], new_mask[0:SROWS, :], ident[0:SROWS, 0:SROWS]).then_inc(s_pickT, 1)
            pe.wait_ge(s_nmT, 1)

            def logits(m):
                h, i = divmod(m, NT)
                n, lo = (i + 1) * P, (h % 2) * HD
                if m >= 2:
                    pe.wait_ge(s_L, m - 1)
                for a in range(0, n, 512):
                    e = min(n, a + 512)
                    ins = nc.tensor.matmul(ps[:, 2 * (m % 2) + a // 512, 0:e - a], qT[lo:lo + HD, h // 2, i * P:(i + 1) * P],
                                           kT[lo:lo + HD, h // 2, a:e], start=True, stop=True)
                ins.then_inc(s_S, 1)

            g = 0
            logits(0)
            for m in range(H * NT):
                h, i = divmod(m, NT)
                if m + 1 < H * NT:
                    logits(m + 1)
                pe.wait_ge(s_E, m + 1)
                for blocks in probs_groups(i):
                    if g >= 2:
                        pe.wait_ge(s_Te, g - 1)
                    for k in blocks:
                        ins = nc.tensor.transpose(ps[:, 4 + g % 2, (k % 4) * P:(k % 4 + 1) * P], rb[:, m % 2, k * P:(k + 1) * P], ident)
                    ins.then_inc(s_T, 1)
                    g += 1
                if i == NT - 1:
                    pe.wait_ge(s_Te, g)
                    pe.wait_ge(s_vo[h % 2], 16 * (h // 2 + 1))
                    pe.wait_ge(s_built, 5)
                    if h:
                        pe.wait_ge(s_po, h)
                    for k in range(NT):
                        for bank in range(2):
                            a, e = max(k * P, bank * 512), (bank + 1) * 512
                            if a < e:
                                ins = nc.tensor.matmul(ps[:, 6 + bank, a - bank * 512:512], vone[:, h % 2, k, :], pT[:, k, a:e],
                                                       start=(k == 0), stop=(k == (3, 7)[bank]), skip_group_check=True)
                    ins.then_inc(s_pv, 1)

            pe.wait_ge(s_nbs, 1)
            for h in range(H):
                ins = nc.tensor.transpose(ps[0:SROWS, 1, h * ST:(h + 1) * ST], own_near(h), ident[0:ST, 0:ST])
            ins.then_inc(s_nbT, 1)
            pe.wait_ge(s_dg, 1)
            for k in range(4):
                ins = nc.tensor.transpose(ps[:, 2, k * P:(k + 1) * P], mx[:, k * P:(k + 1) * P], ident)
            ins.then_inc(s_mxT, 1)
            pe.wait_ge(s_dg, 2)
            nc.tensor.matmul(ps[:, 3, :], ones, diag, start=True, stop=True).then_inc(s_mb, 1)
            pe.wait_ge(s_ls, 1)
            nc.tensor.matmul(ps[:, 2, :], ones, mx, start=True, stop=True).then_inc(s_lb, 1)
            pe.wait_ge(s_pn, 1)
            pe.wait_ge(s_vnl, 16)
            for h in range(H):
                ins = nc.tensor.matmul(ps[0:SROWS, 1, h * HD:(h + 1) * HD], ln[0:SROWS, :].rearrange("p (r h) -> p r h", h=H)[:, :, h],
                                       qrow[0:SROWS, 0, h * HD:(h + 1) * HD], start=True, stop=True)
            ins.then_inc(s_nd, 1)
            for r in range(SROWS):
                pe.wait_ge(s_kg[r % 4], 32 * (SROWS // 4 + r // 4 + 1))
                if r >= 2:
                    pe.wait_ge(s_ve, r - 1)
                for c in range(2):
                    ins = nc.tensor.matmul(ps[0:H, 2 * (r % 2), :], lg[:, c, r * H:(r + 1) * H], kv[:, r % 4, c * W:(c + 1) * W],
                                           start=(c == 0), stop=(c == 1))
                ins.then_inc(s_vd, 1)
            pe.wait_ge(s_os, 1)
            for c in range(PAIRS):
                ins = nc.tensor.transpose(ps[:, 3, c * P:c * P + SROWS], qrow[0:SROWS, 1, c * P:(c + 1) * P], ident[0:SROWS, 0:SROWS])
            ins.then_inc(s_oT, 1)

            pe.wait_ge(s_st, 16)
            for f in range(NF):
                ins = nc.tensor.transpose(ps[:, 4, f * 2 * SB:(f + 1) * 2 * SB], state_rows[0:2 * SB, f * P:(f + 1) * P],
                                          ident[0:2 * SB, 0:2 * SB])
            ins.then_inc(s_stp, 1)

            def turn_residual(t):
                r = rows_of(t)
                pe.wait_ge(s_hn, t + 1)
                pe.wait_ge(*((s_hT, t - 1) if t >= 2 else (s_ste, 1)))
                for c in range(KD):
                    ins = nc.tensor.transpose(ps[:, 4 + 2 * (t % 2) + c // 4, (c % 4) * P:(c % 4) * P + r], hn[0:r, t % 2, c * P:(c + 1) * P],
                                              ident[0:r, 0:r])
                ins.then_inc(s_hp, 1)

            pe.wait_ge(s_po, H)
            pe.wait_ge(s_oTe, 1)
            for t in range(TILES):
                r = rows_of(t)
                if t >= 2:
                    pe.wait_ge(s_h, t - 1)
                for half in range(2):
                    pe.wait_ge(s_wo[half], 16)
                    for k in range(KD):
                        ins = nc.tensor.matmul(ps[0:r, 2 * (t % 2) + half, :], mixT[:, k, t * P:t * P + r],
                                               wo[:, k, half * 512:(half + 1) * 512], start=(k == 0), stop=(k == KD - 1))
                ins.then_inc(s_mo, 1)
                if t:
                    turn_residual(t - 1)
            turn_residual(NT)

            def ffn_block(f, s, it, first):
                pe.wait_ge(s_wf[s], it * 32 + 32)
                for w, done in ((0, s_gm), (1, s_um)):
                    for g, (a, e) in enumerate(GROUPS):
                        if not first:
                            pe.wait_ge((s_gc, s_ag)[w], f * 3 + (g - 2))
                        for k in range(KD):
                            ins = nc.tensor.matmul(ps[:, 3 * w + g, 0:e - a], wf[s][:, w, k, :], hT[:, k, a:e], start=(k == 0), stop=(k == KD - 1))
                        ins.then_inc(done, 1)

            pe.wait_ge(s_hT, TILES)
            ffn_block(0, 0, 0, True)
            ffn_block(1, 1, 0, False)
            with pe.Fori(1, NF // 2) as it:
                for s in range(2):
                    ffn_block(it * 2 + s, s, it, False)

            pe.wait_ge(s_gst, NF + 1)
            pe.wait_ge(s_ag, 3 * NF)
            for f in range(NF):
                bank, c = divmod(f, 4) if f < 14 else (4 + (f - 14) // 4, (f - 14) % 4)
                ins = nc.tensor.transpose(ps[0:2 + 2 * SB, bank, c * P:(c + 1) * P], cs[:, f, :], ident)
            ins.then_inc(s_cst, 1)

            for unit in range(2 * TILES):
                half, t = divmod(unit, TILES)
                r, bank = rows_of(t), (unit + 6) % 8
                if unit >= 8:
                    pe.wait_ge(s_y, unit - 7)
                elif unit == 2:
                    pe.wait_ge(s_cse, 2)
                for f in range(NF):
                    j = half * (NF // 2) + f // 2
                    if t == 0 and f % 2 == 0:
                        pe.wait_ge(s_wdn[j % DSLOTS], 16 * (j // DSLOTS + 1))
                    ins = nc.tensor.matmul(ps[0:r, bank, :], aT[:, f * TOK + t * P:f * TOK + t * P + r], wdn[j % DSLOTS][:, f % 2, :],
                                           start=(f == 0), stop=(f == NF - 1))
                    if unit == NT and f % 2 and f < NF - 1:
                        ins.then_inc(s_du, 1)
                ins.then_inc(s_dm, 1)


OUTS = [("y_p", (1, SEQ, D)), ("y_s", (SB, ST, D)), ("k_p", (1, 1, SEQ, H, HD)), ("v_p", (1, 1, SEQ, H, HD)),
        ("idx_k_p", (1, 1, SEQ, HD)), ("conv_p", (1, 1, 2, DFF)), ("k_s", (1, SB, ST, H, HD)),
        ("v_s", (1, SB, ST, H, HD)), ("idx_k_s", (1, SB, ST, HD)), ("conv_s", (1, SB, 2, DFF)),
        ("chunk_v_s", (1, SB, ST, H, HD))]


def constants():
    rep = np.zeros((H, P), np.float32)
    sel = np.zeros((P, ST), np.float32)
    for c in range(P):
        rep[(c // ST) % H, c] = 1.0
        sel[c, c % ST] = 1.0
    hot = np.zeros((BUCKETS, NEAR), np.float32)
    for y in range(NEAR):
        hot[BUCKET_OF[max(2 * P - 1 - y, 0)], y] = 1.0
    rows = np.zeros((SROWS, 2), np.float32)
    for r in range(SROWS):
        rows[r] = (PAST + r % ST, PAST + r // ST * ST)
    return {"c_rep": rep, "c_sel": sel, "c_hot": hot, "c_rows": rows}


def kernel(**inputs):
    import concourse.bacc as bacc
    from concourse.bass_utils import run_bass_kernel_spmd as run

    nc = bacc.Bacc("TRN2", target_bir_lowering=False, num_devices=1)
    arrays, io = {}, {}
    for name, a in list(inputs.items()) + list(constants().items()):
        a = np.ascontiguousarray(a)
        arrays["in_" + name] = a
        io[name] = nc.dram_tensor("in_" + name, a.shape, mybir.dt.from_np(a.dtype), kind="ExternalInput").ap()
    for name, shape in OUTS:
        io[name] = nc.dram_tensor("out_" + name, shape, F32, kind="ExternalOutput").ap()
    io["pool"] = inputs["cache_k"].shape[1]
    program(nc, io)
    r = run(nc, [arrays], core_ids=[0])
    return tuple(r.results[0]["out_" + name] for name, _ in OUTS)
```

```python
from contextlib import ExitStack

import numpy as np
import concourse.bass as bass
from concourse import mybir

F32 = mybir.dt.float32
F32R = mybir.dt.float32r
I32 = mybir.dt.int32
U32 = mybir.dt.uint32
ALU = mybir.AluOpType
ACT = mybir.ActivationFunctionType
AX_X = mybir.AxisListType.X

P = 128
D = 1024
KD = D // P
SEQ = 1024
NT = SEQ // P
SB, ST = 8, 8
SROWS = SB * ST
TILES = NT + 1
TOK = SEQ + SROWS
H, HD = 8, 64
W = H * HD
PAIRS = H // 2
PAGE = 128
NPAGES = 32
PAST = PAGE * NPAGES
TOPK = 256
DFF = 2816
NF = DFF // P
BUCKETS = 32
EPS = 1e-6
NEG = -1e30
TAKEN = -3e38
HALF = PAST // 2
SCORES = HALF + SROWS
GROUPS = ((0, 364), (364, 728), (728, TOK))
PASSES = TILES // 3
NEAR = 3 * P

CHUNKS = [("small", 6 * W, H + HD), ("iq", 5 * W, W), ("q", 2 * W, W), ("k", 3 * W, W), ("v", 4 * W, W),
          ("ua", 0, W), ("va", W, W)]
VEC_ROWS = [("g1", KD), ("g2", KD), ("cw", 3 * NF), ("cb", NF), ("bs", H)]


_DIST = np.arange(1, 4 * P, dtype=np.float32)
_LARGE = BUCKETS // 2 + (np.log(_DIST / np.float32(BUCKETS // 2)) / np.float32(np.log(128 / (BUCKETS // 2)))
                         * np.float32(BUCKETS // 2)).astype(np.int32)
BUCKET_OF = np.concatenate([[0], np.where(_DIST < BUCKETS // 2, _DIST.astype(np.int32), np.minimum(_LARGE, BUCKETS - 1))])
FIRST_OF = [int(np.argmax(BUCKET_OF == k)) for k in range(BUCKETS)]


def reverse(x):
    (step, rows), (_, n) = x.ap
    return bass.AP(tensor=x.tensor, offset=x.offset + n - 1, ap=[[step, rows], [-1, n]])


def rows_of(t):
    return P if t < NT else SROWS


def program(nc, io):
    ctx = ExitStack()
    with ctx:
        arena_at = -(-nc.sbuf_base // 32) * 32
        arena = ctx.enter_context(nc.sbuf_tensor("arena", [P, 52900], F32))
        ps = ctx.enter_context(nc.psum_tensor("ps", [P, 8, 512], F32))
        ptab = ctx.enter_context(nc.sbuf_tensor("ptab", [1, SB * NPAGES], I32))

        def sem(name):
            return ctx.enter_context(nc.semaphore(name))

        at = {}
        top = [0]

        def region(name, cols):
            at[name] = top[0]
            top[0] += cols
            assert top[0] <= 52900, (name, top[0])

        def view(name, cols, off=0):
            return arena[:, at[name] + off:at[name] + off + cols]

        region("xT", KD * TOK)
        region("wring", 2 * KD * W)
        region("scd", SCORES)
        region("lists", 2560)
        region("rbuf", 2048)
        region("wd", 1088)
        region("iqd", 512)
        region("qbd", 512)
        region("qT", PAIRS * TOK)
        region("kT", PAIRS * TOK)
        region("iqT", TILES * W)
        region("ikc", 5120)
        region("score", 4224)
        region("z", 3 * W)
        region("ikT", TOK)
        region("ident", P)
        region("cols", 112)
        region("stats", 512)
        region("causal", 2 * P)
        region("own", SROWS)
        region("iw", TILES * H)
        region("scn", SROWS)
        region("bias31", H)
        region("idx", P)
        region("small", 256)
        region("bias_steps", 8 * H + 1)

        xT = view("xT", KD * TOK).rearrange("p (c t) -> p c t", c=KD)
        wring = view("wring", 2 * KD * W).rearrange("p (s n) -> p s n", s=2)
        qT = view("qT", PAIRS * TOK).rearrange("p (c t) -> p c t", c=PAIRS)
        kT = view("kT", PAIRS * TOK).rearrange("p (c t) -> p c t", c=PAIRS)
        iqT = view("iqT", PAIRS * TOK).rearrange("p (c t) -> p c t", c=PAIRS)
        ikT = view("ikT", TOK)
        u = view("iqT", TILES * W).rearrange("p (t n) -> p t n", t=TILES)
        vn = view("ikc", TILES * W).rearrange("p (t n) -> p t n", t=TILES)
        xring = view("ikc", 3 * D).rearrange("p (s n) -> p s n", s=3)
        ikc = view("ikc", 2048).rearrange("p (s j e d) -> p s j e d", s=2, e=2, d=HD)
        ikcT = view("ikc", 2048, 2048).rearrange("p (s n) -> p s n", s=2)
        zr = view("z", 3 * W).rearrange("p (s n) -> p s n", s=3)
        rb = view("rbuf", 2048).rearrange("p (s n) -> p s n", s=2)
        twice = view("rbuf", 1024, 1024)
        wd = view("wd", 1024).rearrange("p (b n) -> p b n", b=SB)
        iqd = view("iqd", 512).rearrange("p (b n) -> p b n", b=SB)
        qbd = view("qbd", 512).rearrange("p (b c n) -> p b c n", b=SB, c=PAIRS)
        scd = view("scd", SCORES)
        sc_off = {}
        o = 0
        for i in range(2, NT):
            sc_off[i] = o
            o += (i + 1) * P
        ident = view("ident", P)
        near_mask = view("causal", 2 * P)
        causal = view("causal", P, P)
        own = view("own", SROWS)
        cols = view("cols", 112)
        col_at, o = {}, 0
        for name, n in VEC_ROWS:
            col_at[name] = o
            o += n
        g1 = cols[:, col_at["g1"]:col_at["g1"] + KD]
        iw = view("iw", TILES * H).rearrange("p (t h) -> p t h", t=TILES)
        stats = view("stats", 512)
        ssq, std, rstd = stats[:, 0:9], stats[:, 16:25], stats[:, 32:41]
        epsc = stats[:, 48:49]
        m8 = stats[:, 64:72]
        best = stats[:, 300:364]
        bsd = stats[0:SROWS, 80:88]
        vss = stats[:, 96:168].rearrange("p (t h) -> p t h", t=TILES)
        minus_half = stats[:, 49:50]
        bs = cols[:, col_at["bs"]:col_at["bs"] + H]
        rb4 = view("rbuf", 2048).rearrange("p (s n) -> p s n", s=4)
        ws_in = view("rbuf", 1024).rearrange("p (h s) -> p h s", h=H)
        wsT = view("wd", 1024).rearrange("p (h t) -> p h t", h=H)
        wsd = view("iqd", 512).rearrange("p (h t) -> p h t", h=H)
        mixT = view("xT", KD * TOK).rearrange("p (c t) -> p c t", c=KD)
        scn = view("scn", SROWS)
        b31 = view("bias31", H)
        val, pos = view("lists", TOPK), view("lists", TOPK, TOPK)
        val_b, pos_b = view("lists", TOPK, 2 * TOPK), view("lists", TOPK, 3 * TOPK)
        low, page_of, rows_f, turn_f = (view("lists", TOPK, (4 + i) * TOPK) for i in range(4))
        int_a = view("lists", TOPK, 8 * TOPK)
        int_b = view("lists", TOPK, 9 * TOPK)
        idx4 = view("small", 8).bitcast(I32).rearrange("p (s c) -> p s c", s=4)
        sel_new = view("small", ST, 8)
        row_t, row_new = view("small", 1, 16), view("small", 1, 17)
        neg_max = view("small", 2, 18)
        top_col = view("small", 4, 20)
        i8 = view("small", 8, 24).bitcast(U32)
        ptab_f = view("small", NPAGES, 32)
        ptab_i = view("small", NPAGES, 64).bitcast(I32)
        sel_new2 = view("small", ST, 160)
        new_bias = view("small", SROWS, 168)
        new_mask = view("small", SROWS, 96)
        idxT = view("idx", P).bitcast(I32).rearrange("p (c r) -> p c r", c=2)
        distT = view("ikT", P, 4 * P)
        new_maskT = view("ikT", SROWS, 5 * P)
        reach = view("ikT", P, 5 * P + SROWS + BUCKETS * H)
        kv = view("wring", 4 * 2 * W).rearrange("p (s n) -> p s n", s=4)
        qrow = view("wring", 4 * W, 8 * W).rearrange("p (s n) -> p s n", s=4)
        prod = view("wring", 2 * W, 12 * W)
        ones = view("wring", P, 14 * W)
        diag = view("wring", 4 * P, 15 * W)
        lg = view("scd", 2 * W).rearrange("p (c n) -> p c n", c=2)
        ln = view("scd", W, 2 * W)
        mx = view("scd", W, 3 * W)
        pT = view("iqT", NT * SEQ).rearrange("p (k q) -> p k q", k=NT)
        rl = view("iqT", SEQ, NT * SEQ)
        vone = arena[:, at["z"]:at["z"] + 2 * NT * P].rearrange("p (s k n) -> p s k n", s=2, k=NT)
        bn = view("wd", 2 * P * H).rearrange("p (h u) -> p h u", h=H)
        toep_row = view("lists", NEAR)
        hot = view("lists", NEAR, NEAR)
        relb = view("lists", H, 2 * NEAR)
        def free(first, cols):
            return arena[:, first:first + cols]

        def free_rounded(name, first, cols):
            return nc.alloc_sbuf_tensor_at(name, [P, cols], F32R, offset=arena_at + 4 * first)[:, :]

        wo = view("wring", KD * D).rearrange("p (k n) -> p k n", k=KD)
        x2 = view("lists", 2 * D).rearrange("p (s n) -> p s n", s=2)
        hn = view("rbuf", 2 * D).rearrange("p (s n) -> p s n", s=2)
        parts = at["qT"]
        hT = [[free_rounded(f"hT_part{i}_{c}", parts + (i * KD + c) * TOK, TOK) for c in range(KD)] for i in range(2)]
        raw_at = parts + 2 * KD * TOK
        raw = free(raw_at, 2 * KD * P).rearrange("p (w n) -> p w n", w=2)
        w_parts = [free_rounded(f"ffn_weight_parts{w}", raw_at + (2 + 2 * w) * KD * P, 2 * KD * P).rearrange("p (i n) -> p i n", i=2) for w in range(2)]
        st = free(raw_at + 6 * KD * P, NF * 2 * SB).rearrange("p (f s) -> p f s", f=NF)
        cs = free(raw_at + 6 * KD * P + NF * 2 * SB, NF * (2 + 2 * SB)).rearrange("p (f s) -> p f s", f=NF)
        state_rows = free(raw_at + 2 * KD * P, DFF)
        hx = free(at["qT"], TILES * D).rearrange("p (t n) -> p t n", t=TILES)
        down_at = at["qT"] + TILES * D
        d_raw = free(down_at, 4 * D).rearrange("p (s n) -> p s n", s=4)
        d_parts = free_rounded("w_down_parts", down_at + 4 * D, 4 * D).rearrange("p (s i n) -> p s i n", s=2, i=2)
        a_parts = free_rounded("gated_parts", down_at + 8 * D, 4 * 3 * P).rearrange("p (s i n) -> p s i n", s=2, i=2)
        h_dram = nc.dram_tensor("residual", (TOK, D), F32, kind="Internal").ap()
        aT = arena[:, 0:NF * TOK]
        gb = free(NF * TOK, 2 + SEQ + SB * (2 + ST))
        gb_p = gb[:, 0:2 + SEQ]
        gb_s = gb[:, 2 + SEQ:].rearrange("p (b t) -> p b t", b=SB)
        g2 = cols[:, col_at["g2"]:col_at["g2"] + KD]
        cw = cols[:, col_at["cw"]:col_at["cw"] + 3 * NF]
        cb = cols[:, col_at["cb"]:col_at["cb"] + NF]
        cs_rows = (free(NF * TOK, 14 * P), free(down_at + 8 * D + 4 * 3 * P, 8 * P))
        final_g = free(NF * TOK, D)
        squares = free(NF * TOK + D, 512)
        hq, hr, yq, yr = stats[:, 200:209], stats[:, 216:225], stats[:, 232:250], stats[:, 256:265]
        reached = view("iqT", 16 * TOPK)
        step_k, step_j = view("bias_steps", 4 * H), view("bias_steps", 4 * H, 4 * H)
        first_of = view("bias_steps", 1, 8 * H)
        sbias = view("lists", 2 * W).rearrange("p (c n) -> p c n", c=2)
        dist_dram = nc.dram_tensor("slot_distances", (SROWS, TOPK), F32, kind="Internal").ap()
        q_dram = nc.dram_tensor("sampled_queries", (SROWS, W), F32, kind="Internal").ap()
        toep_dram = nc.dram_tensor("bias_by_distance", (H, P, NEAR), F32, kind="Internal").ap()
        o_dram = nc.dram_tensor("sampled_heads", (SROWS, H, H, HD), F32, kind="Internal").ap()
        rows_in = view("rbuf", P)
        wrep = view("scd", P)
        wsel = view("scd", ST, P)
        iwT = view("scd", SROWS, 2 * P)

        s_const = sem("consts_loaded")
        s_pt = sem("page_table_loaded")
        s_x = [sem(f"x_loaded{i}") for i in range(3)]
        s_w = [sem(f"w_loaded{i}") for i in range(2)]
        s_pool = sem("pool_step")
        s_built = sem("masks_built")
        s_ssq = sem("squares_summed")
        s_root = sem("root_mean_square_ready")
        s_dve = sem("dve_step")
        s_xn = sem("x_normed")
        s_xTp = sem("xT_in_psum")
        s_xT = sem("xT_ready")
        s_mm = sem("projection_done")
        s_z = sem("projection_evacuated")
        s_tz = sem("z_transposed")
        s_tev = sem("transposed_evacuated")
        s_zs = [sem(f"z_stored{i}") for i in range(3)]
        s_cps = sem("columns_in_psum")
        s_col = sem("columns_ready")
        s_twice = sem("index_queries_twice")
        s_dot = sem("index_dots_done")
        s_relu = sem("index_relu_done")
        s_sc = sem("index_relu_used")
        s_scm = sem("index_scores_masked")
        s_topk = sem("topk_done")
        s_iwp = sem("index_weights_in_psum")
        s_iwT = sem("index_weights_turned")
        s_wd = sem("head_sum_weights_ready")
        s_ikc = [sem(f"index_pages_loaded{i}") for i in range(2)]
        s_ct = sem("index_pages_turned")
        s_cT = sem("index_pages_evacuated")
        s_cd = sem("page_dots_done")
        s_cr = sem("page_relu_done")
        s_ch = sem("page_heads_summed")
        s_cs = sem("page_scores_evacuated")
        s_ws = sem("w_s_loaded")
        s_wsp = sem("w_s_turned")
        s_wse = sem("w_s_evacuated")
        s_wsc = sem("w_s_causal")
        s_wsd = sem("w_s_blocks_placed")
        s_vss = sem("gate_squares_summed")
        s_vn = sem("gate_normed")
        s_cv = sem("chunk_v_stored")
        s_sg = sem("spatial_gate_done")
        s_sb = sem("spatial_bias_added")
        s_au = sem("chunk_mlp_done")
        s_at = sem("chunk_mlp_turned")
        s_am = sem("chunk_mlp_evacuated")
        s_qbd = sem("query_blocks_ready")
        s_kn = sem("new_key_logits_done")
        s_ln = sem("new_key_logits_evacuated")
        s_rel = sem("bias_table_loaded")
        s_toep = sem("bias_by_distance_done")
        s_toev = sem("bias_by_distance_evacuated")
        s_tod = sem("bias_by_distance_stored")
        s_bn = sem("near_bias_loaded")
        s_b31 = sem("bucket_bias_loaded")
        s_di = sem("distances_stored")
        s_db = sem("distances_spread")
        s_ind = sem("buckets_reached")
        s_sbT = sem("slot_bias_done")
        s_sbe = sem("slot_bias_evacuated")
        s_rows = sem("row_numbers_loaded")
        s_scn = sem("own_scores_moved")
        s_list = sem("lists_ready")
        s_move = sem("second_list_moved")
        s_pick = sem("picked_rows_ready")
        s_pickT = sem("picked_rows_turned")
        s_idx = sem("gather_rows_ready")
        s_nmT = sem("new_mask_turned")
        s_kg = [sem(f"rows_gathered{i}") for i in range(4)]
        s_qr = [sem(f"query_row_loaded{i}") for i in range(4)]
        s_kp = sem("key_products_done")
        s_kd = sem("key_dots_done")
        s_S = sem("prompt_logits_done")
        s_L = sem("prompt_logits_masked")
        s_nbs = sem("own_bias_spread")
        s_nbT = sem("own_bias_turned")
        s_E = sem("prompt_exp_done")
        s_T = sem("prompt_probs_turned")
        s_Te = sem("prompt_probs_evacuated")
        s_vo = [sem(f"head_values_loaded{i}") for i in range(2)]
        s_pv = sem("prompt_heads_done")
        s_po = sem("prompt_heads_normalised")
        s_mxT = sem("sampled_max_turned")
        s_dg = sem("sampled_max_diagonal")
        s_mb = sem("sampled_max_spread")
        s_lm = sem("sampled_logits_shifted")
        s_le = sem("sampled_exp_done")
        s_ls = sem("sampled_sums_ready")
        s_lb = sem("sampled_sums_spread")
        s_pn = sem("sampled_probs_ready")
        s_vd = sem("sampled_heads_done")
        s_ve = sem("sampled_heads_evacuated")
        s_vs = [sem(f"sampled_heads_stored{i}") for i in range(2)]
        s_vnl = sem("new_values_loaded")
        s_nd = sem("new_key_heads_done")
        s_oh = sem("sampled_heads_loaded")
        s_os = sem("sampled_heads_summed")
        s_oT = sem("sampled_heads_turned")
        s_oTe = sem("sampled_heads_placed")

        s_wo = [sem(f"w_o_loaded{i}") for i in range(2)]
        s_x2 = [sem(f"residual_loaded{i}") for i in range(2)]
        s_mo = sem("w_o_products_done")
        s_h = sem("residual_added")
        s_hq = sem("residual_squares_summed")
        s_hn = sem("residual_normed")
        s_hp = sem("residual_turned")
        s_hT = sem("hT_ready")
        s_st = sem("conv_state_loaded")
        s_stp = sem("conv_state_turned")
        s_ste = sem("conv_state_evacuated")
        s_wf = [sem(f"ffn_weights_loaded{i}") for i in range(2)]
        s_hd = sem("residual_stored")
        s_hl = sem("residual_loaded_again")
        s_hi = sem("weights_rounded")
        s_sp = sem("weights_split")
        s_gst = sem("conv_state_placed")
        s_gm = sem("gate_products_done")
        s_gc = sem("gate_evacuated")
        s_um = sem("up_products_done")
        s_cd2 = sem("conv_done")
        s_si = sem("silu_done")
        s_ag = sem("gated")
        s_cst = sem("new_conv_state_turned")
        s_cse = sem("new_conv_state_evacuated")
        s_cso = sem("new_conv_state_stored")
        s_fg = sem("final_gain_loaded")
        s_wdn = [sem(f"w_down_loaded{i}") for i in range(4)]
        s_dh = sem("down_rounded")
        s_ds = sem("down_split")
        s_du = sem("w_down_used")
        s_y = sem("output_added")
        s_yq = sem("output_squares_summed")
        s_yn = sem("output_normed")
        s_yo = sem("output_stored")

        n_of = lambda c, t: c * TILES + t
        tjob = [(c, t) for c in range(4) for t in range(TILES)]
        tjob.insert(tjob.index((1, NT)) + 1, ("dup", NT))
        tjob_at = {job: i for i, job in enumerate(tjob)}
        zstores = {}
        for c, t in [(c, t) for c in (0, 2, 3, 4) for t in range(TILES) if c != 2 or t == NT]:
            slot = n_of(c, t) % 3
            zstores[(c, t)] = sum(1 for k in zstores if n_of(*k) % 3 == slot) + 1

        def page_numbers(eng, first, n):
            return nc.values_load_multi_w_load_instructions(ptab[0:1, bass.ds(first, n)], engines=(eng.engine,), min_val=0,
                                                            max_val=io["pool"] - 1)[1]

        out8 = view("rbuf", 2 * W)[0:H, :].rearrange("p (s n) -> p s n", s=2)

        def own_near(h):
            return view("rbuf", SROWS * H).rearrange("p (h n) -> p h n", h=H)[0:ST, h, :]

        def probs_groups(i):
            return [range(a, min(a + 4, i + 1)) for a in range(0, i + 1, 4)]

        def turned_after(m):
            h, i = divmod(m, NT)
            return h * sum(len(probs_groups(j)) for j in range(NT)) + sum(len(probs_groups(j)) for j in range(i + 1))

        def evacuate_probs(act, h, i, g):
            if h:
                act.wait_ge(s_pv, (h - 1) * (NT // 2) + i // 2 + 1)
            for blocks in probs_groups(i):
                act.wait_ge(s_T, g + 1)
                n, a = len(blocks), blocks[0]
                nc.scalar.activation(pT[:, a:a + n, i * P:(i + 1) * P], ps[:, 4 + g % 2, 0:n * P].rearrange("p (k q) -> p k q", k=n),
                                     ACT.Copy).then_inc(s_Te, 1)
                g += 1
            return g

        def down_blocks(body, eng, after):
            for p in range(PASSES):
                pieces = (3 * p * P, min(3 * P, TOK - 3 * p * P))
                n0 = p * NF
                lead = 4 - n0 % 4 if n0 % 4 else 4
                for f in range(lead):
                    n = n0 + f
                    body(n, f, n % 2, pieces, n < 2, n % 4, 16 * (n // 4 + 1))
                    if p and f == 1:
                        after(p - 1)
                full = (NF - lead - 1) // 4
                with eng.Fori(0, full) as it:
                    for k in range(4):
                        n = n0 + lead + k
                        body(it * 4 + n, it * 4 + (lead + k), n % 2, pieces, False, n % 4, it * 16 + 16 * (n // 4 + 1))
                for f in range(lead + 4 * full, NF):
                    n = n0 + f
                    body(n, f, n % 2, pieces, False, n % 4, 16 * (n // 4 + 1))
            after(PASSES - 1)

        block = ctx.enter_context(nc.Block())

        @block.sync
        def _(sp):
            sp.dma_start(ptab[:, :], io["page_table"].rearrange("(a b) n -> a (b n)", a=1)).then_inc(s_pt, 16)

            def load_x(t):
                if t >= 3:
                    sp.wait_ge(s_xTp, t - 2)
                src = io["x_prompt"][0, t * P:(t + 1) * P, :] if t < NT else io["x_sample"].rearrange("b t d -> (b t) d")
                sp.dma_start(xring[0:rows_of(t), t % 3, :], src).then_inc(s_x[t % 3], 16)

            def load_w(c):
                _, c0, width = CHUNKS[c]
                if c >= 2:
                    sp.wait_ge(s_mm, n_of(c - 1, 0))
                sp.dma_start(wring[:, c % 2, 0:KD * width].rearrange("p (k n) -> p k n", k=KD),
                             io["w_in"][0, :, c0:c0 + width].rearrange("(k p) n -> p k n", p=P)).then_inc(s_w[c % 2], 16)

            load_x(0)
            r = 0
            for name, n in VEC_ROWS:
                src = {"g1": io["norm1_g"], "g2": io["norm2_g"], "cw": io["conv_w"][0], "cb": io["conv_b"], "bs": io["b_s"][0]}[name]
                src = src if name == "bs" else src.rearrange("a (c p) -> (a c) p", p=P)
                sp.dma_start(rows_in[r:r + n, :], src).then_inc(s_const, 16)
                r += n
            sp.dma_start(wrep[0:H, :], io["c_rep"]).then_inc(s_const, 16)
            sp.dma_start(wsel[:, :], io["c_sel"]).then_inc(s_const, 16)
            load_x(1)
            load_x(2)
            for dst, src in ((relb[0:BUCKETS, :], io["rel_bias"]), (hot[0:BUCKETS, :], io["c_hot"])):
                sp.dma_start(dst, src).then_inc(s_rel, 16)
            sp.dma_start(b31, io["rel_bias"][BUCKETS - 1:BUCKETS, :].partition_broadcast(P)).then_inc(s_rows, 16)
            sp.dma_start(view("small", 2, 16)[0:SROWS, :], io["c_rows"]).then_inc(s_rows, 16)
            sp.dma_start(first_of, io["c_first"]).then_inc(s_b31, 16)
            sp.wait_ge(s_built, 4)
            for g in range(4):
                sp.dma_start(step_k[g * BUCKETS:(g + 1) * BUCKETS, g * H:(g + 1) * H], io["rel_bias"]).then_inc(s_b31, 16)
                sp.dma_start(step_j[g * BUCKETS + 1:(g + 1) * BUCKETS, g * H:(g + 1) * H], io["rel_bias"][0:BUCKETS - 1, :]).then_inc(s_b31, 16)
            for b in range(SB):
                sp.dma_start(ptab_i[b * ST:(b + 1) * ST, :], io["page_table"][b:b + 1, :].partition_broadcast(ST)).then_inc(s_rows, 16)
            load_w(0)
            load_w(1)
            for t in range(3, TILES):
                load_x(t)
            load_w(2)
            sp.wait_ge(s_pt, 16)
            sp.wait_ge(s_xTp, TILES)

            def load_index_pages(b, first):
                for half in range(2):
                    for e in range(2):
                        for j, page in enumerate(page_numbers(sp, b * NPAGES + (e * 16 + half * 8), 8)):
                            if not first and (e, j) == (0, 0):
                                sp.wait_ge(s_ct, b * 2 + (half - 1))
                            sp.dma_start(ikc[:, half, j, e, :],
                                         io["cache_idx_k"][0, bass.ds(page, 1), :, :].rearrange("a p d -> (a p) d")).then_inc(s_ikc[half], 16)

            load_index_pages(0, True)
            load_w(3)
            with sp.Fori(1, SB) as b:
                load_index_pages(b, False)
            sp.wait_ge(s_scm, NT - 1)
            sp.dma_start(scd[SROWS:P, HALF:SCORES], scn[0:SROWS, :]).then_inc(s_scn, 16)
            sp.wait_ge(s_ch, 4 * SB)
            sp.dma_start(ws_in, io["w_s"][0].rearrange("h t s -> t h s")).then_inc(s_ws, 16)
            for c in range(4, 7):
                load_w(c)
            sp.wait_ge(s_wsc, 1)
            for b in range(SB):
                r = slice(b * ST, (b + 1) * ST)
                sp.dma_start(wsd[r, :, r], wsT[0:ST, :, 0:ST]).then_inc(s_wsd, 16)
                sp.dma_start(bsd[r, :], bs[0:ST, :]).then_inc(s_wsd, 16)

            sp.wait_ge(s_toev, 1)
            sp.dma_start(toep_dram, toep_row[0:H, :].unsqueeze(1).to_broadcast([H, P, NEAR])).then_inc(s_tod, 16)
            sp.wait_ge(s_tod, 16)
            sp.wait_ge(s_ln, 1)
            sp.dma_start(bn, bass.AP(tensor=toep_dram.tensor, offset=P - 1, ap=[[NEAR - 1, P], [P * NEAR, H], [1, 2 * P]])).then_inc(s_bn, 16)

            sp.wait_ge(s_list, 1)
            sp.dma_start(val_b[0:SROWS, :], val[SROWS:P, :]).then_inc(s_move, 16)
            sp.dma_start(pos_b[0:SROWS, :], pos[SROWS:P, :]).then_inc(s_move, 16)

            sp.wait_ge(s_pick, 1)
            sp.dma_start(dist_dram, turn_f[0:SROWS, :]).then_inc(s_di, 16)
            sp.wait_ge(s_di, 16)
            sp.wait_ge(s_am, TILES)
            for g in range(4):
                sp.dma_start(reached[g * BUCKETS:(g + 1) * BUCKETS, :],
                             dist_dram[g * (SROWS // 4):(g + 1) * (SROWS // 4), :].rearrange("(a r) n -> a (r n)", a=1)
                             .partition_broadcast(BUCKETS)).then_inc(s_db, 16)

            def load_head(h):
                if h >= 2:
                    sp.wait_ge(s_pv, (h - 1) * (NT // 2))
                sp.dma_start(vone[:, h % 2, :, 0:HD],
                             io["v_p"][0, 0, :, h, :].rearrange("(k p) d -> p k d", p=P)).then_inc(s_vo[h % 2], 16)

            for s in range(3):
                sp.wait_ge(s_zs[s], 16 * sum(1 for k in zstores if n_of(*k) % 3 == s))
            load_head(0)
            load_head(1)
            for h in range(H):
                for r in range(h * 8, h * 8 + 8):
                    if r >= 4:
                        sp.wait_ge(s_kd, r - 3)
                    sp.dma_start(qrow[:, r % 4, :], q_dram[r:r + 1, :].partition_broadcast(P)).then_inc(s_qr[r % 4], 16)
                    if r % 8 == 3 and 0 < h < H - 1:
                        load_head(h + 1)
            sp.wait_ge(s_kd, SROWS)
            sp.dma_start(qrow[0:SROWS, 0, :], io["v_s"][0].rearrange("b t h d -> (b t) (h d)")).then_inc(s_vnl, 16)
            for s in range(2):
                sp.wait_ge(s_vs[s], 16 * SROWS // 2)
            sp.dma_start(qrow[0:SROWS, 1, :].rearrange("p (h d) -> p h d", h=H),
                         bass.AP(tensor=o_dram.tensor, offset=0, ap=[[H * W, SROWS], [W + HD, H], [1, HD]])).then_inc(s_oh, 16)

            sp.wait_ge(s_oT, 1)
            for half in range(2):
                sp.dma_start(wo[:, :, half * 512:(half + 1) * 512],
                             io["w_o"][0, :, half * 512:(half + 1) * 512].rearrange("(k p) n -> p k n", p=P)).then_inc(s_wo[half], 16)
            sp.wait_ge(s_po, H)

            def load_residual(t):
                src = io["x_prompt"][0, t * P:(t + 1) * P, :] if t < NT else io["x_sample"].rearrange("b t d -> (b t) d")
                sp.dma_start(x2[0:rows_of(t), t % 2, :], src).then_inc(s_x2[t % 2], 16)

            def load_ffn(f, w):
                sp.dma_start(raw[:, w].rearrange("p (k n) -> p k n", k=KD),
                             io[("w_gate", "w_up")[w]][0, :, bass.ds(f * P, P)].rearrange("(k p) n -> p k n", p=P)).then_inc(s_wf[w], 16)

            load_residual(0)
            load_residual(1)
            sp.dma_start(state_rows[0:2 * SB, :], io["state_ffn_conv"][0].rearrange("b j f -> (b j) f")).then_inc(s_st, 16)
            load_ffn(0, 0)
            load_ffn(0, 1)
            for t in range(TILES):
                sp.wait_ge(s_h, t + 1)
                sp.dma_start(h_dram[t * P:t * P + rows_of(t), :], x2[0:rows_of(t), t % 2, :]).then_inc(s_hd, 16)
                sp.wait_ge(s_hd, 16 * (t + 1))
                if t + 2 < TILES:
                    sp.wait_ge(s_hn, t + 1)
                    load_residual(t + 2)
            with sp.Fori(1, NF) as f:
                for w in range(2):
                    sp.wait_ge(s_sp, f * 2 + (w - 1))
                    load_ffn(f, w)

            def load_down(f, slot):
                sp.dma_start(d_raw[:, slot, :], io["w_down"][0, bass.ds(f * P, P), :]).then_inc(s_wdn[slot], 16)

            sp.wait_ge(s_um, 3 * NF)
            for f in range(4):
                load_down(f, f)
            sp.dma_start(hx[:, 0:NT, :], h_dram[0:SEQ, :].rearrange("(t p) n -> p t n", p=P)).then_inc(s_hl, 16)
            sp.dma_start(hx[0:SROWS, NT, :], h_dram[SEQ:TOK, :]).then_inc(s_hl, 16)

            def load_downs(n, f, slots):
                for k, slot in enumerate(slots):
                    sp.wait_ge(s_ds, n + (k - 3))
                    load_down(f + k, slot)

            with sp.Fori(1, 5) as it:
                load_downs(it * 4, it * 4, range(4))
            load_downs(20, 20, (0, 1))
            sp.wait_ge(s_cse, 2)
            for (first, n), rows in zip(((0, 14), (14, 8)), cs_rows):
                c = slice(first * P, (first + n) * P)
                sp.dma_start(io["conv_p"][0, 0, :, c], rows[0:2, :]).then_inc(s_cso, 16)
                sp.dma_start(io["conv_s"][0].rearrange("b j f -> (b j) f")[:, c], rows[2:2 + 2 * SB, :]).then_inc(s_cso, 16)
            sp.wait_ge(s_cso, 64)
            sp.dma_start(final_g, io["final_g"].rearrange("(a n) -> a n", a=1).partition_broadcast(P)).then_inc(s_fg, 16)

            def store_outputs(p):
                for t in range(3 * p, 3 * p + 3):
                    sp.wait_ge(s_yn, t + 1)
                    dst = io["y_p"][0, t * P:(t + 1) * P, :] if t < NT else io["y_s"].rearrange("b t d -> (b t) d")
                    sp.dma_start(dst, hx[0:rows_of(t), t, :]).then_inc(s_yo, 16)

            load_downs(NF, 0, (2, 3))
            with sp.Fori(0, 5) as it:
                load_downs(it * 4 + (NF + 2), it * 4 + 2, range(4))
            store_outputs(0)
            with sp.Fori(0, 5) as it:
                load_downs(it * 4 + 2 * NF, it * 4, range(4))
            load_downs(2 * NF + 20, 20, (0, 1))
            store_outputs(1)
            store_outputs(2)
            sp.wait_ge(s_yo, 16 * TILES)

        @block.gpsimd
        def _(pool):
            step = [0]

            def link(ins):
                step[0] += 1
                ins.then_inc(s_pool, 1)
                pool.wait_ge(s_pool, step[0])

            link(nc.gpsimd.memset(ident, 0.0))
            link(nc.gpsimd.affine_select(out=ident, in_=ident, compare_op=ALU.not_equal, fill=1.0, base=0,
                                         pattern=[[-1, P]], channel_multiplier=1))
            nc.gpsimd.memset(minus_half, -0.5)
            nc.gpsimd.memset(epsc, EPS).then_inc(s_built, 1)

            def root(squares, out, t):
                r = rows_of(t)
                link(nc.gpsimd.tensor_scalar(out[0:r, t:t + 1], squares[0:r, t:t + 1], 1.0 / D, EPS, ALU.mult, ALU.add))
                link(nc.gpsimd.tensor_tensor(out[0:r, t:t + 1], out[0:r, t:t + 1], minus_half[0:r, :], ALU.pow))
                nc.gpsimd.drain().then_inc(s_root, 1)

            link(nc.gpsimd.memset(near_mask, 0.0))
            nc.gpsimd.affine_select(out=causal, in_=causal, compare_op=ALU.is_ge, fill=NEG, base=0,
                                    pattern=[[-1, P]], channel_multiplier=1).then_inc(s_built, 1)
            link(nc.gpsimd.memset(own[0:SROWS, :], 0.0))
            for base, pattern, mult in ((0, [[-8, SB], [-1, ST]], 1), (0, [[-8, SB], [0, ST]], 1), (7, [[8, SB], [0, ST]], -1)):
                o3 = own[0:SROWS, :].rearrange("p (b t) -> p b t", b=SB)
                link(nc.gpsimd.affine_select(out=o3, in_=o3, compare_op=ALU.is_ge, fill=NEG, base=base,
                                             pattern=pattern, channel_multiplier=mult))
            nc.gpsimd.memset(stats[:, 500:501], 0.0).then_inc(s_built, 1)

            link(nc.gpsimd.memset(view("bias_steps", 8 * H), 0.0))
            link(nc.gpsimd.memset(wd, 0.0))
            nc.gpsimd.memset(scd[0:SROWS, HALF:SCORES], NEG).then_inc(s_built, 1)
            link(nc.gpsimd.memset(qbd, 0.0))
            for t in range(TILES):
                pool.wait_ge(s_ssq, t + 1)
                root(ssq, rstd, t)

            for c, t in zstores:
                name, r = CHUNKS[c][0], rows_of(t)
                z = zr[0:r, n_of(c, t) % 3, 0:(HD if name == "small" else W)]
                pool.wait_ge(s_z, n_of(c, t) + 1)
                if name == "q":
                    pool.dma_start(q_dram, z).then_inc(s_zs[n_of(c, t) % 3], 16)
                    continue
                out = {"small": ("idx_k_p", "idx_k_s"), "k": ("k_p", "k_s"), "v": ("v_p", "v_s")}[name]
                if t < NT:
                    dst = io[out[0]][0, 0, t * P:(t + 1) * P]
                    dst = dst if name == "small" else dst.rearrange("t h d -> t (h d)")
                else:
                    dst = io[out[1]][0].rearrange("b t d -> (b t) d" if name == "small" else "b t h d -> (b t) (h d)")
                pool.dma_start(dst, z).then_inc(s_zs[n_of(c, t) % 3], 16)
                if (c, t) == (3, 0):
                    pool.wait_ge(s_tev, tjob_at[(2, NT)] + 1)
                    for j in range(2):
                        r = slice(j * HD, (j + 1) * HD)
                        nc.gpsimd.tensor_copy(qbd[r, :, :, j * ST:(j + 1) * ST],
                                              qT[r, :, SEQ:TOK].rearrange("p c (b q) -> p b c q", b=SB)).then_inc(s_qbd, 1)
                        pool.wait_ge(s_qbd, j + 1)
                if (c, t) == (3, 1):
                    pool.wait_ge(s_wse, 1)
                    link(nc.gpsimd.affine_select(out=wsT, in_=wsT, compare_op=ALU.is_ge, fill=0.0, base=0,
                                                 pattern=[[0, H], [1, P]], channel_multiplier=-1))
                    nc.gpsimd.memset(wsd, 0.0).then_inc(s_wsc, 1)
            for t in range(TILES):
                r = rows_of(t)
                pool.wait_ge(s_z, n_of(6, t) + 1)
                sq = rb4[0:r, 3, :]
                link(nc.gpsimd.tensor_tensor(sq, vn[0:r, t, :], vn[0:r, t, :], ALU.mult))
                sq = sq.rearrange("p (h d) -> p h d", h=H)
                half = HD // 2
                while half > 1:
                    link(nc.gpsimd.tensor_tensor(sq[:, :, 0:half], sq[:, :, 0:half], sq[:, :, half:2 * half], ALU.add))
                    half //= 2
                nc.gpsimd.tensor_tensor(vss[0:r, t, :], sq[:, :, 0], sq[:, :, 1], ALU.add).then_inc(s_vss, 1)
                pool.wait_ge(s_vss, t + 1)
                link(nc.gpsimd.tensor_scalar(vss[0:r, t, :], vss[0:r, t, :], 1.0 / HD, EPS, ALU.mult, ALU.add))
                link(nc.gpsimd.tensor_tensor(vss[0:r, t, :], vss[0:r, t, :], minus_half[0:r, :].to_broadcast([r, H]), ALU.pow))
                v = vn[0:r, t, :].rearrange("p (h d) -> p h d", h=H)
                nc.gpsimd.tensor_tensor(v, v, vss[0:r, t, :].unsqueeze(2).to_broadcast([r, H, HD]), ALU.mult).then_inc(s_vn, 1)
                pool.wait_ge(s_vn, t + 1)
            pool.wait_ge(s_vn, TILES)
            pool.dma_start(io["chunk_v_s"][0].rearrange("b t h d -> (b t) (h d)"), vn[0:SROWS, NT, :]).then_inc(s_cv, 16)
            for h in range(H):
                c = slice(h * HD, (h + 1) * HD)
                pool.wait_ge(s_sb, h + 1)
                link(nc.gpsimd.tensor_tensor(u[:, 0:NT, c], u[:, 0:NT, c], rb4[:, h % 2, :].rearrange("p (t d) -> p t d", t=NT), ALU.mult))
                nc.gpsimd.tensor_tensor(u[0:SROWS, NT, c], u[0:SROWS, NT, c], rb4[0:SROWS, 2, (h % 2) * HD:(h % 2 + 1) * HD],
                                        ALU.mult).then_inc(s_au, 1)
                pool.wait_ge(s_au, h + 1)
            pool.wait_ge(s_cv, 16)
            for s in range(3):
                pool.wait_ge(s_zs[s], 16 * sum(1 for k in zstores if n_of(*k) % 3 == s))
            for s in range(2):
                link(nc.gpsimd.memset(vone[:, s, :, HD:P], 1.0))
            nc.gpsimd.memset(ones, 1.0).then_inc(s_built, 1)

            def gather(cache, done, used):
                def body(it, first):
                    for s in range(4):
                        if not first:
                            pool.wait_ge(used, it * 4 + (s - 3))
                        nc.gpsimd.tensor_copy(idx4[:, s, :], idxT[:, :, bass.ds(it * 4 + s, 1)].rearrange("p c a -> p (c a)"))
                        nc.gpsimd.drain()
                        for c in range(2):
                            pool.indirect_dma_start(out=kv[:, s, c * W:(c + 1) * W], out_offset=None,
                                                    in_=cache[0].rearrange("n p h d -> (n p) (h d)"),
                                                    in_offset=bass.IndirectOffsetOnAxis(ap=idx4[:, s, c:c + 1], axis=0)).then_inc(done[s], 16)

                body(0, True)
                with pool.Fori(1, SROWS // 4) as it:
                    body(it, False)

            pool.wait_ge(s_idx, 1)
            pool.wait_ge(s_mm, 7 * TILES)
            gather(io["cache_k"], s_kg, s_kd)
            pool.wait_ge(s_kd, SROWS)
            gather(io["cache_v"], s_kg, s_vd)

            for t in range(TILES):
                pool.wait_ge(s_hq, t + 1)
                root(hq, hr, t)

            pool.wait_ge(s_ste, 1)
            pool.wait_ge(s_oTe, 1)
            link(nc.gpsimd.memset(gb_p[:, 0:2], 0.0))
            nc.gpsimd.tensor_copy(gb_s[:, :, 0:2], st[:, 0, :].rearrange("p (b j) -> p b j", b=SB)).then_inc(s_gst, 1)

            def keep_state(f):
                nc.gpsimd.tensor_copy(cs[:, bass.ds(f, 1), 0:2].rearrange("p a s -> p (a s)"), gb_p[:, SEQ:])
                nc.gpsimd.drain()
                nc.gpsimd.tensor_copy(cs[:, bass.ds(f, 1), 2:].rearrange("p a (b j) -> p (a b) j", b=SB), gb_s[:, :, ST:])
                nc.gpsimd.drain()

            with pool.Fori(0, NF - 1) as f:
                pool.wait_ge(s_cd2, f + 1)
                keep_state(f)
                nc.gpsimd.tensor_copy(gb_s[:, :, 0:2], st[:, bass.ds(f + 1, 1), :].rearrange("p a (b j) -> p (a b) j", b=SB)).then_inc(s_gst, 1)
                pool.wait_ge(s_gst, f + 2)
            pool.wait_ge(s_cd2, NF)
            keep_state(NF - 1)
            nc.gpsimd.drain().then_inc(s_gst, 1)
            for t in range(TILES):
                r = rows_of(t)
                pool.wait_ge(s_yq, 2 * t + 2)
                link(nc.gpsimd.tensor_tensor(yq[0:r, t:t + 1], yq[0:r, t:t + 1], yq[0:r, TILES + t:TILES + t + 1], ALU.add))
                root(yq, yr, t)

        @block.scalar
        def _(act):
            act.wait_ge(s_built, 1)
            for t in range(TILES):
                r = rows_of(t)
                act.wait_ge(s_x[t % 3], 16 * (t // 3 + 1))
                if t:
                    act.wait_ge(s_ssq, t)
                nc.scalar.activation(rb[0:r, 1, :], xring[0:r, t % 3, :], ACT.Square, accum_out=ssq[0:r, t:t + 1]).then_inc(s_ssq, 1)

            def evacuate(c, t):
                name, n, r = CHUNKS[c][0], n_of(c, t), rows_of(t)
                act.wait_ge(s_mm, n + 1)
                src = ps[0:r, 4 + n % 2, :]
                slot = n % 3
                if c < 5 and n >= 3:
                    pc, pt = divmod(n - 3, TILES)
                    if pc < 4:
                        act.wait_ge(s_tz, tjob_at[("dup", NT) if (pc, pt) == (1, NT) else (pc, pt)] + 1)
                    if (pc, pt) in zstores:
                        act.wait_ge(s_zs[slot], 16 * zstores[(pc, pt)])
                if name == "small":
                    nc.scalar.activation(iw[0:r, t, :], src[:, 0:H], ACT.Copy, scale=H ** -0.5)
                    nc.scalar.activation(zr[0:r, slot, 0:HD], src[:, H:H + HD], ACT.Copy)
                    nc.scalar.activation(zr[0:r, slot, HD:2 * HD], src[:, H:H + HD], ACT.Copy).then_inc(s_z, 1)
                elif c < 5:
                    nc.scalar.activation(zr[0:r, slot, :], src, ACT.Copy).then_inc(s_z, 1)
                    if (c, t) == (1, NT):
                        act.wait_ge(s_z, n + 1)
                        nc.scalar.activation(twice[0:r, :].rearrange("p (h e d) -> p h e d", h=H, e=2),
                                             zr[0:r, slot, :].rearrange("p (h d) -> p h d", h=H).unsqueeze(2).to_broadcast([r, H, 2, HD]),
                                             ACT.Copy).then_inc(s_twice, 1)
                elif name == "ua":
                    nc.scalar.activation(u[0:r, t, :], src, ACT.Gelu_apprx_tanh).then_inc(s_z, 1)
                else:
                    nc.scalar.activation(vn[0:r, t, :], src, ACT.Gelu_apprx_tanh).then_inc(s_z, 1)

            def evacuate_t(job):
                c, t = job
                i = tjob_at[job]
                r = rows_of(t)
                tok = slice(t * P, t * P + r)
                act.wait_ge(s_tz, i + 1)
                src = ps[:, 6 + i % 2, :]
                if c == "dup":
                    out = iqd.rearrange("p b (h q) -> p b h q", h=H)
                    nc.scalar.activation(out, src.rearrange("p (h b q) -> p b h q", h=H, b=SB), ACT.Copy,
                                         scale=HD ** -0.5).then_inc(s_tev, 1)
                elif c == 0:
                    nc.scalar.activation(ikT[:, tok], src[:, 0:r], ACT.Copy).then_inc(s_tev, 1)
                else:
                    dst = {1: iqT, 2: qT, 3: kT}[c]
                    nc.scalar.activation(dst[:, :, tok], src.rearrange("p (c t) -> p c t", c=PAIRS)[:, :, 0:r], ACT.Copy,
                                         scale=1.0 if c == 3 else HD ** -0.5).then_inc(s_tev, 1)

            def project(chunks):
                last = None
                for c in chunks:
                    for t in range(TILES):
                        evacuate(c, t)
                        if last and last[0] < 4:
                            evacuate_t(last)
                        if last == (1, NT):
                            evacuate_t(("dup", NT))
                        last = (c, t)
                if last[0] < 4:
                    evacuate_t(last)
                if last == (1, NT):
                    evacuate_t(("dup", NT))

            project([0, 1])
            m = 0
            for i in list(range(2, NT)) + [NT]:
                n, r = ((i + 1) * P, P) if i < NT else (SROWS, SROWS)
                for h in range(H):
                    act.wait_ge(s_dot, m + 1)
                    if m >= 2:
                        act.wait_ge(s_sc, m - 1)
                    src = ps[0:r, 2 * (m % 2):2 * (m % 2) + 2, :].rearrange("p a n -> p (a n)")[:, 0:n]
                    nc.scalar.activation(rb[0:r, m % 2, 0:n], src, ACT.Relu).then_inc(s_relu, 1)
                    m += 1
            act.wait_ge(s_sc, m)

            def evacuate_index_pages(un):
                act.wait_ge(s_ct, un + 1)
                if un >= 2:
                    act.wait_ge(s_cd, 2 * (un - 1))
                nc.scalar.activation(ikcT[:, un % 2, :], ps[:, 0:2, :].rearrange("p a n -> p (a n)"), ACT.Copy).then_inc(s_cT, 1)

            evacuate_index_pages(0)
            for un in range(2 * SB):
                if un + 1 < 2 * SB:
                    evacuate_index_pages(un + 1)
                for r2 in range(2):
                    act.wait_ge(s_cd, 2 * un + r2 + 1)
                    if un:
                        act.wait_ge(s_ch, 2 * (un - 1) + r2 + 1)
                    nc.scalar.activation(rb4[:, r2, :], ps[:, 2 + r2, :], ACT.Relu).then_inc(s_cr, 1)
            act.wait_ge(s_ch, 4 * SB)
            nc.scalar.activation(scd[:, 0:HALF], ps[:, 4:8, :].rearrange("p a n -> p (a n)"), ACT.Copy).then_inc(s_cs, 1)
            project([2])
            act.wait_ge(s_wsp, 1)
            nc.scalar.activation(wsT.rearrange("p h t -> p (h t)"), ps[:, 0:2, :].rearrange("p a n -> p (a n)"), ACT.Copy).then_inc(s_wse, 1)
            project([3, 4, 5, 6])

            act.wait_ge(s_wsd, 16 * 2 * SB)
            for h in range(H):
                act.wait_ge(s_sg, h + 1)
                if h >= 2:
                    act.wait_ge(s_au, h - 1)
                nc.scalar.activation(rb4[:, h % 2, :], ps[:, h % 2, :], ACT.Identity, bias=bs[:, h:h + 1])
                nc.scalar.activation(rb4[0:SROWS, 2, (h % 2) * HD:(h % 2 + 1) * HD], ps[0:SROWS, 2 + h % 2, 0:HD], ACT.Identity,
                                     bias=bsd[:, h:h + 1]).then_inc(s_sb, 1)
            for t in range(TILES):
                r = rows_of(t)
                act.wait_ge(s_at, t + 1)
                nc.scalar.activation(mixT[:, 0:PAIRS, t * P:t * P + r],
                                     ps[:, 6 + t % 2, :].rearrange("p (c t) -> p c t", c=PAIRS)[:, :, 0:r], ACT.Copy).then_inc(s_am, 1)
            act.wait_ge(s_kn, 1)
            act.wait_ge(s_list, 1)
            nc.scalar.activation(ln[0:SROWS, :].rearrange("p (b q h) -> p b h q", b=SB, q=ST),
                                 ps[0:SROWS, 5, :].rearrange("p (b h q) -> p b h q", b=SB, h=H), ACT.Copy).then_inc(s_ln, 1)

            m = g = 0
            for h in range(H):
                for i in range(NT):
                    act.wait_ge(s_L, m + 1)
                    l = rb[:, m % 2, 0:(i + 1) * P]
                    nc.scalar.activation(l, l, ACT.Exp, scale=-1.0, bias=neg_max[:, m % 2:m % 2 + 1]).then_inc(s_E, 1)
                    m += 1
                    if i:
                        g = evacuate_probs(act, h, i - 1, g)
                g = evacuate_probs(act, h, NT - 1, g)

            nc.scalar.activation(view("rbuf", SROWS * H).rearrange("p (h b t) -> p h b t", h=H, b=SB)[0:ST],
                                 bn[0:ST, :, P:P + ST].unsqueeze(2).to_broadcast([ST, H, SB, ST]), ACT.Copy).then_inc(s_nbs, 1)

            act.wait_ge(s_lm, 3)
            nc.scalar.activation(lg, lg, ACT.Exp)
            nc.scalar.activation(ln[0:SROWS, :], ln[0:SROWS, :], ACT.Exp).then_inc(s_le, 1)
            for r in range(SROWS):
                act.wait_ge(s_vd, r + 1)
                if r >= 2:
                    act.wait_ge(s_vs[r % 2], 16 * (r // 2))
                nc.scalar.activation(out8[:, r % 2, :], ps[0:H, 2 * (r % 2), :], ACT.Copy).then_inc(s_ve, 1)
                act.wait_ge(s_ve, r + 1)
                act.dma_start(o_dram[r].rearrange("g h d -> g (h d)"), out8[:, r % 2, :]).then_inc(s_vs[r % 2], 16)


            for t in range(TILES):
                r = rows_of(t)
                act.wait_ge(s_h, t + 1)
                if t >= 2:
                    act.wait_ge(s_hp, t - 1)
                nc.scalar.activation(hn[0:r, t % 2, :], x2[0:r, t % 2, :], ACT.Square, accum_out=hq[0:r, t:t + 1]).then_inc(s_hq, 1)

            def round_weights(f, w, first=False):
                act.wait_ge(s_wf[w], f * 16 + 16)
                if not first:
                    act.wait_ge((s_gm, s_um)[w], f * 3)
                nc.scalar.activation(w_parts[w][:, 0, :], raw[:, w, :], ACT.Copy).then_inc(s_hi, 1)

            act.wait_ge(s_ste, 1)
            round_weights(0, 0, True)
            round_weights(0, 1, True)

            def gate(f, last):
                act.wait_ge(s_gst, f + 1)
                for g, (a, e) in enumerate(GROUPS):
                    act.wait_ge(s_gm, f * 3 + (g + 1))
                    if e <= SEQ:
                        nc.scalar.activation(gb_p[:, 2 + a:2 + e], ps[:, g, 0:e - a], ACT.Copy).then_inc(s_gc, 1)
                    else:
                        nc.scalar.activation(gb_p[:, 2 + a:2 + SEQ], ps[:, g, 0:SEQ - a], ACT.Copy)
                        nc.scalar.activation(gb_s[:, :, 2:], ps[:, g, SEQ - a:e - a].rearrange("p (b t) -> p b t", b=SB), ACT.Copy).then_inc(s_gc, 1)
                if not last:
                    round_weights(f + 1, 0)
                act.wait_ge(s_cd2, f + 1)
                a = aT[:, bass.ds(f * TOK, TOK)]
                nc.scalar.activation(a, a, ACT.Silu).then_inc(s_si, 1)
                if not last:
                    round_weights(f + 1, 1)

            with act.Fori(0, NF - 1) as f:
                gate(f, False)
            gate(NF - 1, True)
            for half, blocks in enumerate(cs_rows):
                n = 2 + 2 * SB
                act.wait_ge(s_cst, 1)
                src = ps[0:n, 0:4, :] if half == 0 else ps[0:n, 4:6, :]
                nc.scalar.activation(blocks[0:n, :], src.rearrange("p a n -> p (a n)")[:, 0:(14, 8)[half] * P], ACT.Copy).then_inc(s_cse, 1)

            def round_down(n, f, s, pieces, first=False, raw_slot=None, loads=0):
                act.wait_ge(s_wdn[raw_slot], loads)
                if not first:
                    act.wait_ge(s_du, n - 1)
                nc.scalar.activation(d_parts[:, s, 0, :], d_raw[:, raw_slot, :], ACT.Copy)
                a, w = pieces
                nc.scalar.activation(a_parts[:, s, 0, 0:w], aT[:, bass.ds(f * TOK + a, w)], ACT.Copy).then_inc(s_dh, 1)

            def output_squares(p):
                for t in range(3 * p, 3 * p + 3):
                    r = rows_of(t)
                    for half in range(2):
                        act.wait_ge(s_y, 2 * t + half + 1)
                        if t or half:
                            act.wait_ge(s_yq, 2 * t + half)
                        nc.scalar.activation(squares[0:r, :], hx[0:r, t, half * 512:(half + 1) * 512], ACT.Square,
                                             accum_out=yq[0:r, half * TILES + t:half * TILES + t + 1]).then_inc(s_yq, 1)

            down_blocks(round_down, act, output_squares)

        @block.vector
        def _(dve):
            step = [0]

            def link(ins):
                step[0] += 1
                ins.then_inc(s_dve, 1)
                dve.wait_ge(s_dve, step[0])

            dve.wait_ge(s_cps, 1)
            nc.vector.tensor_copy(cols, ps[:, 4, 0:112]).then_inc(s_col, 1)
            dve.wait_ge(s_col, 1)

            def scale(t):
                r = rows_of(t)
                dve.wait_ge(s_root, t + 1)
                nc.vector.tensor_scalar(xring[0:r, t % 3, :], xring[0:r, t % 3, :], rstd[0:r, t:t + 1], None, ALU.mult).then_inc(s_xn, 1)

            def gain(t):
                r = rows_of(t)
                dve.wait_ge(s_xTp, t + 1)
                src = ps[:, 2 * (t % 2):2 * (t % 2) + 2, :].rearrange("p a (c t) -> p (a c) t", c=4)[:, :, 0:r]
                nc.vector.tensor_tensor(xT[:, :, t * P:t * P + r], src, g1.unsqueeze(2).to_broadcast([P, KD, r]), ALU.mult).then_inc(s_xT, 1)

            for t in range(TILES):
                scale(t)
                if t:
                    gain(t - 1)
            gain(TILES - 1)
            dve.wait_ge(s_iwp, 1)
            nc.vector.tensor_copy(iwT[0:H, :], ps[0:H, 2, 0:SROWS]).then_inc(s_iwT, 1)
            dve.wait_ge(s_iwp, 2)
            dve.wait_ge(s_built, 4)
            for b in range(SB):
                for e in range(2):
                    r = slice(e * SROWS, (e + 1) * SROWS)
                    c = e * SROWS + b * ST
                    ins = nc.vector.tensor_tensor(wd[r, b, c:c + ST], ps[r, 2, SROWS + b * ST:SROWS + (b + 1) * ST], wsel[r, :], ALU.mult)
            ins.then_inc(s_wd, 1)
            dve.wait_ge(s_toep, 1)
            link(nc.vector.tensor_copy(toep_row[0:H, :], ps[0:H, 3, 0:NEAR]))
            nc.vector.tensor_scalar(toep_row[0:H, :], toep_row[0:H, :], toep_row[0:H, 0:1], None, ALU.subtract).then_inc(s_toev, 1)

            m = 0
            for i in list(range(2, NT)) + [NT]:
                n, r = ((i + 1) * P, P) if i < NT else (SROWS, SROWS)
                sc = view("score", n, sc_off[i]) if i < NT else scn[0:r, :]
                for h in range(H):
                    dve.wait_ge(s_relu, m + 1)
                    w = iw[0:r, i, h:h + 1]
                    if h == 0:
                        ins = nc.vector.tensor_scalar(sc, rb[0:r, m % 2, 0:n], w, None, ALU.mult)
                    else:
                        ins = nc.vector.scalar_tensor_tensor(out=sc, in0=rb[0:r, m % 2, 0:n], scalar=w, in1=sc, op0=ALU.mult, op1=ALU.add)
                    m += 1
                    ins.then_inc(s_sc, 1)
                    dve.wait_ge(s_sc, m)
                dve.wait_ge(s_built, 3)
                if i < NT:
                    nc.vector.tensor_tensor(sc[:, i * P:n], sc[:, i * P:n], causal, ALU.add).then_inc(s_scm, 1)
                else:
                    nc.vector.tensor_tensor(sc, sc, own[0:r, :], ALU.add).then_inc(s_scm, 1)

            dve.wait_ge(s_scm, NT - 1)

            tiles = [(view("score", (i + 1) * P, sc_off[i]), best[:, 8 * i:8 * i + 8]) for i in range(2, NT)]
            with dve.Fori(0, TOPK // 8):
                for sc, eight in tiles:
                    nc.vector.max(eight, sc)
                nc.vector.drain()
                for sc, eight in tiles:
                    nc.vector.match_replace(sc, eight, sc, TAKEN)
                nc.vector.drain()
            for sc, eight in tiles:
                nc.vector.tensor_scalar(sc, sc, -2e38, NEG, ALU.is_gt, ALU.mult).then_inc(s_topk, 1)

            dve.wait_ge(s_tod, 16)
            dve.wait_ge(s_scn, 16)
            dve.wait_ge(s_cs, 1)
            sc = scd[:, 0:SCORES]
            with dve.Fori(0, TOPK // 8) as it:
                nc.vector.max(m8, sc)
                nc.vector.drain()
                nc.vector.max_index(i8, m8, sc)
                nc.vector.tensor_copy(val[:, bass.ds(it * 8, 8)], m8)
                nc.vector.drain()
                nc.vector.match_replace(sc, m8, sc, TAKEN)
                nc.vector.tensor_copy(pos[:, bass.ds(it * 8, 8)], i8)
                nc.vector.drain()
            nc.vector.drain().then_inc(s_list, 1)

            rows = slice(0, SROWS)
            a_v, a_p, b_v, b_p = val[rows], pos[rows], reverse(val_b[rows]), reverse(pos_b[rows])
            lo_, pg, rf, tf = low[rows], page_of[rows], rows_f[rows], turn_f[rows]
            ia, ib = int_a[rows].bitcast(I32), int_b[rows].bitcast(I32)
            dve.wait_ge(s_move, 32)
            dve.wait_ge(s_rows, 16 * (2 + SB))
            link(nc.vector.tensor_tensor(lo_, a_v, b_v, ALU.is_ge))
            link(nc.vector.tensor_scalar(pg, b_p, float(HALF), None, ALU.add))
            link(nc.vector.tensor_tensor(a_p, a_p, pg, ALU.subtract))
            link(nc.vector.tensor_tensor(a_p, a_p, lo_, ALU.mult))
            link(nc.vector.tensor_tensor(a_p, a_p, pg, ALU.add))
            link(nc.vector.tensor_copy(ia, a_p))
            link(nc.vector.tensor_scalar(ib, ia, 7, None, ALU.logical_shift_right))
            link(nc.vector.tensor_copy(pg, ib))
            link(nc.vector.tensor_scalar(ib, ia, PAGE - 1, None, ALU.bitwise_and))
            link(nc.vector.tensor_copy(rf, ib))
            link(nc.vector.tensor_copy(ptab_f[rows], ptab_i[rows]))
            link(nc.vector.tensor_scalar(ptab_f[rows], ptab_f[rows], float(PAGE), None, ALU.mult))
            for j in range(NPAGES):
                link(nc.vector.tensor_scalar(lo_, pg, float(j), ptab_f[rows, j:j + 1], ALU.is_equal, ALU.mult))
                link(nc.vector.tensor_tensor(rf, rf, lo_, ALU.add))
            link(nc.vector.tensor_scalar(tf, a_p, -1.0, row_t[rows], ALU.mult, ALU.add))
            link(nc.vector.tensor_scalar(lo_, a_p, float(PAST), -1000.0, ALU.is_ge, ALU.mult))
            nc.vector.tensor_tensor(tf, tf, lo_, ALU.add).then_inc(s_pick, 1)
            own_hits = prod[rows, 0:ST * P].rearrange("p (t n) -> p t n", t=ST)
            dve.wait_ge(s_mm, 7 * TILES)
            link(nc.vector.tensor_scalar(a_p, a_p, row_new[rows], None, ALU.subtract))
            for c in range(2):
                for t in range(ST):
                    link(nc.vector.tensor_scalar(own_hits[:, t, :], a_p[:, c * P:(c + 1) * P], float(t), None, ALU.is_equal))
                link(nc.vector.tensor_reduce(sel_new[rows] if c == 0 else sel_new2[rows], own_hits, AX_X, ALU.add))
            link(nc.vector.tensor_tensor(sel_new[rows], sel_new[rows], sel_new2[rows], ALU.add))
            nm = new_mask[rows]
            nm3 = nm.rearrange("p (b t) -> p b t", b=SB)
            link(nc.vector.tensor_scalar(nm, own[rows, :], -1.0, None, ALU.is_ge))
            link(nc.vector.tensor_tensor(nm3, nm3, sel_new[rows].unsqueeze(1).to_broadcast([SROWS, SB, ST]), ALU.mult))
            nc.vector.tensor_scalar(nm, nm, -1.0, -NEG, ALU.add, ALU.mult).then_inc(s_pick, 1)
            dve.wait_ge(s_pickT, 1)
            nc.vector.tensor_copy(idxT, ps[:, 0, 0:P].rearrange("p (c r) -> p c r", c=2)).then_inc(s_idx, 1)
            link(nc.vector.tensor_copy(distT, ps[:, 0, P:2 * P]))
            link(nc.vector.tensor_copy(new_maskT[rows], ps[rows, 0, 2 * P:2 * P + SROWS]))
            nc.vector.drain().then_inc(s_nmT, 1)

            def sampled_bias():
                dve.wait_ge(s_db, 16 * 4)
                dve.wait_ge(s_b31, 16 * 9)
                nc.vector.tensor_scalar(reached, reached, first_of, None, ALU.is_ge)
                nc.vector.tensor_tensor(step_k, step_k, step_j, ALU.subtract).then_inc(s_ind, 1)
                link(nc.vector.tensor_scalar(reach, distT, 0.0, NEG, ALU.is_lt, ALU.mult))
                dve.wait_ge(s_sbT, 1)
                nc.vector.tensor_tensor(sbias.rearrange("p c (r h) -> p (c r) h", h=H),
                                        ps[:, 0:2, :].rearrange("p c (r h) -> p (c r) h", h=H),
                                        reach.unsqueeze(2).to_broadcast([P, P, H]), ALU.add).then_inc(s_sbe, 1)

            sampled_bias()

            def normalise(h):
                dve.wait_ge(s_pv, (h + 1) * (NT // 2))
                up, dn = ps[HD:P, 6:8, :].rearrange("p a n -> p (a n)"), ps[0:HD, 6:8, :].rearrange("p a n -> p (a n)")
                link(nc.vector.reciprocal(rl[0:HD, :], up))
                nc.vector.tensor_tensor(mixT[(h % 2) * HD:(h % 2 + 1) * HD, PAIRS + h // 2, 0:SEQ], dn, rl[0:HD, :], ALU.mult).then_inc(s_po, 1)
                dve.wait_ge(s_po, h + 1)

            dve.wait_ge(s_topk, NT - 2)
            m = 0
            for h in range(H):
                for i in range(NT):
                    n = (i + 1) * P
                    r = h * NT + i
                    dve.wait_ge(s_kg[r % 4], 32 * (r // 4 + 1))
                    dve.wait_ge(s_qr[r % 4], 16 * (r // 4 + 1))
                    if r:
                        dve.wait_ge(s_kd, r)
                    nc.vector.scalar_tensor_tensor(out=prod.rearrange("p (c n) -> p c n", c=2), in0=kv[:, r % 4, :].rearrange("p (c n) -> p c n", c=2),
                                                   scalar=HD ** -0.5, in1=qrow[:, r % 4, :].unsqueeze(1).to_broadcast([P, 2, W]),
                                                   op0=ALU.mult, op1=ALU.mult).then_inc(s_kp, 1)
                    dve.wait_ge(s_S, m + 1)
                    if m >= 2:
                        dve.wait_ge(s_T, turned_after(m - 2))
                    l = rb[:, m % 2, 0:n]
                    mask = causal if i == 0 else near_mask if i == 1 else view("score", n, sc_off[i])
                    src = ps[:, 2 * (m % 2):2 * (m % 2) + 2, :].rearrange("p a n -> p (a n)")[:, 0:n]
                    nc.vector.tensor_tensor_reduce(out=l, in0=src, in1=mask, scale=-1.0, scalar=3e38, op0=ALU.add, op1=ALU.min,
                                                   accum_out=neg_max[:, m % 2:m % 2 + 1]).then_inc(s_L, 1)
                    m += 1
                    dve.wait_ge(s_kp, r + 1)
                    nc.vector.tensor_reduce(lg[:, :, r * H:(r + 1) * H], prod.rearrange("p (c h d) -> p c h d", c=2, h=H),
                                            AX_X, ALU.add).then_inc(s_kd, 1)
                    if h and i == 1:
                        normalise(h - 1)
            normalise(H - 1)

            dve.wait_ge(s_kd, SROWS)
            link(nc.vector.tensor_tensor(lg, lg, sbias, ALU.add))
            l3 = ln[rows].rearrange("p (r h) -> p r h", h=H)
            dve.wait_ge(s_ln, 1)
            link(nc.vector.tensor_tensor(l3, l3, new_maskT[rows].unsqueeze(2).to_broadcast([SROWS, SROWS, H]), ALU.add))
            link(nc.vector.tensor_tensor(l3, l3, b31[rows].unsqueeze(1).to_broadcast([SROWS, SROWS, H]), ALU.add))
            dve.wait_ge(s_nbT, 1)
            l4 = ln[rows].rearrange("p (b q h) -> p b q h", b=SB, q=ST)
            nb = new_bias[rows].rearrange("p (h q) -> p q h", h=H)
            link(nc.vector.tensor_copy(new_bias[rows], ps[rows, 1, 0:SROWS]))
            link(nc.vector.tensor_tensor(l4, l4, nb.unsqueeze(1).to_broadcast([SROWS, SB, ST, H]), ALU.add))
            link(nc.vector.tensor_tensor(mx, lg[:, 0, :], lg[:, 1, :], ALU.max))
            nc.vector.tensor_tensor(mx[rows], mx[rows], ln[rows], ALU.max).then_inc(s_dg, 1)
            dve.wait_ge(s_mxT, 1)
            link(nc.vector.tensor_reduce(top_col, ps[:, 2, :].rearrange("p (k n) -> p k n", k=4), AX_X, ALU.max))
            for k in range(4):
                ins = nc.vector.tensor_scalar(diag[:, k * P:(k + 1) * P], ident, top_col[:, k:k + 1], None, ALU.mult)
            ins.then_inc(s_dg, 1)
            dve.wait_ge(s_mb, 1)
            for c in range(2):
                nc.vector.tensor_tensor(lg[:, c, :], lg[:, c, :], ps[:, 3, :], ALU.subtract).then_inc(s_lm, 1)
            nc.vector.tensor_tensor(ln[rows], ln[rows], ps[rows, 3, :], ALU.subtract).then_inc(s_lm, 1)
            dve.wait_ge(s_le, 1)
            link(nc.vector.tensor_tensor(mx, lg[:, 0, :], lg[:, 1, :], ALU.add))
            nc.vector.tensor_tensor(mx[rows], mx[rows], ln[rows], ALU.add).then_inc(s_ls, 1)
            dve.wait_ge(s_lb, 1)
            link(nc.vector.reciprocal(mx, ps[:, 2, :]))
            for c in range(2):
                nc.vector.tensor_tensor(lg[:, c, :], lg[:, c, :], mx, ALU.mult)
            nc.vector.tensor_tensor(ln[rows], ln[rows], mx[rows], ALU.mult).then_inc(s_pn, 1)
            dve.wait_ge(s_oh, 16)
            dve.wait_ge(s_nd, 1)
            nc.vector.tensor_tensor(qrow[rows, 1, :], qrow[rows, 1, :], ps[rows, 1, :], ALU.add).then_inc(s_os, 1)
            dve.wait_ge(s_oT, 1)
            nc.vector.tensor_copy(mixT[:, PAIRS:, SEQ:TOK], ps[:, 3, :].rearrange("p (c t) -> p c t", c=PAIRS)[:, :, 0:SROWS]).then_inc(s_oTe, 1)


            dve.wait_ge(s_stp, 1)
            nc.vector.tensor_copy(st, ps[:, 4, 0:NF * 2 * SB].rearrange("p (f s) -> p f s", f=NF)).then_inc(s_ste, 1)

            def gain2(t):
                r = rows_of(t)
                dve.wait_ge(s_hp, t + 1)
                src = ps[:, 4 + 2 * (t % 2):6 + 2 * (t % 2), :].rearrange("p a (c t) -> p (a c) t", c=4)[:, :, 0:r]
                tok = slice(t * P, t * P + r)
                for c in range(KD):
                    ins = nc.vector.tensor_scalar(hT[0][c][:, tok], src[:, c, :], g2[:, c:c + 1], None, ALU.mult)
                link(ins)
                for c in range(KD):
                    ins = nc.vector.scalar_tensor_tensor(out=hT[1][c][:, tok], in0=src[:, c, :], scalar=g2[:, c:c + 1],
                                                         in1=hT[0][c][:, tok].bitcast(F32), op0=ALU.mult, op1=ALU.subtract)
                ins.then_inc(s_hT, 1)

            for t in range(TILES):
                r = rows_of(t)
                dve.wait_ge(s_mo, t + 1)
                dve.wait_ge(s_x2[t % 2], 16 * (t // 2 + 1))
                src = ps[0:r, 2 * (t % 2):2 * (t % 2) + 2, :].rearrange("p a n -> p (a n)")
                nc.vector.tensor_tensor(x2[0:r, t % 2, :], src, x2[0:r, t % 2, :], ALU.add).then_inc(s_h, 1)
                if t:
                    gain2(t - 1)
                dve.wait_ge(s_root, TILES + t + 1)
                nc.vector.tensor_scalar(hn[0:r, t % 2, :], x2[0:r, t % 2, :], hr[0:r, t:t + 1], None, ALU.mult).then_inc(s_hn, 1)
            gain2(NT)

            def split_weights(f, w):
                dve.wait_ge(s_hi, f * 2 + (w + 1))
                nc.vector.tensor_tensor(w_parts[w][:, 1, :], raw[:, w, :], w_parts[w][:, 0, :].bitcast(F32), ALU.subtract).then_inc(s_sp, 1)

            split_weights(0, 0)
            split_weights(0, 1)

            def conv(f, last):
                dve.wait_ge(s_gc, f * 3 + 3)
                a = aT[:, bass.ds(f * TOK, SEQ)]
                a_s = aT[:, bass.ds(f * TOK + SEQ, SROWS)].rearrange("p (b t) -> p b t", b=SB)
                for j in (2, 1, 0):
                    w = cw[:, bass.ds(f + j * NF, 1)]
                    for out, src in ((a, gb_p[:, j:j + SEQ]), (a_s, gb_s[:, :, j:j + ST])):
                        if j == 2:
                            nc.vector.tensor_scalar(out, src, w, cb[:, bass.ds(f, 1)], ALU.mult, ALU.add)
                        else:
                            nc.vector.scalar_tensor_tensor(out=out, in0=src, scalar=w, in1=out, op0=ALU.mult, op1=ALU.add)
                    if j:
                        nc.vector.drain()
                nc.vector.drain().then_inc(s_cd2, 1)
                if not last:
                    split_weights(f + 1, 0)
                dve.wait_ge(s_si, f + 1)
                for g, (b, e) in enumerate(GROUPS):
                    dve.wait_ge(s_um, f * 3 + (g + 1))
                    o = aT[:, bass.ds(f * TOK + b, e - b)]
                    nc.vector.tensor_tensor(o, o, ps[:, 3 + g, 0:e - b], ALU.mult).then_inc(s_ag, 1)

                if not last:
                    split_weights(f + 1, 1)

            with dve.Fori(0, NF - 1) as f:
                conv(f, False)
            conv(NF - 1, True)

            def split_down(n, f, s, pieces, first=False, raw_slot=None, loads=0):
                dve.wait_ge(s_dh, n + 1)
                a, w = pieces
                nc.vector.tensor_tensor(d_parts[:, s, 1, :], d_raw[:, raw_slot, :], d_parts[:, s, 0, :].bitcast(F32), ALU.subtract)
                nc.vector.tensor_tensor(a_parts[:, s, 1, 0:w], aT[:, bass.ds(f * TOK + a, w)], a_parts[:, s, 0, 0:w].bitcast(F32),
                                        ALU.subtract).then_inc(s_ds, 1)

            def outputs(p):
                for t in range(3 * p, 3 * p + 3):
                    r = rows_of(t)
                    if t == 0:
                        dve.wait_ge(s_hl, 32)
                        dve.wait_ge(s_fg, 16)
                    dve.wait_ge(s_du, (p + 1) * NF)
                    for half in range(2):
                        o = hx[0:r, t, half * 512:(half + 1) * 512]
                        nc.vector.tensor_tensor(o, o, ps[0:r, 2 * (t % 3) + half, :], ALU.add).then_inc(s_y, 1)
                for t in range(3 * p, 3 * p + 3):
                    r = rows_of(t)
                    dve.wait_ge(s_root, 2 * TILES + t + 1)
                    nc.vector.scalar_tensor_tensor(out=hx[0:r, t, :], in0=hx[0:r, t, :], scalar=yr[0:r, t:t + 1], in1=final_g[0:r, :],
                                                   op0=ALU.mult, op1=ALU.mult).then_inc(s_yn, 1)

            down_blocks(split_down, dve, outputs)

        @block.tensor
        def _(pe):
            pe.wait_ge(s_built, 1)
            pe.wait_ge(s_const, 16 * 7)
            nc.tensor.transpose(ps[:, 4, 0:112], rows_in[0:112, :], ident[0:112, 0:112]).then_inc(s_cps, 1)
            for t in range(TILES):
                r = rows_of(t)
                pe.wait_ge(s_xn, t + 1)
                if t >= 2:
                    pe.wait_ge(s_xT, t - 1)
                for c in range(KD):
                    o = ps[:, 2 * (t % 2) + c // 4, (c % 4) * P:(c % 4) * P + r]
                    ins = nc.tensor.transpose(o, xring[0:r, t % 3, c * P:(c + 1) * P], ident[0:r, 0:r])
                ins.then_inc(s_xTp, 1)

            def project_tile(c, t):
                n, r, width = n_of(c, t), rows_of(t), CHUNKS[c][2]
                pe.wait_ge(s_w[c % 2], 16 * (c // 2 + 1))
                pe.wait_ge(s_xT, t + 1)
                if n >= 2:
                    pe.wait_ge(s_z, n - 1)
                if n == 0:
                    pe.wait_ge(s_col, 1)
                w = wring[:, c % 2, 0:KD * width].rearrange("p (k n) -> p k n", k=KD)
                for k in range(KD):
                    ins = nc.tensor.matmul(ps[0:r, 4 + n % 2, 0:width], xT[:, k, t * P:t * P + r], w[:, k, :],
                                           start=(k == 0), stop=(k == KD - 1))
                ins.then_inc(s_mm, 1)

            def transpose_z(job):
                c, t = job
                i = tjob_at[job]
                cc = 1 if c == "dup" else c
                n, r = n_of(cc, t), rows_of(t)
                pe.wait_ge(*((s_twice, 1) if c == "dup" else (s_z, n + 1)))
                if i >= 2:
                    pe.wait_ge(s_tev, i - 1)
                for b in range({0: 1, "dup": H}.get(c, PAIRS)):
                    if c == "dup":
                        src = twice[0:r, b * P:(b + 1) * P]
                        o = ps[:, 6 + i % 2, b * SROWS:(b + 1) * SROWS]
                    else:
                        src = zr[0:r, n % 3, b * P:(b + 1) * P]
                        o = ps[:, 6 + i % 2, b * P:b * P + r]
                    ins = nc.tensor.transpose(o, src, ident[0:r, 0:r])
                ins.then_inc(s_tz, 1)

            def project(chunks):
                last = None
                for c in chunks:
                    for t in range(TILES):
                        project_tile(c, t)
                        if last and last[0] < 4:
                            transpose_z(last)
                        if last == (1, NT):
                            transpose_z(("dup", NT))
                        last = (c, t)
                if last[0] < 4:
                    transpose_z(last)
                if last == (1, NT):
                    transpose_z(("dup", NT))

            project([0, 1])
            nc.tensor.transpose(ps[0:H, 2, 0:SROWS], iw[0:SROWS, NT, :], ident[0:SROWS, 0:SROWS]).then_inc(s_iwp, 1)
            pe.wait_ge(s_iwT, 1)
            nc.tensor.matmul(ps[:, 2, SROWS:2 * SROWS], wrep[0:H, :], iwT[0:H, :], start=True, stop=True).then_inc(s_iwp, 1)
            pe.wait_ge(s_rel, 32)
            nc.tensor.matmul(ps[0:H, 3, 0:NEAR], relb[0:BUCKETS, :], hot[0:BUCKETS, :], start=True, stop=True).then_inc(s_toep, 1)
            pe.wait_ge(s_wd, 1)
            pe.wait_ge(s_toev, 1)
            m = 0
            pe.wait_ge(s_tev, 2 * TILES + 1)
            for i in list(range(2, NT)) + [NT]:
                n, r, k0 = ((i + 1) * P, P, 0) if i < NT else (SROWS, SROWS, SEQ)
                for h in range(H):
                    lo = (h % 2) * HD
                    if m >= 2:
                        pe.wait_ge(s_relu, m - 1)
                    for a in range(0, n, 512):
                        e = min(n, a + 512)
                        ins = nc.tensor.matmul(ps[0:r, 2 * (m % 2) + a // 512, 0:e - a],
                                               iqT[lo:lo + HD, h // 2, i * P:i * P + r],
                                               ikT[lo:lo + HD, k0 + a:k0 + e], start=True, stop=True)
                    ins.then_inc(s_dot, 1)
                    m += 1
            def turn_index_pages(un):
                b, half = divmod(un, 2)
                pe.wait_ge(s_ikc[half], 16 * 16 * (b + 1))
                pe.wait_ge(*((s_cT, un) if un else (s_relu, m)))
                for j in range(8):
                    ins = nc.tensor.transpose(ps[:, j // 4, (j % 4) * P:(j % 4 + 1) * P],
                                              ikc[:, half, j, :, :].rearrange("p e d -> p (e d)"), ident)
                ins.then_inc(s_ct, 1)

            turn_index_pages(0)
            for un in range(2 * SB):
                b, half = divmod(un, 2)
                if un + 1 < 2 * SB:
                    turn_index_pages(un + 1)
                pe.wait_ge(s_cT, un + 1)
                for r2 in range(2):
                    if un:
                        pe.wait_ge(s_cr, 2 * (un - 1) + r2 + 1)
                    for e in range(2):
                        r = slice(e * SROWS, (e + 1) * SROWS)
                        ins = nc.tensor.matmul(ps[r, 2 + r2, :], iqd[r, b, :], ikcT[r, half, r2 * 512:(r2 + 1) * 512], start=True, stop=True)
                    ins.then_inc(s_cd, 1)
                for r2 in range(2):
                    pe.wait_ge(s_cr, 2 * un + r2 + 1)
                    nc.tensor.matmul(ps[:, 4 + 2 * half + r2, :], wd[:, b, :], rb4[:, r2, :], start=(b == 0), stop=(b == SB - 1),
                                     skip_group_check=True).then_inc(s_ch, 1)
            pe.wait_ge(s_cs, 1)
            project([2])
            pe.wait_ge(s_ws, 16)
            for h in range(H):
                ins = nc.tensor.transpose(ps[:, h // 4, (h % 4) * P:(h % 4 + 1) * P], ws_in[:, h, :], ident)
            ins.then_inc(s_wsp, 1)
            project([3, 4, 5, 6])

            pe.wait_ge(s_vn, TILES)
            pe.wait_ge(s_wsd, 16 * 2 * SB)
            for h in range(H):
                c = slice(h * HD, (h + 1) * HD)
                pe.wait_ge(*((s_sb, h - 1) if h >= 2 else (s_wse, 1)))
                nc.tensor.matmul(ps[:, h % 2, :], wsT[:, h, :], vn[:, 0:NT, c], start=True, stop=True)
                nc.tensor.matmul(ps[0:SROWS, 2 + h % 2, 0:HD], wsd[0:SROWS, h, :], vn[0:SROWS, NT, c], start=True, stop=True).then_inc(s_sg, 1)
            pe.wait_ge(s_qbd, 2)
            for c in range(PAIRS):
                ins = nc.tensor.matmul(ps[0:SROWS, 5, :].rearrange("p (b c n) -> p b c n", b=SB, c=PAIRS)[:, :, c, :],
                                       kT[:, c, SEQ:TOK], qbd[:, :, c, :], start=True, stop=True)
            ins.then_inc(s_kn, 1)
            pe.wait_ge(s_au, H)
            for t in range(TILES):
                r = rows_of(t)
                if t >= 2:
                    pe.wait_ge(s_am, t - 1)
                for c in range(PAIRS):
                    ins = nc.tensor.transpose(ps[:, 6 + t % 2, c * P:c * P + r], u[0:r, t, c * P:(c + 1) * P], ident[0:r, 0:r])
                ins.then_inc(s_at, 1)

            pe.wait_ge(s_pick, 2)
            pe.wait_ge(s_am, TILES)
            for k, src in enumerate((rows_f, turn_f)):
                for c in range(2):
                    nc.tensor.transpose(ps[:, 0, k * P + c * SROWS:k * P + (c + 1) * SROWS], src[0:SROWS, c * P:(c + 1) * P],
                                        ident[0:SROWS, 0:SROWS])
            nc.tensor.transpose(ps[0:SROWS, 0, 2 * P:2 * P + SROWS], new_mask[0:SROWS, :], ident[0:SROWS, 0:SROWS]).then_inc(s_pickT, 1)
            pe.wait_ge(s_nmT, 1)
            pe.wait_ge(s_ind, 1)
            for a in range(SROWS // 4):
                for c in range(2):
                    ins = nc.tensor.matmul(ps[:, c, :].rearrange("p (g a h) -> p g a h", g=4, h=H)[:, :, a, :],
                                           reached[:, a * TOPK + c * P:a * TOPK + (c + 1) * P], step_k, start=True, stop=True)
            ins.then_inc(s_sbT, 1)
            pe.wait_ge(s_sbe, 1)

            def logits(m):
                h, i = divmod(m, NT)
                n, lo = (i + 1) * P, (h % 2) * HD
                if m >= 2:
                    pe.wait_ge(s_L, m - 1)
                near = max(n - 2 * P, 0)
                for a in range(0, n, 512):
                    e = min(n, a + 512)
                    o = ps[:, 2 * (m % 2) + a // 512, :]
                    nc.tensor.matmul(o[:, 0:e - a], qT[lo:lo + HD, h // 2, i * P:(i + 1) * P], kT[lo:lo + HD, h // 2, a:e],
                                     start=True, stop=True)
                for a in range(0, n, 512):
                    c, e = max(a, near), min(n, a + 512)
                    if c < e:
                        first = c - (n - 2 * P)
                        ins = nc.tensor.matmul(ps[:, 2 * (m % 2) + a // 512, c - a:e - a], ident, bn[:, h, first:first + e - c],
                                               start=False, stop=True, skip_group_check=True)
                ins.then_inc(s_S, 1)

            def head_values(h, i):
                if i == 1:
                    pe.wait_ge(s_vo[h % 2], 16 * (h // 2 + 1))
                    if h:
                        pe.wait_ge(s_po, h)
                pe.wait_ge(s_Te, turned_after(h * NT + i))
                for k in range(i + 1):
                    a, e = max(i - 1, k) * P, (i + 1) * P
                    ins = nc.tensor.matmul(ps[:, 6 + a // 512, a % 512:a % 512 + e - a], vone[:, h % 2, k, :], pT[:, k, a:e],
                                           start=(k == 0), stop=(k == i), skip_group_check=True)
                ins.then_inc(s_pv, 1)

            g = 0
            pe.wait_ge(s_bn, 16)
            pe.wait_ge(s_built, 5)
            logits(0)
            for m in range(H * NT):
                h, i = divmod(m, NT)
                if m + 1 < H * NT:
                    logits(m + 1)
                pe.wait_ge(s_E, m + 1)
                for blocks in probs_groups(i):
                    if g >= 2:
                        pe.wait_ge(s_Te, g - 1)
                    for k in blocks:
                        ins = nc.tensor.transpose(ps[:, 4 + g % 2, (k % 4) * P:(k % 4 + 1) * P], rb[:, m % 2, k * P:(k + 1) * P], ident)
                    ins.then_inc(s_T, 1)
                    g += 1
                if m and i % 2 == 0:
                    head_values(*((h, i - 1) if i else (h - 1, NT - 1)))
            head_values(H - 1, NT - 1)

            pe.wait_ge(s_nbs, 1)
            for h in range(H):
                ins = nc.tensor.transpose(ps[0:SROWS, 1, h * ST:(h + 1) * ST], own_near(h), ident[0:ST, 0:ST])
            ins.then_inc(s_nbT, 1)
            pe.wait_ge(s_dg, 1)
            for k in range(4):
                ins = nc.tensor.transpose(ps[:, 2, k * P:(k + 1) * P], mx[:, k * P:(k + 1) * P], ident)
            ins.then_inc(s_mxT, 1)
            pe.wait_ge(s_dg, 2)
            nc.tensor.matmul(ps[:, 3, :], ones, diag, start=True, stop=True).then_inc(s_mb, 1)
            pe.wait_ge(s_ls, 1)
            nc.tensor.matmul(ps[:, 2, :], ones, mx, start=True, stop=True).then_inc(s_lb, 1)
            pe.wait_ge(s_pn, 1)
            pe.wait_ge(s_vnl, 16)
            for h in range(H):
                ins = nc.tensor.matmul(ps[0:SROWS, 1, h * HD:(h + 1) * HD], ln[0:SROWS, :].rearrange("p (r h) -> p r h", h=H)[:, :, h],
                                       qrow[0:SROWS, 0, h * HD:(h + 1) * HD], start=True, stop=True)
            ins.then_inc(s_nd, 1)
            for r in range(SROWS):
                pe.wait_ge(s_kg[r % 4], 32 * (SROWS // 4 + r // 4 + 1))
                if r >= 2:
                    pe.wait_ge(s_ve, r - 1)
                for c in range(2):
                    ins = nc.tensor.matmul(ps[0:H, 2 * (r % 2), :], lg[:, c, r * H:(r + 1) * H], kv[:, r % 4, c * W:(c + 1) * W],
                                           start=(c == 0), stop=(c == 1))
                ins.then_inc(s_vd, 1)
            pe.wait_ge(s_os, 1)
            for c in range(PAIRS):
                ins = nc.tensor.transpose(ps[:, 3, c * P:c * P + SROWS], qrow[0:SROWS, 1, c * P:(c + 1) * P], ident[0:SROWS, 0:SROWS])
            ins.then_inc(s_oT, 1)

            pe.wait_ge(s_st, 16)
            for f in range(NF):
                ins = nc.tensor.transpose(ps[:, 4, f * 2 * SB:(f + 1) * 2 * SB], state_rows[0:2 * SB, f * P:(f + 1) * P],
                                          ident[0:2 * SB, 0:2 * SB])
            ins.then_inc(s_stp, 1)

            def turn_residual(t):
                r = rows_of(t)
                pe.wait_ge(s_hn, t + 1)
                pe.wait_ge(*((s_hT, t - 1) if t >= 2 else (s_ste, 1)))
                for c in range(KD):
                    ins = nc.tensor.transpose(ps[:, 4 + 2 * (t % 2) + c // 4, (c % 4) * P:(c % 4) * P + r], hn[0:r, t % 2, c * P:(c + 1) * P],
                                              ident[0:r, 0:r])
                ins.then_inc(s_hp, 1)

            pe.wait_ge(s_po, H)
            pe.wait_ge(s_oTe, 1)
            for t in range(TILES):
                r = rows_of(t)
                if t >= 2:
                    pe.wait_ge(s_h, t - 1)
                for half in range(2):
                    pe.wait_ge(s_wo[half], 16)
                    for k in range(KD):
                        ins = nc.tensor.matmul(ps[0:r, 2 * (t % 2) + half, :], mixT[:, k, t * P:t * P + r],
                                               wo[:, k, half * 512:(half + 1) * 512], start=(k == 0), stop=(k == KD - 1))
                ins.then_inc(s_mo, 1)
                if t:
                    turn_residual(t - 1)
            turn_residual(NT)

            def ffn_block(f, first=False):
                for w, done in ((0, s_gm), (1, s_um)):
                    pe.wait_ge(s_sp, f * 2 + (w + 1))
                    for g, (a, e) in enumerate(GROUPS):
                        if not first:
                            pe.wait_ge((s_gc, s_ag)[w], f * 3 + (g - 2))
                        for k in range(KD):
                            for n, (i, j) in enumerate(((0, 0), (0, 1), (1, 0))):
                                ins = nc.tensor.matmul(ps[:, 3 * w + g, 0:e - a], w_parts[w][:, i, k * P:(k + 1) * P], hT[j][k][:, a:e],
                                                       start=(k + n == 0), stop=(k + n == KD + 1))
                        ins.then_inc(done, 1)

            pe.wait_ge(s_hT, TILES)
            ffn_block(0, True)
            with pe.Fori(1, NF) as f:
                ffn_block(f)

            pe.wait_ge(s_gst, NF + 1)
            pe.wait_ge(s_ag, 3 * NF)
            for f in range(NF):
                bank, c = divmod(f, 4) if f < 14 else (4 + (f - 14) // 4, (f - 14) % 4)
                ins = nc.tensor.transpose(ps[0:2 + 2 * SB, bank, c * P:(c + 1) * P], cs[:, f, :], ident)
            ins.then_inc(s_cst, 1)

            pe.wait_ge(s_cse, 2)

            def down(n, f, s, pieces, first=False, raw_slot=None, loads=0):
                p = pieces[0] // (3 * P)
                pe.wait_ge(s_ds, n + 1)
                start, stop = isinstance(f, int) and f == 0, isinstance(f, int) and f == NF - 1
                for j in range(3):
                    t = 3 * p + j
                    r = rows_of(t)
                    if start and p:
                        pe.wait_ge(s_y, 6 * (p - 1) + 2 * j + 2)
                    for half in range(2):
                        for q, (x, y) in enumerate(((0, 0), (0, 1), (1, 0))):
                            ins = nc.tensor.matmul(ps[0:r, 2 * j + half, :], a_parts[:, s, x, j * P:j * P + r],
                                                   d_parts[:, s, y, half * 512:(half + 1) * 512],
                                                   start=start and q == 0, stop=stop and q == 2)
                ins.then_inc(s_du, 1)

            down_blocks(down, pe, lambda p: None)


OUTS = [("y_p", (1, SEQ, D)), ("y_s", (SB, ST, D)), ("k_p", (1, 1, SEQ, H, HD)), ("v_p", (1, 1, SEQ, H, HD)),
        ("idx_k_p", (1, 1, SEQ, HD)), ("conv_p", (1, 1, 2, DFF)), ("k_s", (1, SB, ST, H, HD)),
        ("v_s", (1, SB, ST, H, HD)), ("idx_k_s", (1, SB, ST, HD)), ("conv_s", (1, SB, 2, DFF)),
        ("chunk_v_s", (1, SB, ST, H, HD))]


def constants():
    rep = np.zeros((H, P), np.float32)
    sel = np.zeros((P, ST), np.float32)
    for c in range(P):
        rep[(c // ST) % H, c] = 1.0
        sel[c, c % ST] = 1.0
    hot = np.zeros((BUCKETS, NEAR), np.float32)
    for y in range(NEAR):
        hot[BUCKET_OF[max(2 * P - 1 - y, 0)], y] = 1.0
    first = np.array([[FIRST_OF[k]] for _ in range(P // BUCKETS) for k in range(BUCKETS)], np.float32)
    rows = np.zeros((SROWS, 2), np.float32)
    for r in range(SROWS):
        rows[r] = (PAST + r % ST, PAST + r // ST * ST)
    return {"c_rep": rep, "c_sel": sel, "c_hot": hot, "c_rows": rows, "c_first": first}


def kernel(**inputs):
    import concourse.bacc as bacc
    from concourse.bass_utils import run_bass_kernel_spmd as run

    nc = bacc.Bacc("TRN2", target_bir_lowering=False, num_devices=1)
    arrays, io = {}, {}
    for name, a in list(inputs.items()) + list(constants().items()):
        a = np.ascontiguousarray(a)
        arrays["in_" + name] = a
        io[name] = nc.dram_tensor("in_" + name, a.shape, mybir.dt.from_np(a.dtype), kind="ExternalInput").ap()
    for name, shape in OUTS:
        io[name] = nc.dram_tensor("out_" + name, shape, F32, kind="ExternalOutput").ap()
    io["pool"] = inputs["cache_k"].shape[1]
    program(nc, io)
    r = run(nc, [arrays], core_ids=[0])
    return tuple(r.results[0]["out_" + name] for name, _ in OUTS)
```

```python
from contextlib import ExitStack

import numpy as np
import concourse.bass as bass
from concourse import mybir

F32 = mybir.dt.float32
F32R = mybir.dt.float32r
I32 = mybir.dt.int32
U32 = mybir.dt.uint32
ALU = mybir.AluOpType
ACT = mybir.ActivationFunctionType
AX_X = mybir.AxisListType.X

P = 128
D = 1024
KD = D // P
SEQ = 1024
NT = SEQ // P
SB, ST = 8, 8
SROWS = SB * ST
TILES = NT + 1
TOK = SEQ + SROWS
H, HD = 8, 64
W = H * HD
PAIRS = H // 2
PAGE = 128
NPAGES = 32
PAST = PAGE * NPAGES
TOPK = 256
DFF = 2816
NF = DFF // P
BUCKETS = 32
EPS = 1e-6
NEG = -1e30
TAKEN = -3e38
HALF = PAST // 2
SCORES = HALF + SROWS
GROUPS = ((0, 364), (364, 728), (728, TOK))
PASSES = TILES // 3
NEAR = 3 * P

CHUNKS = [("small", 6 * W, H + HD), ("iq", 5 * W, W), ("q", 2 * W, W), ("k", 3 * W, W), ("v", 4 * W, W),
          ("ua", 0, W), ("va", W, W)]
VEC_ROWS = [("g1", KD), ("g2", KD), ("cw", 3 * NF), ("cb", NF), ("bs", H)]


_DIST = np.arange(1, 4 * P, dtype=np.float32)
_LARGE = BUCKETS // 2 + (np.log(_DIST / np.float32(BUCKETS // 2)) / np.float32(np.log(128 / (BUCKETS // 2)))
                         * np.float32(BUCKETS // 2)).astype(np.int32)
BUCKET_OF = np.concatenate([[0], np.where(_DIST < BUCKETS // 2, _DIST.astype(np.int32), np.minimum(_LARGE, BUCKETS - 1))])
FIRST_OF = [int(np.argmax(BUCKET_OF == k)) for k in range(BUCKETS)]


def reverse(x):
    (step, rows), (_, n) = x.ap
    return bass.AP(tensor=x.tensor, offset=x.offset + n - 1, ap=[[step, rows], [-1, n]])


def rows_of(t):
    return P if t < NT else SROWS


def program(nc, io):
    ctx = ExitStack()
    with ctx:
        arena_at = -(-nc.sbuf_base // 32) * 32
        arena = ctx.enter_context(nc.sbuf_tensor("arena", [P, 52900], F32))
        ps = ctx.enter_context(nc.psum_tensor("ps", [P, 8, 512], F32))
        ptab = ctx.enter_context(nc.sbuf_tensor("ptab", [1, SB * NPAGES], I32))

        def sem(name):
            return ctx.enter_context(nc.semaphore(name))

        at = {}
        top = [0]

        def region(name, cols):
            at[name] = top[0]
            top[0] += cols
            assert top[0] <= 52900, (name, top[0])

        def view(name, cols, off=0):
            return arena[:, at[name] + off:at[name] + off + cols]

        region("xT", KD * TOK)
        region("wring", 2 * KD * W)
        region("scd", SCORES)
        region("lists", 2560)
        region("rbuf", 2048)
        region("wd", 1088)
        region("iqd", 512)
        region("qbd", 512)
        region("qT", PAIRS * TOK)
        region("kT", PAIRS * TOK)
        region("iqT", TILES * W)
        region("ikc", 5120)
        region("score", 4224)
        region("z", 3 * W)
        region("ikT", TOK)
        region("ident", P)
        region("cols", 112)
        region("stats", 512)
        region("causal", 2 * P)
        region("own", SROWS)
        region("iw", TILES * H)
        region("scn", SROWS)
        region("bias31", H)
        region("idx", P)
        region("small", 256)
        region("bias_steps", 8 * H + 1)

        xT = view("xT", KD * TOK).rearrange("p (c t) -> p c t", c=KD)
        wring = view("wring", 2 * KD * W).rearrange("p (s n) -> p s n", s=2)
        qT = view("qT", PAIRS * TOK).rearrange("p (c t) -> p c t", c=PAIRS)
        kT = view("kT", PAIRS * TOK).rearrange("p (c t) -> p c t", c=PAIRS)
        iqT = view("iqT", PAIRS * TOK).rearrange("p (c t) -> p c t", c=PAIRS)
        ikT = view("ikT", TOK)
        u = view("iqT", TILES * W).rearrange("p (t n) -> p t n", t=TILES)
        vn = view("ikc", TILES * W).rearrange("p (t n) -> p t n", t=TILES)
        xring = view("ikc", 3 * D).rearrange("p (s n) -> p s n", s=3)
        ikc = view("ikc", 2048).rearrange("p (s j e d) -> p s j e d", s=2, e=2, d=HD)
        ikcT = view("ikc", 2048, 2048).rearrange("p (s n) -> p s n", s=2)
        zr = view("z", 3 * W).rearrange("p (s n) -> p s n", s=3)
        rb = view("rbuf", 2048).rearrange("p (s n) -> p s n", s=2)
        twice = view("scd", 1024, 512)
        wd = view("wd", 1024).rearrange("p (b n) -> p b n", b=SB)
        iqd = view("iqd", 512).rearrange("p (b n) -> p b n", b=SB)
        qbd = view("qbd", 512).rearrange("p (b c n) -> p b c n", b=SB, c=PAIRS)
        scd = view("scd", SCORES)
        sc_off = {}
        o = 0
        for i in range(2, NT):
            sc_off[i] = o
            o += (i + 1) * P
        ident = view("ident", P)
        near_mask = view("causal", 2 * P)
        causal = view("causal", P, P)
        own = view("own", SROWS)
        cols = view("cols", 112)
        col_at, o = {}, 0
        for name, n in VEC_ROWS:
            col_at[name] = o
            o += n
        g1 = cols[:, col_at["g1"]:col_at["g1"] + KD]
        iw = view("iw", TILES * H).rearrange("p (t h) -> p t h", t=TILES)
        stats = view("stats", 512)
        ssq, rstd = stats[:, 0:9], stats[:, 32:41]
        epsc = stats[:, 48:49]
        m8 = stats[:, 64:72]
        best = stats[:, 300:364]
        bsd = stats[0:SROWS, 80:88]
        vss = stats[:, 96:168].rearrange("p (t h) -> p t h", t=TILES)
        minus_half, one_dth = stats[:, 49:50], stats[:, 50:51]
        bs = cols[:, col_at["bs"]:col_at["bs"] + H]
        rb4 = view("rbuf", 2048).rearrange("p (s n) -> p s n", s=4)
        ws_in = view("rbuf", 1024).rearrange("p (h s) -> p h s", h=H)
        wsT = view("wd", 1024).rearrange("p (h t) -> p h t", h=H)
        wsd = view("iqd", 512).rearrange("p (h t) -> p h t", h=H)
        mixT = view("xT", KD * TOK).rearrange("p (c t) -> p c t", c=KD)
        scn = view("scn", SROWS)
        b31 = view("bias31", H)
        val, pos = view("lists", TOPK), view("lists", TOPK, TOPK)
        val_b, pos_b = view("lists", TOPK, 2 * TOPK), view("lists", TOPK, 3 * TOPK)
        low, page_of, rows_f, turn_f = (view("lists", TOPK, (4 + i) * TOPK) for i in range(4))
        int_a = view("lists", TOPK, 8 * TOPK)
        int_b = view("lists", TOPK, 9 * TOPK)
        idx4 = view("small", 8).bitcast(I32).rearrange("p (s c) -> p s c", s=4)
        sel_new = view("small", ST, 8)
        row_t, row_new = view("small", 1, 16), view("small", 1, 17)
        neg_max = view("small", 2, 18)
        top_col = view("small", 4, 20)
        i8 = view("small", 8, 24).bitcast(U32)
        ptab_f = view("small", NPAGES, 32)
        ptab_i = view("small", NPAGES, 64).bitcast(I32)
        sel_new2 = view("small", ST, 160)
        new_bias = view("small", SROWS, 168)
        idx8 = view("small", 16, 232).bitcast(I32).rearrange("p (s c) -> p s c", s=8)
        new_mask = view("small", SROWS, 96)
        idxT = view("idx", P).bitcast(I32).rearrange("p (c r) -> p c r", c=2)
        distT = view("ikT", P, 4 * P)
        new_maskT = view("ikT", SROWS, 5 * P)
        reach = view("ikT", P, 5 * P + SROWS + BUCKETS * H)
        kv = view("wring", 4 * 2 * W).rearrange("p (s n) -> p s n", s=4)
        qrow = view("wring", 4 * W, 8 * W).rearrange("p (s n) -> p s n", s=4)
        prod = view("wring", 2 * W, 12 * W)
        ones = view("wring", P, 14 * W)
        diag = view("wring", 4 * P, 15 * W)
        lg = view("scd", 2 * W).rearrange("p (c n) -> p c n", c=2)
        ln = view("scd", W, 2 * W)
        mx = view("scd", W, 3 * W)
        pT = view("iqT", NT * SEQ).rearrange("p (k q) -> p k q", k=NT)
        rl = view("iqT", SEQ, NT * SEQ)
        vone = arena[:, at["z"]:at["z"] + 2 * NT * P].rearrange("p (s k n) -> p s k n", s=2, k=NT)
        bn = view("wd", 2 * P * H).rearrange("p (h u) -> p h u", h=H)
        toep_row = view("lists", NEAR)
        hot = view("lists", NEAR, NEAR)
        relb = view("lists", H, 2 * NEAR)
        def free(first, cols):
            return arena[:, first:first + cols]

        def free_rounded(name, first, cols):
            return nc.alloc_sbuf_tensor_at(name, [P, cols], F32R, offset=arena_at + 4 * first)[:, :]

        hx = free(at["qT"], TILES * D).rearrange("p (t n) -> p t n", t=TILES)
        wo = free(at["qT"] + TILES * D, KD * D).rearrange("p (k n) -> p k n", k=KD)
        hn = view("lists", 2 * D).rearrange("p (s n) -> p s n", s=2)
        v_rows = [kv[:, s, :] if s < 4 else free(at["qT"] + TILES * D + (KD + s - 4) * D, D) for s in range(8)]
        own_v, sampled = view("rbuf", W, 2 * W), view("rbuf", W, 3 * W)
        out4 = view("rbuf", 2 * W).rearrange("p (s n) -> p s n", s=2)
        hT = [[free_rounded(f"hT_part{i}_{c}", (i * KD + c) * TOK, TOK) for c in range(KD)] for i in range(2)]
        a_at = 2 * KD * TOK
        gb_at = a_at + NF * TOK
        raw_at = at["qT"] + 2 * KD * TOK
        raw = free(raw_at, 2 * KD * P).rearrange("p (w n) -> p w n", w=2)
        w_parts = [free_rounded(f"ffn_weight_parts{w}", raw_at + (2 + 2 * w) * KD * P, 2 * KD * P).rearrange("p (i n) -> p i n", i=2) for w in range(2)]
        st = free(raw_at + 6 * KD * P, NF * 2 * SB).rearrange("p (f s) -> p f s", f=NF)
        cs = free(raw_at + 6 * KD * P + NF * 2 * SB, NF * (2 + 2 * SB)).rearrange("p (f s) -> p f s", f=NF)
        state_rows = free(raw_at + 4 * D, DFF)
        aT = free(a_at, NF * TOK)
        gb = free(gb_at, 2 + SEQ + SB * (2 + ST))
        gb_p = gb[:, 0:2 + SEQ]
        gb_s = gb[:, 2 + SEQ:].rearrange("p (b t) -> p b t", b=SB)
        y = free(0, TILES * D).rearrange("p (t n) -> p t n", t=TILES)
        d_raw = free(TILES * D, 4 * D).rearrange("p (s n) -> p s n", s=4)
        d_parts = free_rounded("w_down_parts", (TILES + 4) * D, 4 * D).rearrange("p (s i n) -> p s i n", s=2, i=2)
        a_parts = free_rounded("gated_parts", raw_at, 4 * 3 * P).rearrange("p (s i n) -> p s i n", s=2, i=2)
        h_dram = nc.dram_tensor("residual", (TOK, D), F32, kind="Internal").ap()
        g2 = cols[:, col_at["g2"]:col_at["g2"] + KD]
        cw = cols[:, col_at["cw"]:col_at["cw"] + 3 * NF]
        cb = cols[:, col_at["cb"]:col_at["cb"] + NF]
        cs_rows = (free(gb_at, 14 * P), free(raw_at + 4 * 3 * P, 8 * P))
        final_g = free(gb_at, D)
        squares = free(gb_at + D, 512)
        hq, hr, yq, yr = stats[:, 200:209], stats[:, 216:225], stats[:, 232:250], stats[:, 256:265]
        reached = view("iqT", 16 * TOPK)
        step_k, step_j = view("bias_steps", 4 * H), view("bias_steps", 4 * H, 4 * H)
        first_of = view("bias_steps", 1, 8 * H)
        sbias = view("lists", 2 * W).rearrange("p (c n) -> p c n", c=2)
        dist_dram = nc.dram_tensor("slot_distances", (SROWS, TOPK), F32, kind="Internal").ap()
        q_dram = nc.dram_tensor("sampled_queries", (SROWS, W), F32, kind="Internal").ap()
        toep_dram = nc.dram_tensor("bias_by_distance", (H, P, NEAR), F32, kind="Internal").ap()
        o_dram = nc.dram_tensor("sampled_heads", (SROWS, H, H, HD), F32, kind="Internal").ap()
        rows_in = view("rbuf", P)
        wrep = view("scd", P)
        wsel = view("scd", ST, P)
        iwT = view("scd", SROWS, 2 * P)

        s_const = sem("consts_loaded")
        s_pt = sem("page_table_loaded")
        s_x = [sem(f"x_loaded{i}") for i in range(3)]
        s_w = [sem(f"w_loaded{i}") for i in range(2)]
        s_pool = sem("pool_step")
        s_built = sem("masks_built")
        s_ssq = sem("squares_summed")
        s_root = sem("root_mean_square_ready")
        s_dve = sem("dve_step")
        s_xn = sem("x_normed")
        s_xTp = sem("xT_in_psum")
        s_xT = sem("xT_ready")
        s_mm = sem("projection_done")
        s_z = sem("projection_evacuated")
        s_tz = sem("z_transposed")
        s_tev = sem("transposed_evacuated")
        s_zs = [sem(f"z_stored{i}") for i in range(3)]
        s_cps = sem("columns_in_psum")
        s_col = sem("columns_ready")
        s_twice = sem("index_queries_twice")
        s_dot = sem("index_dots_done")
        s_relu = sem("index_relu_done")
        s_sc = sem("index_relu_used")
        s_scm = sem("index_scores_masked")
        s_topk = sem("topk_done")
        s_iwp = sem("index_weights_in_psum")
        s_iwT = sem("index_weights_turned")
        s_wd = sem("head_sum_weights_ready")
        s_ikc = [sem(f"index_pages_loaded{i}") for i in range(2)]
        s_ct = sem("index_pages_turned")
        s_cT = sem("index_pages_evacuated")
        s_cd = sem("page_dots_done")
        s_cr = sem("page_relu_done")
        s_ch = sem("page_heads_summed")
        s_cs = sem("page_scores_evacuated")
        s_ws = sem("w_s_loaded")
        s_wsp = sem("w_s_turned")
        s_wse = sem("w_s_evacuated")
        s_wsc = sem("w_s_causal")
        s_wsd = sem("w_s_blocks_placed")
        s_vss = sem("gate_squares_summed")
        s_vn = sem("gate_normed")
        s_cv = sem("chunk_v_stored")
        s_sg = sem("spatial_gate_done")
        s_sb = sem("spatial_bias_added")
        s_au = sem("chunk_mlp_done")
        s_at = sem("chunk_mlp_turned")
        s_am = sem("chunk_mlp_evacuated")
        s_qbd = sem("query_blocks_ready")
        s_kn = sem("new_key_logits_done")
        s_ln = sem("new_key_logits_evacuated")
        s_rel = sem("bias_table_loaded")
        s_toep = sem("bias_by_distance_done")
        s_toev = sem("bias_by_distance_evacuated")
        s_tod = sem("bias_by_distance_stored")
        s_bn = sem("near_bias_loaded")
        s_b31 = sem("bucket_bias_loaded")
        s_di = sem("distances_stored")
        s_db = sem("distances_spread")
        s_ind = sem("buckets_reached")
        s_sbT = sem("slot_bias_done")
        s_sbe = sem("slot_bias_evacuated")
        s_rows = sem("row_numbers_loaded")
        s_scn = sem("own_scores_moved")
        s_list = sem("lists_ready")
        s_move = sem("second_list_moved")
        s_pick = sem("picked_rows_ready")
        s_pickT = sem("picked_rows_turned")
        s_idx = sem("gather_rows_ready")
        s_nmT = sem("new_mask_turned")
        s_kg = [sem(f"rows_gathered{i}") for i in range(4)]
        s_qr = [sem(f"query_row_loaded{i}") for i in range(4)]
        s_ic = sem("value_rows_numbered")
        s_rs = sem("root_step")
        s_kp = sem("key_products_done")
        s_kd = sem("key_dots_done")
        s_S = sem("prompt_logits_done")
        s_L = sem("prompt_logits_masked")
        s_nbs = sem("own_bias_spread")
        s_nbT = sem("own_bias_turned")
        s_E = sem("prompt_exp_done")
        s_T = sem("prompt_probs_turned")
        s_Te = sem("prompt_probs_evacuated")
        s_vo = [sem(f"head_values_loaded{i}") for i in range(2)]
        s_pv = sem("prompt_heads_done")
        s_po = sem("prompt_heads_normalised")
        s_mxT = sem("sampled_max_turned")
        s_dg = sem("sampled_max_diagonal")
        s_mb = sem("sampled_max_spread")
        s_lm = sem("sampled_logits_shifted")
        s_le = sem("sampled_exp_done")
        s_ls = sem("sampled_sums_ready")
        s_lb = sem("sampled_sums_spread")
        s_pn = sem("sampled_probs_ready")
        s_vd = sem("sampled_heads_done")
        s_ve = sem("sampled_heads_evacuated")
        s_vs = [sem(f"sampled_heads_stored{i}") for i in range(2)]
        s_vnl = sem("new_values_loaded")
        s_nd = sem("new_key_heads_done")
        s_oh = sem("sampled_heads_loaded")
        s_os = sem("sampled_heads_summed")
        s_oT = sem("sampled_heads_turned")
        s_oTe = sem("sampled_heads_placed")

        s_wo = [sem(f"w_o_loaded{i}") for i in range(2)]
        s_x2 = [sem(f"residual_loaded{i}") for i in range(2)]
        s_mo = sem("w_o_products_done")
        s_h = sem("residual_added")
        s_hq = sem("residual_squares_summed")
        s_hn = sem("residual_normed")
        s_hp = sem("residual_turned")
        s_hTr = sem("hT_rounded")
        s_hT = sem("hT_ready")
        s_st = sem("conv_state_loaded")
        s_stp = sem("conv_state_turned")
        s_ste = sem("conv_state_evacuated")
        s_wf = [sem(f"ffn_weights_loaded{i}") for i in range(2)]
        s_hd = sem("residual_stored")
        s_hl = sem("residual_loaded_again")
        s_hi = sem("weights_rounded")
        s_sp = sem("weights_split")
        s_gst = sem("conv_state_placed")
        s_gm = sem("gate_products_done")
        s_gc = sem("gate_evacuated")
        s_um = sem("up_products_done")
        s_cd2 = sem("conv_done")
        s_si = sem("silu_done")
        s_ag = sem("gated")
        s_cst = sem("new_conv_state_turned")
        s_cse = sem("new_conv_state_evacuated")
        s_cso = sem("new_conv_state_stored")
        s_fg = sem("final_gain_loaded")
        s_wdn = s_x + [sem("w_down_loaded3")]
        wdn_base = [16 * TILES // 3] * 3 + [0]
        s_dh = sem("down_rounded")
        s_ds = sem("down_split")
        s_du = sem("w_down_used")
        s_y = sem("output_added")
        s_yq = sem("output_squares_summed")
        s_yn = sem("output_normed")
        s_yo = sem("output_stored")

        n_of = lambda c, t: c * TILES + t
        tjob = [(c, t) for c in range(4) for t in range(TILES)]
        tjob.insert(tjob.index((1, NT)) + 1, ("dup", NT))
        tjob_at = {job: i for i, job in enumerate(tjob)}
        zstores = {}
        for c, t in [(c, t) for c in (0, 2, 3, 4) for t in range(TILES) if c != 2 or t == NT]:
            slot = n_of(c, t) % 3
            zstores[(c, t)] = sum(1 for k in zstores if n_of(*k) % 3 == slot) + 1

        order = [(c, t) for c in range(len(CHUNKS)) for t in range(TILES)]
        between = []
        for un in range(2 * SB):
            between.append(list(range(2 * TILES + 3 * un // 2, 2 * TILES + 3 * (un + 1) // 2)))
        FIRST_BETWEEN, AFTER = between[0][0] if between[0] else between[1][0], between[-1][-1] + 1

        def bank_of(n):
            return 6 if FIRST_BETWEEN <= n < AFTER else 4 + n % 2

        def turned_bank(i):
            return 7 if i > 2 * TILES else 6 + i % 2

        def run_items(items, item, turned, index=None):
            for n in items:
                item(*order[n])
                if n and n != 2 * TILES:
                    turn_last(n - 1, turned)
                if index and n >= TILES:
                    index(n - TILES - 2)

        def turn_last(n, turned):
            if order[n][0] < 4:
                turned(order[n])
            if order[n] == (1, NT):
                turned(("dup", NT))

        def page_numbers(eng, first, n):
            return nc.values_load_multi_w_load_instructions(ptab[0:1, bass.ds(first, n)], engines=(eng.engine,), min_val=0,
                                                            max_val=io["pool"] - 1)[1]

        def own_near(h):
            return view("rbuf", SROWS * H).rearrange("p (h n) -> p h n", h=H)[0:ST, h, :]

        def probs_groups(i):
            return [range(a, min(a + 4, i + 1)) for a in range(0, i + 1, 4)]

        def turned_after(m):
            h, i = divmod(m, NT)
            return h * sum(len(probs_groups(j)) for j in range(NT)) + sum(len(probs_groups(j)) for j in range(i + 1))

        def evacuate_probs(act, h, i, g):
            if h:
                act.wait_ge(s_pv, (h - 1) * (NT // 2) + i // 2 + 1)
            for blocks in probs_groups(i):
                act.wait_ge(s_T, g + 1)
                n, a = len(blocks), blocks[0]
                nc.scalar.activation(pT[:, a:a + n, i * P:(i + 1) * P], ps[:, 4 + g % 2, 0:n * P].rearrange("p (k q) -> p k q", k=n),
                                     ACT.Copy).then_inc(s_Te, 1)
                g += 1
            return g

        def down_blocks(body, eng, after):
            for p in range(PASSES):
                pieces = (3 * p * P, min(3 * P, TOK - 3 * p * P))
                n0 = p * NF
                lead = 4 - n0 % 4 if n0 % 4 else 4
                for f in range(lead):
                    n = n0 + f
                    body(n, f, n % 2, pieces, n < 2, n % 4, 16 * (n // 4 + 1))
                    if p and f == 1:
                        after(p - 1)
                full = (NF - lead - 1) // 4
                with eng.Fori(0, full) as it:
                    for k in range(4):
                        n = n0 + lead + k
                        body(it * 4 + n, it * 4 + (lead + k), n % 2, pieces, False, n % 4, it * 16 + 16 * (n // 4 + 1))
                for f in range(lead + 4 * full, NF):
                    n = n0 + f
                    body(n, f, n % 2, pieces, False, n % 4, 16 * (n // 4 + 1))
            after(PASSES - 1)

        block = ctx.enter_context(nc.Block())

        @block.sync
        def _(sp):
            sp.dma_start(ptab[:, :], io["page_table"].rearrange("(a b) n -> a (b n)", a=1)).then_inc(s_pt, 16)

            def load_x(t):
                if t >= 3:
                    sp.wait_ge(s_xTp, t - 2)
                src = io["x_prompt"][0, t * P:(t + 1) * P, :] if t < NT else io["x_sample"].rearrange("b t d -> (b t) d")
                sp.dma_start(xring[0:rows_of(t), t % 3, :], src).then_inc(s_x[t % 3], 16)

            def load_w(c):
                _, c0, width = CHUNKS[c]
                if c >= 2:
                    sp.wait_ge(s_mm, n_of(c - 1, 0))
                sp.dma_start(wring[:, c % 2, 0:KD * width].rearrange("p (k n) -> p k n", k=KD),
                             io["w_in"][0, :, c0:c0 + width].rearrange("(k p) n -> p k n", p=P)).then_inc(s_w[c % 2], 16)

            load_x(0)
            r = 0
            for name, n in VEC_ROWS:
                src = {"g1": io["norm1_g"], "g2": io["norm2_g"], "cw": io["conv_w"][0], "cb": io["conv_b"], "bs": io["b_s"][0]}[name]
                src = src if name == "bs" else src.rearrange("a (c p) -> (a c) p", p=P)
                sp.dma_start(rows_in[r:r + n, :], src).then_inc(s_const, 16)
                r += n
            sp.dma_start(wrep[0:H, :], io["c_rep"]).then_inc(s_const, 16)
            sp.dma_start(wsel[:, :], io["c_sel"]).then_inc(s_const, 16)
            load_x(1)
            load_x(2)
            for dst, src in ((relb[0:BUCKETS, :], io["rel_bias"]), (hot[0:BUCKETS, :], io["c_hot"])):
                sp.dma_start(dst, src).then_inc(s_rel, 16)
            sp.dma_start(b31, io["rel_bias"][BUCKETS - 1:BUCKETS, :].partition_broadcast(P)).then_inc(s_rows, 16)
            sp.dma_start(view("small", 2, 16)[0:SROWS, :], io["c_rows"]).then_inc(s_rows, 16)
            sp.dma_start(first_of, io["c_first"]).then_inc(s_b31, 16)
            sp.wait_ge(s_built, 4)
            for g in range(4):
                sp.dma_start(step_k[g * BUCKETS:(g + 1) * BUCKETS, g * H:(g + 1) * H], io["rel_bias"]).then_inc(s_b31, 16)
                sp.dma_start(step_j[g * BUCKETS + 1:(g + 1) * BUCKETS, g * H:(g + 1) * H], io["rel_bias"][0:BUCKETS - 1, :]).then_inc(s_b31, 16)
            for b in range(SB):
                sp.dma_start(ptab_i[b * ST:(b + 1) * ST, :], io["page_table"][b:b + 1, :].partition_broadcast(ST)).then_inc(s_rows, 16)
            load_w(0)
            load_w(1)
            for t in range(3, TILES):
                load_x(t)
            load_w(2)
            sp.wait_ge(s_pt, 16)
            sp.wait_ge(s_xTp, TILES)

            def load_index_pages(it, half, first=False):
                for slot in range(2):
                    for e in range(2):
                        for j, page in enumerate(page_numbers(sp, it * (2 * NPAGES) + ((slot - 8 * half) * NPAGES + e * 16 + half * 8), 8)):
                            if not first and (e, j) == (0, 0):
                                sp.wait_ge(s_ct, it * 2 + (slot - 1))
                            sp.dma_start(ikc[:, slot, j, e, :],
                                         io["cache_idx_k"][0, bass.ds(page, 1), :, :].rearrange("a p d -> (a p) d")).then_inc(s_ikc[slot], 16)

            load_index_pages(0, 0, True)
            load_w(3)
            with sp.Fori(1, 4) as it:
                load_index_pages(it, 0)
            with sp.Fori(4, 6) as it:
                load_index_pages(it, 1)
            load_w(4)
            with sp.Fori(6, 8) as it:
                load_index_pages(it, 1)
            sp.wait_ge(s_scm, NT - 1)
            sp.dma_start(scd[SROWS:P, HALF:SCORES], scn[0:SROWS, :]).then_inc(s_scn, 16)
            sp.wait_ge(s_ch, 4 * SB)
            sp.dma_start(ws_in, io["w_s"][0].rearrange("h t s -> t h s")).then_inc(s_ws, 16)
            for c in range(5, 7):
                load_w(c)
            sp.wait_ge(s_wsc, 1)
            for b in range(SB):
                r = slice(b * ST, (b + 1) * ST)
                sp.dma_start(wsd[r, :, r], wsT[0:ST, :, 0:ST]).then_inc(s_wsd, 16)
                sp.dma_start(bsd[r, :], bs[0:ST, :]).then_inc(s_wsd, 16)

            sp.wait_ge(s_toev, 1)
            sp.dma_start(toep_dram, toep_row[0:H, :].unsqueeze(1).to_broadcast([H, P, NEAR])).then_inc(s_tod, 16)
            sp.wait_ge(s_tod, 16)
            sp.wait_ge(s_ln, 1)
            sp.dma_start(bn, bass.AP(tensor=toep_dram.tensor, offset=P - 1, ap=[[NEAR - 1, P], [P * NEAR, H], [1, 2 * P]])).then_inc(s_bn, 16)

            sp.wait_ge(s_list, 1)
            sp.dma_start(val_b[0:SROWS, :], val[SROWS:P, :]).then_inc(s_move, 16)
            sp.dma_start(pos_b[0:SROWS, :], pos[SROWS:P, :]).then_inc(s_move, 16)

            sp.wait_ge(s_pick, 1)
            sp.dma_start(dist_dram, turn_f[0:SROWS, :]).then_inc(s_di, 16)
            sp.wait_ge(s_di, 16)
            sp.wait_ge(s_am, TILES)
            for g in range(4):
                sp.dma_start(reached[g * BUCKETS:(g + 1) * BUCKETS, :],
                             dist_dram[g * (SROWS // 4):(g + 1) * (SROWS // 4), :].rearrange("(a r) n -> a (r n)", a=1)
                             .partition_broadcast(BUCKETS)).then_inc(s_db, 16)

            def load_head(h):
                if h >= 2:
                    sp.wait_ge(s_pv, (h - 1) * (NT // 2))
                sp.dma_start(vone[:, h % 2, :, 0:HD],
                             io["v_p"][0, 0, :, h, :].rearrange("(k p) d -> p k d", p=P)).then_inc(s_vo[h % 2], 16)

            for s in range(3):
                sp.wait_ge(s_zs[s], 16 * sum(1 for k in zstores if n_of(*k) % 3 == s))
            load_head(0)
            load_head(1)
            for h in range(H):
                for r in range(h * 8, h * 8 + 8):
                    if r >= 4:
                        sp.wait_ge(s_kd, r - 3)
                    sp.dma_start(qrow[:, r % 4, :], q_dram[r:r + 1, :].partition_broadcast(P)).then_inc(s_qr[r % 4], 16)
                    if r % 8 == 3 and 0 < h < H - 1:
                        load_head(h + 1)
            sp.wait_ge(s_po, H)
            sp.dma_start(own_v[0:SROWS, :], io["v_s"][0].rearrange("b t h d -> (b t) (h d)")).then_inc(s_vnl, 16)
            sp.wait_ge(s_po, H)
            for half in range(2):
                sp.dma_start(wo[:, :, half * 512:(half + 1) * 512],
                             io["w_o"][0, :, half * 512:(half + 1) * 512].rearrange("(k p) n -> p k n", p=P)).then_inc(s_wo[half], 16)
            sp.dma_start(hx[:, 0:NT, :], io["x_prompt"][0].rearrange("(t p) n -> p t n", p=P)).then_inc(s_x2[0], 16)
            sp.dma_start(hx[0:SROWS, NT, :], io["x_sample"].rearrange("b t d -> (b t) d")).then_inc(s_x2[1], 16)
            sp.dma_start(state_rows[0:2 * SB, :], io["state_ffn_conv"][0].rearrange("b j f -> (b j) f")).then_inc(s_st, 16)

            def store_residual(t):
                sp.wait_ge(s_h, t + 1)
                sp.dma_start(h_dram[t * P:t * P + rows_of(t), :], hx[0:rows_of(t), t, :]).then_inc(s_hd, 16)
                sp.wait_ge(s_hd, 16 * (t + 1))

            for t in range(NT):
                store_residual(t)
            for s in range(2):
                sp.wait_ge(s_vs[s], 16 * SROWS // 2)
            sp.dma_start(sampled[0:SROWS, :].rearrange("p (h d) -> p h d", h=H),
                         bass.AP(tensor=o_dram.tensor, offset=0, ap=[[H * W, SROWS], [W + HD, H], [1, HD]])).then_inc(s_oh, 16)

            def load_ffn(f, w):
                sp.dma_start(raw[:, w].rearrange("p (k n) -> p k n", k=KD),
                             io[("w_gate", "w_up")[w]][0, :, bass.ds(f * P, P)].rearrange("(k p) n -> p k n", p=P)).then_inc(s_wf[w], 16)

            load_ffn(0, 0)
            load_ffn(0, 1)
            store_residual(NT)
            with sp.Fori(1, NF) as f:
                for w in range(2):
                    sp.wait_ge(s_sp, f * 2 + (w - 1))
                    load_ffn(f, w)

            def load_down(f, slot):
                sp.dma_start(d_raw[:, slot, :], io["w_down"][0, bass.ds(f * P, P), :]).then_inc(s_wdn[slot], 16)

            sp.wait_ge(s_um, 3 * NF)
            for f in range(4):
                load_down(f, f)
            sp.dma_start(y[:, 0:NT, :], h_dram[0:SEQ, :].rearrange("(t p) n -> p t n", p=P)).then_inc(s_hl, 16)
            sp.dma_start(y[0:SROWS, NT, :], h_dram[SEQ:TOK, :]).then_inc(s_hl, 16)

            def load_downs(n, f, slots):
                for k, slot in enumerate(slots):
                    sp.wait_ge(s_ds, n + (k - 3))
                    load_down(f + k, slot)

            with sp.Fori(1, 5) as it:
                load_downs(it * 4, it * 4, range(4))
            load_downs(20, 20, (0, 1))
            sp.wait_ge(s_cse, 2)
            for (first, n), rows in zip(((0, 14), (14, 8)), cs_rows):
                c = slice(first * P, (first + n) * P)
                sp.dma_start(io["conv_p"][0, 0, :, c], rows[0:2, :]).then_inc(s_cso, 16)
                sp.dma_start(io["conv_s"][0].rearrange("b j f -> (b j) f")[:, c], rows[2:2 + 2 * SB, :]).then_inc(s_cso, 16)
            sp.wait_ge(s_cso, 64)
            sp.dma_start(final_g, io["final_g"].rearrange("(a n) -> a n", a=1).partition_broadcast(P)).then_inc(s_fg, 16)

            def store_outputs(p):
                for t in range(3 * p, 3 * p + 3):
                    sp.wait_ge(s_yn, t + 1)
                    dst = io["y_p"][0, t * P:(t + 1) * P, :] if t < NT else io["y_s"].rearrange("b t d -> (b t) d")
                    sp.dma_start(dst, y[0:rows_of(t), t, :]).then_inc(s_yo, 16)

            load_downs(NF, 0, (2, 3))
            with sp.Fori(0, 5) as it:
                load_downs(it * 4 + (NF + 2), it * 4 + 2, range(4))
            store_outputs(0)
            with sp.Fori(0, 5) as it:
                load_downs(it * 4 + 2 * NF, it * 4, range(4))
            load_downs(2 * NF + 20, 20, (0, 1))
            store_outputs(1)
            store_outputs(2)
            sp.wait_ge(s_yo, 16 * TILES)

        @block.gpsimd
        def _(pool):
            step = [0]

            def link(ins):
                step[0] += 1
                ins.then_inc(s_pool, 1)
                pool.wait_ge(s_pool, step[0])

            link(nc.gpsimd.memset(ident, 0.0))
            link(nc.gpsimd.affine_select(out=ident, in_=ident, compare_op=ALU.not_equal, fill=1.0, base=0,
                                         pattern=[[-1, P]], channel_multiplier=1))
            nc.gpsimd.memset(minus_half, -0.5)
            nc.gpsimd.memset(one_dth, 1.0 / D)
            nc.gpsimd.memset(epsc, EPS).then_inc(s_built, 1)

            def root(squares, out, t):
                r = rows_of(t)
                link(nc.gpsimd.tensor_scalar(out[0:r, t:t + 1], squares[0:r, t:t + 1], 1.0 / D, EPS, ALU.mult, ALU.add))
                link(nc.gpsimd.tensor_tensor(out[0:r, t:t + 1], out[0:r, t:t + 1], minus_half[0:r, :], ALU.pow))
                nc.gpsimd.drain().then_inc(s_root, 1)

            link(nc.gpsimd.memset(near_mask, 0.0))
            nc.gpsimd.affine_select(out=causal, in_=causal, compare_op=ALU.is_ge, fill=NEG, base=0,
                                    pattern=[[-1, P]], channel_multiplier=1).then_inc(s_built, 1)
            link(nc.gpsimd.memset(own[0:SROWS, :], 0.0))
            for base, pattern, mult in ((0, [[-8, SB], [-1, ST]], 1), (0, [[-8, SB], [0, ST]], 1), (7, [[8, SB], [0, ST]], -1)):
                o3 = own[0:SROWS, :].rearrange("p (b t) -> p b t", b=SB)
                link(nc.gpsimd.affine_select(out=o3, in_=o3, compare_op=ALU.is_ge, fill=NEG, base=base,
                                             pattern=pattern, channel_multiplier=mult))
            nc.gpsimd.memset(stats[:, 500:501], 0.0).then_inc(s_built, 1)

            link(nc.gpsimd.memset(view("bias_steps", 8 * H), 0.0))
            link(nc.gpsimd.memset(wd, 0.0))
            nc.gpsimd.memset(scd[0:SROWS, HALF:SCORES], NEG).then_inc(s_built, 1)
            link(nc.gpsimd.memset(qbd, 0.0))
            for t in range(TILES):
                pool.wait_ge(s_ssq, t + 1)
                root(ssq, rstd, t)

            for c, t in zstores:
                name, r = CHUNKS[c][0], rows_of(t)
                z = zr[0:r, n_of(c, t) % 3, 0:(HD if name == "small" else W)]
                pool.wait_ge(s_z, n_of(c, t) + 1)
                if name == "q":
                    pool.dma_start(q_dram, z).then_inc(s_zs[n_of(c, t) % 3], 16)
                    continue
                out = {"small": ("idx_k_p", "idx_k_s"), "k": ("k_p", "k_s"), "v": ("v_p", "v_s")}[name]
                if t < NT:
                    dst = io[out[0]][0, 0, t * P:(t + 1) * P]
                    dst = dst if name == "small" else dst.rearrange("t h d -> t (h d)")
                else:
                    dst = io[out[1]][0].rearrange("b t d -> (b t) d" if name == "small" else "b t h d -> (b t) (h d)")
                pool.dma_start(dst, z).then_inc(s_zs[n_of(c, t) % 3], 16)
                if (c, t) == (3, 0):
                    pool.wait_ge(s_tev, tjob_at[(2, NT)] + 1)
                    for j in range(2):
                        r = slice(j * HD, (j + 1) * HD)
                        nc.gpsimd.tensor_copy(qbd[r, :, :, j * ST:(j + 1) * ST],
                                              qT[r, :, SEQ:TOK].rearrange("p c (b q) -> p b c q", b=SB)).then_inc(s_qbd, 1)
                        pool.wait_ge(s_qbd, j + 1)
                if (c, t) == (4, NT - 1):
                    pool.wait_ge(s_wse, 1)
                    link(nc.gpsimd.affine_select(out=wsT, in_=wsT, compare_op=ALU.is_ge, fill=0.0, base=0,
                                                 pattern=[[0, H], [1, P]], channel_multiplier=-1))
                    nc.gpsimd.memset(wsd, 0.0).then_inc(s_wsc, 1)
            for t in range(TILES):
                r = rows_of(t)
                pool.wait_ge(s_z, n_of(6, t) + 1)
                sq = rb4[0:r, 3, :]
                link(nc.gpsimd.tensor_tensor(sq, vn[0:r, t, :], vn[0:r, t, :], ALU.mult))
                sq = sq.rearrange("p (h d) -> p h d", h=H)
                half = HD // 2
                while half > 1:
                    link(nc.gpsimd.tensor_tensor(sq[:, :, 0:half], sq[:, :, 0:half], sq[:, :, half:2 * half], ALU.add))
                    half //= 2
                nc.gpsimd.tensor_tensor(vss[0:r, t, :], sq[:, :, 0], sq[:, :, 1], ALU.add).then_inc(s_vss, 1)
                pool.wait_ge(s_vss, t + 1)
                link(nc.gpsimd.tensor_scalar(vss[0:r, t, :], vss[0:r, t, :], 1.0 / HD, EPS, ALU.mult, ALU.add))
                link(nc.gpsimd.tensor_tensor(vss[0:r, t, :], vss[0:r, t, :], minus_half[0:r, :].to_broadcast([r, H]), ALU.pow))
                v = vn[0:r, t, :].rearrange("p (h d) -> p h d", h=H)
                nc.gpsimd.tensor_tensor(v, v, vss[0:r, t, :].unsqueeze(2).to_broadcast([r, H, HD]), ALU.mult).then_inc(s_vn, 1)
                pool.wait_ge(s_vn, t + 1)
            pool.wait_ge(s_vn, TILES)
            pool.dma_start(io["chunk_v_s"][0].rearrange("b t h d -> (b t) (h d)"), vn[0:SROWS, NT, :]).then_inc(s_cv, 16)
            for h in range(H):
                c = slice(h * HD, (h + 1) * HD)
                pool.wait_ge(s_sb, h + 1)
                link(nc.gpsimd.tensor_tensor(u[:, 0:NT, c], u[:, 0:NT, c], rb4[:, h % 2, :].rearrange("p (t d) -> p t d", t=NT), ALU.mult))
                nc.gpsimd.tensor_tensor(u[0:SROWS, NT, c], u[0:SROWS, NT, c], rb4[0:SROWS, 2, (h % 2) * HD:(h % 2 + 1) * HD],
                                        ALU.mult).then_inc(s_au, 1)
                pool.wait_ge(s_au, h + 1)
            pool.wait_ge(s_cv, 16)
            for s in range(3):
                pool.wait_ge(s_zs[s], 16 * sum(1 for k in zstores if n_of(*k) % 3 == s))
            for s in range(2):
                link(nc.gpsimd.memset(vone[:, s, :, HD:P], 1.0))
            nc.gpsimd.memset(ones, 1.0).then_inc(s_built, 1)

            def gather(cache, done, used):
                def body(it, first):
                    for s in range(4):
                        if not first:
                            pool.wait_ge(used, it * 4 + (s - 3))
                        nc.gpsimd.tensor_copy(idx4[:, s, :], idxT[:, :, bass.ds(it * 4 + s, 1)].rearrange("p c a -> p (c a)"))
                        nc.gpsimd.drain()
                        for c in range(2):
                            pool.indirect_dma_start(out=kv[:, s, c * W:(c + 1) * W], out_offset=None,
                                                    in_=cache[0].rearrange("n p h d -> (n p) (h d)"),
                                                    in_offset=bass.IndirectOffsetOnAxis(ap=idx4[:, s, c:c + 1], axis=0)).then_inc(done[s], 16)

                body(0, True)
                with pool.Fori(1, SROWS // 4) as it:
                    body(it, False)

            pool.wait_ge(s_idx, 1)
            pool.wait_ge(s_mm, 7 * TILES)
            gather(io["cache_k"], s_kg, s_kd)
            pool.wait_ge(s_kd, SROWS)

            def gather_values(g, odd):
                for j in range(4):
                    nc.gpsimd.tensor_copy(idx8[:, 4 * odd + j, :], idxT[:, :, bass.ds(g * 4 + j, 1)].rearrange("p c a -> p (c a)")).then_inc(s_ic, 1)
                pool.wait_ge(s_ic, g * 4 + 4)
                for j in range(4):
                    for c in range(2):
                        pool.indirect_dma_start(out=v_rows[4 * odd + j][:, c * W:(c + 1) * W], out_offset=None,
                                                in_=io["cache_v"][0].rearrange("n p h d -> (n p) (h d)"),
                                                in_offset=bass.IndirectOffsetOnAxis(ap=idx8[:, 4 * odd + j, c:c + 1], axis=0)).then_inc(s_kg[odd], 16)

            def residual_root(t):
                pool.wait_ge(s_hq, t + 1)
                nc.gpsimd.tensor_tensor(hr[:, bass.ds(t, 1)], hq[:, bass.ds(t, 1)], one_dth, ALU.mult).then_inc(s_rs, 1)
                pool.wait_ge(s_rs, t * 2 + 1)
                nc.gpsimd.tensor_tensor(hr[:, bass.ds(t, 1)], hr[:, bass.ds(t, 1)], epsc, ALU.add).then_inc(s_rs, 1)
                pool.wait_ge(s_rs, t * 2 + 2)
                nc.gpsimd.tensor_tensor(hr[:, bass.ds(t, 1)], hr[:, bass.ds(t, 1)], minus_half, ALU.pow).then_inc(s_root, 1)

            gather_values(0, 0)
            pool.wait_ge(s_po, H)
            gather_values(1, 1)
            for it in range(1, NT):
                for odd in range(2):
                    pool.wait_ge(s_vd, it * 2 + (odd - 1))
                    gather_values(it * 2 + odd, odd)
                residual_root(it - 1)
            residual_root(NT - 1)
            pool.wait_ge(s_hq, TILES)
            root(hq, hr, NT)

            pool.wait_ge(s_ste, 1)
            pool.wait_ge(s_oTe, 1)
            link(nc.gpsimd.memset(gb_p[:, 0:2], 0.0))
            nc.gpsimd.tensor_copy(gb_s[:, :, 0:2], st[:, 0, :].rearrange("p (b j) -> p b j", b=SB)).then_inc(s_gst, 1)

            def keep_state(f):
                nc.gpsimd.tensor_copy(cs[:, bass.ds(f, 1), 0:2].rearrange("p a s -> p (a s)"), gb_p[:, SEQ:])
                nc.gpsimd.drain()
                nc.gpsimd.tensor_copy(cs[:, bass.ds(f, 1), 2:].rearrange("p a (b j) -> p (a b) j", b=SB), gb_s[:, :, ST:])
                nc.gpsimd.drain()

            with pool.Fori(0, NF - 1) as f:
                pool.wait_ge(s_cd2, f + 1)
                keep_state(f)
                nc.gpsimd.tensor_copy(gb_s[:, :, 0:2], st[:, bass.ds(f + 1, 1), :].rearrange("p a (b j) -> p (a b) j", b=SB)).then_inc(s_gst, 1)
                pool.wait_ge(s_gst, f + 2)
            pool.wait_ge(s_cd2, NF)
            keep_state(NF - 1)
            nc.gpsimd.drain().then_inc(s_gst, 1)
            for t in range(TILES):
                r = rows_of(t)
                pool.wait_ge(s_yq, 2 * t + 2)
                link(nc.gpsimd.tensor_tensor(yq[0:r, t:t + 1], yq[0:r, t:t + 1], yq[0:r, TILES + t:TILES + t + 1], ALU.add))
                root(yq, yr, t)

        @block.scalar
        def _(act):
            act.wait_ge(s_built, 1)
            for t in range(TILES):
                r = rows_of(t)
                act.wait_ge(s_x[t % 3], 16 * (t // 3 + 1))
                if t:
                    act.wait_ge(s_ssq, t)
                nc.scalar.activation(rb[0:r, 1, :], xring[0:r, t % 3, :], ACT.Square, accum_out=ssq[0:r, t:t + 1]).then_inc(s_ssq, 1)

            def evacuate(c, t):
                name, n, r = CHUNKS[c][0], n_of(c, t), rows_of(t)
                act.wait_ge(s_mm, n + 1)
                src = ps[0:r, bank_of(n), :]
                slot = n % 3
                if c < 5 and n >= 3:
                    pc, pt = divmod(n - 3, TILES)
                    if pc < 4:
                        act.wait_ge(s_tz, tjob_at[("dup", NT) if (pc, pt) == (1, NT) else (pc, pt)] + 1)
                    if (pc, pt) in zstores:
                        act.wait_ge(s_zs[slot], 16 * zstores[(pc, pt)])
                if name == "small":
                    nc.scalar.activation(iw[0:r, t, :], src[:, 0:H], ACT.Copy, scale=H ** -0.5)
                    nc.scalar.activation(zr[0:r, slot, 0:HD], src[:, H:H + HD], ACT.Copy)
                    nc.scalar.activation(zr[0:r, slot, HD:2 * HD], src[:, H:H + HD], ACT.Copy).then_inc(s_z, 1)
                elif c < 5:
                    nc.scalar.activation(zr[0:r, slot, :], src, ACT.Copy).then_inc(s_z, 1)
                    if (c, t) == (1, NT):
                        act.wait_ge(s_z, n + 1)
                        nc.scalar.activation(twice[0:r, :].rearrange("p (h e d) -> p h e d", h=H, e=2),
                                             zr[0:r, slot, :].rearrange("p (h d) -> p h d", h=H).unsqueeze(2).to_broadcast([r, H, 2, HD]),
                                             ACT.Copy).then_inc(s_twice, 1)
                elif name == "ua":
                    nc.scalar.activation(u[0:r, t, :], src, ACT.Gelu_apprx_tanh).then_inc(s_z, 1)
                else:
                    nc.scalar.activation(vn[0:r, t, :], src, ACT.Gelu_apprx_tanh).then_inc(s_z, 1)

            def evacuate_t(job):
                c, t = job
                i = tjob_at[job]
                r = rows_of(t)
                tok = slice(t * P, t * P + r)
                act.wait_ge(s_tz, i + 1)
                src = ps[:, turned_bank(i), :]
                if c == "dup":
                    out = iqd.rearrange("p b (h q) -> p b h q", h=H)
                    nc.scalar.activation(out, src.rearrange("p (h b q) -> p b h q", h=H, b=SB), ACT.Copy,
                                         scale=HD ** -0.5).then_inc(s_tev, 1)
                elif c == 0:
                    nc.scalar.activation(ikT[:, tok], src[:, 0:r], ACT.Copy).then_inc(s_tev, 1)
                else:
                    dst = {1: iqT, 2: qT, 3: kT}[c]
                    nc.scalar.activation(dst[:, :, tok], src.rearrange("p (c t) -> p c t", c=PAIRS)[:, :, 0:r], ACT.Copy,
                                         scale=1.0 if c == 3 else HD ** -0.5).then_inc(s_tev, 1)

            def index_relus(i):
                if i < 2:
                    return
                n, r = ((i + 1) * P, P) if i < NT else (SROWS, SROWS)
                for m in range((i - 2) * H, (i - 1) * H):
                    act.wait_ge(s_dot, m + 1)
                    if m >= 2:
                        act.wait_ge(s_sc, m - 1)
                    src = ps[0:r, 2 * (m % 2):2 * (m % 2) + 2, :].rearrange("p a n -> p (a n)")[:, 0:n]
                    nc.scalar.activation(rb[0:r, m % 2, 0:n], src, ACT.Relu).then_inc(s_relu, 1)

            run_items(range(2 * TILES), evacuate, evacuate_t, index_relus)
            turn_last(2 * TILES - 1, evacuate_t)
            index_relus(NT - 1)
            index_relus(NT)
            m = (NT - 1) * H
            act.wait_ge(s_sc, m)

            def evacuate_index_pages(un):
                act.wait_ge(s_ct, un + 1)
                if un >= 2:
                    act.wait_ge(s_cd, 2 * (un - 1))
                nc.scalar.activation(ikcT[:, un % 2, :], ps[:, 0:2, :].rearrange("p a n -> p (a n)"), ACT.Copy).then_inc(s_cT, 1)

            evacuate_index_pages(0)
            for un in range(2 * SB):
                if un + 1 < 2 * SB:
                    evacuate_index_pages(un + 1)
                for r2 in range(2):
                    act.wait_ge(s_cd, 2 * un + r2 + 1)
                    if un:
                        act.wait_ge(s_ch, 2 * (un - 1) + r2 + 1)
                    nc.scalar.activation(rb4[:, r2, :], ps[:, 2 + r2, :], ACT.Relu).then_inc(s_cr, 1)
                if un % SB == SB - 1:
                    half = un // SB
                    act.wait_ge(s_ch, 2 * un + 2)
                    nc.scalar.activation(scd[:, half * D:(half + 1) * D], ps[:, 4:6, :].rearrange("p a n -> p (a n)"), ACT.Copy).then_inc(s_cs, 1)
                run_items(between[un], evacuate, evacuate_t)
            act.wait_ge(s_wsp, 1)
            nc.scalar.activation(wsT.rearrange("p h t -> p (h t)"), ps[:, 0:2, :].rearrange("p a n -> p (a n)"), ACT.Copy).then_inc(s_wse, 1)
            run_items(range(AFTER, len(order)), evacuate, evacuate_t)

            act.wait_ge(s_wsd, 16 * 2 * SB)
            for h in range(H):
                act.wait_ge(s_sg, h + 1)
                if h >= 2:
                    act.wait_ge(s_au, h - 1)
                nc.scalar.activation(rb4[:, h % 2, :], ps[:, h % 2, :], ACT.Identity, bias=bs[:, h:h + 1])
                nc.scalar.activation(rb4[0:SROWS, 2, (h % 2) * HD:(h % 2 + 1) * HD], ps[0:SROWS, 2 + h % 2, 0:HD], ACT.Identity,
                                     bias=bsd[:, h:h + 1]).then_inc(s_sb, 1)
            for t in range(TILES):
                r = rows_of(t)
                act.wait_ge(s_at, t + 1)
                nc.scalar.activation(mixT[:, 0:PAIRS, t * P:t * P + r],
                                     ps[:, 6 + t % 2, :].rearrange("p (c t) -> p c t", c=PAIRS)[:, :, 0:r], ACT.Copy).then_inc(s_am, 1)
            act.wait_ge(s_kn, 1)
            act.wait_ge(s_list, 1)
            nc.scalar.activation(ln[0:SROWS, :].rearrange("p (b q h) -> p b h q", b=SB, q=ST),
                                 ps[0:SROWS, 5, :].rearrange("p (b h q) -> p b h q", b=SB, h=H), ACT.Copy).then_inc(s_ln, 1)

            m = g = 0
            for h in range(H):
                for i in range(NT):
                    act.wait_ge(s_L, m + 1)
                    l = rb[:, m % 2, 0:(i + 1) * P]
                    nc.scalar.activation(l, l, ACT.Exp, scale=-1.0, bias=neg_max[:, m % 2:m % 2 + 1]).then_inc(s_E, 1)
                    m += 1
                    if i:
                        g = evacuate_probs(act, h, i - 1, g)
                g = evacuate_probs(act, h, NT - 1, g)

            nc.scalar.activation(view("rbuf", SROWS * H).rearrange("p (h b t) -> p h b t", h=H, b=SB)[0:ST],
                                 bn[0:ST, :, P:P + ST].unsqueeze(2).to_broadcast([ST, H, SB, ST]), ACT.Copy).then_inc(s_nbs, 1)

            act.wait_ge(s_lm, 3)
            nc.scalar.activation(lg, lg, ACT.Exp)
            nc.scalar.activation(ln[0:SROWS, :], ln[0:SROWS, :], ACT.Exp).then_inc(s_le, 1)
            def residual_squares(t):
                r = rows_of(t)
                act.wait_ge(s_h, t + 1)
                if t:
                    act.wait_ge(s_hq, t)
                nc.scalar.activation(hn[0:r, 0, :], hx[0:r, t, :], ACT.Square, accum_out=hq[0:r, t:t + 1]).then_inc(s_hq, 1)

            for g in range(SROWS // 4):
                act.wait_ge(s_vd, g + 1)
                if g >= 2:
                    act.wait_ge(s_vs[g % 2], 64 * (g // 2))
                nc.scalar.activation(out4[:, g % 2, :], ps[:, 2 * (g % 2), :], ACT.Copy).then_inc(s_ve, 1)
                act.wait_ge(s_ve, g + 1)
                for j in range(4):
                    act.dma_start(o_dram[4 * g + j].rearrange("g h d -> g (h d)"), out4[32 * j:32 * j + H, g % 2, :]).then_inc(s_vs[g % 2], 16)
                if g % 2:
                    residual_squares(g // 2)

            def round_hT(t):
                r = rows_of(t)
                act.wait_ge(s_hp, t + 1)
                for c in range(KD):
                    ins = nc.scalar.activation(hT[0][c][:, t * P:t * P + r], ps[:, 4 + 2 * (t % 2) + c // 4, (c % 4) * P:(c % 4) * P + r],
                                               ACT.Copy, scale=g2[:, c:c + 1])
                ins.then_inc(s_hTr, 1)

            for t in range(NT):
                if t == NT - 2:
                    residual_squares(NT)
                round_hT(t)
            round_hT(NT)

            def round_weights(f, w, first=False):
                act.wait_ge(s_wf[w], f * 16 + 16)
                if not first:
                    act.wait_ge((s_gm, s_um)[w], f * 3)
                nc.scalar.activation(w_parts[w][:, 0, :], raw[:, w, :], ACT.Copy).then_inc(s_hi, 1)

            act.wait_ge(s_ste, 1)
            round_weights(0, 0, True)
            round_weights(0, 1, True)

            def gate(f, last):
                act.wait_ge(s_gst, f + 1)
                for g, (a, e) in enumerate(GROUPS):
                    act.wait_ge(s_gm, f * 3 + (g + 1))
                    if e <= SEQ:
                        nc.scalar.activation(gb_p[:, 2 + a:2 + e], ps[:, g, 0:e - a], ACT.Copy).then_inc(s_gc, 1)
                    else:
                        nc.scalar.activation(gb_p[:, 2 + a:2 + SEQ], ps[:, g, 0:SEQ - a], ACT.Copy)
                        nc.scalar.activation(gb_s[:, :, 2:], ps[:, g, SEQ - a:e - a].rearrange("p (b t) -> p b t", b=SB), ACT.Copy).then_inc(s_gc, 1)
                if not last:
                    round_weights(f + 1, 0)
                act.wait_ge(s_cd2, f + 1)
                a = aT[:, bass.ds(f * TOK, TOK)]
                nc.scalar.activation(a, a, ACT.Silu).then_inc(s_si, 1)
                if not last:
                    round_weights(f + 1, 1)

            with act.Fori(0, NF - 1) as f:
                gate(f, False)
            gate(NF - 1, True)
            for half, blocks in enumerate(cs_rows):
                n = 2 + 2 * SB
                act.wait_ge(s_cst, 1)
                src = ps[0:n, 0:4, :] if half == 0 else ps[0:n, 4:6, :]
                nc.scalar.activation(blocks[0:n, :], src.rearrange("p a n -> p (a n)")[:, 0:(14, 8)[half] * P], ACT.Copy).then_inc(s_cse, 1)

            def round_down(n, f, s, pieces, first=False, raw_slot=None, loads=0):
                act.wait_ge(s_wdn[raw_slot], loads + wdn_base[raw_slot])
                if not first:
                    act.wait_ge(s_du, n - 1)
                nc.scalar.activation(d_parts[:, s, 0, :], d_raw[:, raw_slot, :], ACT.Copy)
                a, w = pieces
                nc.scalar.activation(a_parts[:, s, 0, 0:w], aT[:, bass.ds(f * TOK + a, w)], ACT.Copy).then_inc(s_dh, 1)

            def output_squares(p):
                for t in range(3 * p, 3 * p + 3):
                    r = rows_of(t)
                    for half in range(2):
                        act.wait_ge(s_y, 2 * t + half + 1)
                        if t or half:
                            act.wait_ge(s_yq, 2 * t + half)
                        nc.scalar.activation(squares[0:r, :], y[0:r, t, half * 512:(half + 1) * 512], ACT.Square,
                                             accum_out=yq[0:r, half * TILES + t:half * TILES + t + 1]).then_inc(s_yq, 1)

            down_blocks(round_down, act, output_squares)

        @block.vector
        def _(dve):
            step = [0]

            def link(ins):
                step[0] += 1
                ins.then_inc(s_dve, 1)
                dve.wait_ge(s_dve, step[0])

            dve.wait_ge(s_cps, 1)
            nc.vector.tensor_copy(cols, ps[:, 4, 0:112]).then_inc(s_col, 1)
            dve.wait_ge(s_col, 1)

            def scale(t):
                r = rows_of(t)
                dve.wait_ge(s_root, t + 1)
                nc.vector.tensor_scalar(xring[0:r, t % 3, :], xring[0:r, t % 3, :], rstd[0:r, t:t + 1], None, ALU.mult).then_inc(s_xn, 1)

            def gain(t):
                r = rows_of(t)
                dve.wait_ge(s_xTp, t + 1)
                src = ps[:, 2 * (t % 2):2 * (t % 2) + 2, :].rearrange("p a (c t) -> p (a c) t", c=4)[:, :, 0:r]
                nc.vector.tensor_tensor(xT[:, :, t * P:t * P + r], src, g1.unsqueeze(2).to_broadcast([P, KD, r]), ALU.mult).then_inc(s_xT, 1)

            for t in range(TILES):
                scale(t)
                if t:
                    gain(t - 1)
            gain(TILES - 1)
            dve.wait_ge(s_iwp, 1)
            nc.vector.tensor_copy(iwT[0:H, :], ps[0:H, 2, 0:SROWS]).then_inc(s_iwT, 1)
            dve.wait_ge(s_iwp, 2)
            dve.wait_ge(s_built, 4)
            for b in range(SB):
                for e in range(2):
                    r = slice(e * SROWS, (e + 1) * SROWS)
                    c = e * SROWS + b * ST
                    ins = nc.vector.tensor_tensor(wd[r, b, c:c + ST], ps[r, 2, SROWS + b * ST:SROWS + (b + 1) * ST], wsel[r, :], ALU.mult)
            ins.then_inc(s_wd, 1)
            dve.wait_ge(s_toep, 1)
            link(nc.vector.tensor_copy(toep_row[0:H, :], ps[0:H, 3, 0:NEAR]))
            nc.vector.tensor_scalar(toep_row[0:H, :], toep_row[0:H, :], toep_row[0:H, 0:1], None, ALU.subtract).then_inc(s_toev, 1)

            def index_scores(i):
                n, r = ((i + 1) * P, P) if i < NT else (SROWS, SROWS)
                sc = view("score", n, sc_off[i]) if i < NT else scn[0:r, :]
                for h in range(H):
                    m = (i - 2) * H + h
                    dve.wait_ge(s_relu, m + 1)
                    w = iw[0:r, i, h:h + 1]
                    if h == 0:
                        ins = nc.vector.tensor_scalar(sc, rb[0:r, m % 2, 0:n], w, None, ALU.mult)
                    else:
                        ins = nc.vector.scalar_tensor_tensor(out=sc, in0=rb[0:r, m % 2, 0:n], scalar=w, in1=sc, op0=ALU.mult, op1=ALU.add)
                    ins.then_inc(s_sc, 1)
                    dve.wait_ge(s_sc, m + 1)
                dve.wait_ge(s_built, 3)
                if i < NT:
                    nc.vector.tensor_tensor(sc[:, i * P:n], sc[:, i * P:n], causal, ALU.add).then_inc(s_scm, 1)
                else:
                    nc.vector.tensor_tensor(sc, sc, own[0:r, :], ALU.add).then_inc(s_scm, 1)
                dve.wait_ge(s_scm, i - 1)

            def prompt_topk(group):
                tiles = [(view("score", (i + 1) * P, sc_off[i]), best[:, 8 * i:8 * i + 8]) for i in group]
                with dve.Fori(0, TOPK // 8):
                    for sc, eight in tiles:
                        nc.vector.max(eight, sc)
                    nc.vector.drain()
                    for sc, eight in tiles:
                        nc.vector.match_replace(sc, eight, sc, TAKEN)
                    nc.vector.drain()
                for sc, eight in tiles:
                    nc.vector.tensor_scalar(sc, sc, -2e38, NEG, ALU.is_gt, ALU.mult).then_inc(s_topk, 1)

            for i in range(2, NT + 1):
                index_scores(i)
            prompt_topk(range(2, NT))

            dve.wait_ge(s_tod, 16)
            dve.wait_ge(s_scn, 16)
            dve.wait_ge(s_cs, 2)
            sc = scd[:, 0:SCORES]
            with dve.Fori(0, TOPK // 8) as it:
                nc.vector.max(m8, sc)
                nc.vector.drain()
                nc.vector.max_index(i8, m8, sc)
                nc.vector.tensor_copy(val[:, bass.ds(it * 8, 8)], m8)
                nc.vector.drain()
                nc.vector.match_replace(sc, m8, sc, TAKEN)
                nc.vector.tensor_copy(pos[:, bass.ds(it * 8, 8)], i8)
                nc.vector.drain()
            nc.vector.drain().then_inc(s_list, 1)

            rows = slice(0, SROWS)
            a_v, a_p, b_v, b_p = val[rows], pos[rows], reverse(val_b[rows]), reverse(pos_b[rows])
            lo_, pg, rf, tf = low[rows], page_of[rows], rows_f[rows], turn_f[rows]
            ia, ib = int_a[rows].bitcast(I32), int_b[rows].bitcast(I32)
            dve.wait_ge(s_move, 32)
            dve.wait_ge(s_rows, 16 * (2 + SB))
            link(nc.vector.tensor_tensor(lo_, a_v, b_v, ALU.is_ge))
            link(nc.vector.tensor_scalar(pg, b_p, float(HALF), None, ALU.add))
            link(nc.vector.tensor_tensor(a_p, a_p, pg, ALU.subtract))
            link(nc.vector.tensor_tensor(a_p, a_p, lo_, ALU.mult))
            link(nc.vector.tensor_tensor(a_p, a_p, pg, ALU.add))
            link(nc.vector.tensor_copy(ia, a_p))
            link(nc.vector.tensor_scalar(ib, ia, 7, None, ALU.logical_shift_right))
            link(nc.vector.tensor_copy(pg, ib))
            link(nc.vector.tensor_scalar(ib, ia, PAGE - 1, None, ALU.bitwise_and))
            link(nc.vector.tensor_copy(rf, ib))
            link(nc.vector.tensor_copy(ptab_f[rows], ptab_i[rows]))
            link(nc.vector.tensor_scalar(ptab_f[rows], ptab_f[rows], float(PAGE), None, ALU.mult))
            for j in range(NPAGES):
                link(nc.vector.tensor_scalar(lo_, pg, float(j), ptab_f[rows, j:j + 1], ALU.is_equal, ALU.mult))
                link(nc.vector.tensor_tensor(rf, rf, lo_, ALU.add))
            link(nc.vector.tensor_scalar(tf, a_p, -1.0, row_t[rows], ALU.mult, ALU.add))
            link(nc.vector.tensor_scalar(lo_, a_p, float(PAST), -1000.0, ALU.is_ge, ALU.mult))
            nc.vector.tensor_tensor(tf, tf, lo_, ALU.add).then_inc(s_pick, 1)
            own_hits = prod[rows, 0:ST * P].rearrange("p (t n) -> p t n", t=ST)
            dve.wait_ge(s_mm, 7 * TILES)
            link(nc.vector.tensor_scalar(a_p, a_p, row_new[rows], None, ALU.subtract))
            for c in range(2):
                for t in range(ST):
                    link(nc.vector.tensor_scalar(own_hits[:, t, :], a_p[:, c * P:(c + 1) * P], float(t), None, ALU.is_equal))
                link(nc.vector.tensor_reduce(sel_new[rows] if c == 0 else sel_new2[rows], own_hits, AX_X, ALU.add))
            link(nc.vector.tensor_tensor(sel_new[rows], sel_new[rows], sel_new2[rows], ALU.add))
            nm = new_mask[rows]
            nm3 = nm.rearrange("p (b t) -> p b t", b=SB)
            link(nc.vector.tensor_scalar(nm, own[rows, :], -1.0, None, ALU.is_ge))
            link(nc.vector.tensor_tensor(nm3, nm3, sel_new[rows].unsqueeze(1).to_broadcast([SROWS, SB, ST]), ALU.mult))
            nc.vector.tensor_scalar(nm, nm, -1.0, -NEG, ALU.add, ALU.mult).then_inc(s_pick, 1)
            dve.wait_ge(s_pickT, 1)
            nc.vector.tensor_copy(idxT, ps[:, 0, 0:P].rearrange("p (c r) -> p c r", c=2)).then_inc(s_idx, 1)
            link(nc.vector.tensor_copy(distT, ps[:, 0, P:2 * P]))
            link(nc.vector.tensor_copy(new_maskT[rows], ps[rows, 0, 2 * P:2 * P + SROWS]))
            nc.vector.drain().then_inc(s_nmT, 1)

            def sampled_bias():
                dve.wait_ge(s_db, 16 * 4)
                dve.wait_ge(s_b31, 16 * 9)
                nc.vector.tensor_scalar(reached, reached, first_of, None, ALU.is_ge)
                nc.vector.tensor_tensor(step_k, step_k, step_j, ALU.subtract).then_inc(s_ind, 1)
                link(nc.vector.tensor_scalar(reach, distT, 0.0, NEG, ALU.is_lt, ALU.mult))
                dve.wait_ge(s_sbT, 1)
                nc.vector.tensor_tensor(sbias.rearrange("p c (r h) -> p (c r) h", h=H),
                                        ps[:, 0:2, :].rearrange("p c (r h) -> p (c r) h", h=H),
                                        reach.unsqueeze(2).to_broadcast([P, P, H]), ALU.add).then_inc(s_sbe, 1)

            sampled_bias()

            def normalise(h):
                dve.wait_ge(s_pv, (h + 1) * (NT // 2))
                up, dn = ps[HD:P, 6:8, :].rearrange("p a n -> p (a n)"), ps[0:HD, 6:8, :].rearrange("p a n -> p (a n)")
                link(nc.vector.reciprocal(rl[0:HD, :], up))
                nc.vector.tensor_tensor(mixT[(h % 2) * HD:(h % 2 + 1) * HD, PAIRS + h // 2, 0:SEQ], dn, rl[0:HD, :], ALU.mult).then_inc(s_po, 1)
                dve.wait_ge(s_po, h + 1)

            dve.wait_ge(s_topk, NT - 2)
            m = 0
            for h in range(H):
                for i in range(NT):
                    n = (i + 1) * P
                    r = h * NT + i
                    dve.wait_ge(s_kg[r % 4], 32 * (r // 4 + 1))
                    dve.wait_ge(s_qr[r % 4], 16 * (r // 4 + 1))
                    if r:
                        dve.wait_ge(s_kd, r)
                    nc.vector.scalar_tensor_tensor(out=prod.rearrange("p (c n) -> p c n", c=2), in0=kv[:, r % 4, :].rearrange("p (c n) -> p c n", c=2),
                                                   scalar=HD ** -0.5, in1=qrow[:, r % 4, :].unsqueeze(1).to_broadcast([P, 2, W]),
                                                   op0=ALU.mult, op1=ALU.mult).then_inc(s_kp, 1)
                    dve.wait_ge(s_S, m + 1)
                    if m >= 2:
                        dve.wait_ge(s_T, turned_after(m - 2))
                    l = rb[:, m % 2, 0:n]
                    mask = causal if i == 0 else near_mask if i == 1 else view("score", n, sc_off[i])
                    src = ps[:, 2 * (m % 2):2 * (m % 2) + 2, :].rearrange("p a n -> p (a n)")[:, 0:n]
                    nc.vector.tensor_tensor_reduce(out=l, in0=src, in1=mask, scale=-1.0, scalar=3e38, op0=ALU.add, op1=ALU.min,
                                                   accum_out=neg_max[:, m % 2:m % 2 + 1]).then_inc(s_L, 1)
                    m += 1
                    dve.wait_ge(s_kp, r + 1)
                    nc.vector.tensor_reduce(lg[:, :, r * H:(r + 1) * H], prod.rearrange("p (c h d) -> p c h d", c=2, h=H),
                                            AX_X, ALU.add).then_inc(s_kd, 1)
                    if h and i == 1:
                        normalise(h - 1)
            normalise(H - 1)

            dve.wait_ge(s_kd, SROWS)
            link(nc.vector.tensor_tensor(lg, lg, sbias, ALU.add))
            l3 = ln[rows].rearrange("p (r h) -> p r h", h=H)
            dve.wait_ge(s_ln, 1)
            link(nc.vector.tensor_tensor(l3, l3, new_maskT[rows].unsqueeze(2).to_broadcast([SROWS, SROWS, H]), ALU.add))
            link(nc.vector.tensor_tensor(l3, l3, b31[rows].unsqueeze(1).to_broadcast([SROWS, SROWS, H]), ALU.add))
            dve.wait_ge(s_nbT, 1)
            l4 = ln[rows].rearrange("p (b q h) -> p b q h", b=SB, q=ST)
            nb = new_bias[rows].rearrange("p (h q) -> p q h", h=H)
            link(nc.vector.tensor_copy(new_bias[rows], ps[rows, 1, 0:SROWS]))
            link(nc.vector.tensor_tensor(l4, l4, nb.unsqueeze(1).to_broadcast([SROWS, SB, ST, H]), ALU.add))
            link(nc.vector.tensor_tensor(mx, lg[:, 0, :], lg[:, 1, :], ALU.max))
            nc.vector.tensor_tensor(mx[rows], mx[rows], ln[rows], ALU.max).then_inc(s_dg, 1)
            dve.wait_ge(s_mxT, 1)
            link(nc.vector.tensor_reduce(top_col, ps[:, 2, :].rearrange("p (k n) -> p k n", k=4), AX_X, ALU.max))
            for k in range(4):
                ins = nc.vector.tensor_scalar(diag[:, k * P:(k + 1) * P], ident, top_col[:, k:k + 1], None, ALU.mult)
            ins.then_inc(s_dg, 1)
            dve.wait_ge(s_mb, 1)
            for c in range(2):
                nc.vector.tensor_tensor(lg[:, c, :], lg[:, c, :], ps[:, 3, :], ALU.subtract).then_inc(s_lm, 1)
            nc.vector.tensor_tensor(ln[rows], ln[rows], ps[rows, 3, :], ALU.subtract).then_inc(s_lm, 1)
            dve.wait_ge(s_le, 1)
            link(nc.vector.tensor_tensor(mx, lg[:, 0, :], lg[:, 1, :], ALU.add))
            nc.vector.tensor_tensor(mx[rows], mx[rows], ln[rows], ALU.add).then_inc(s_ls, 1)
            dve.wait_ge(s_lb, 1)
            link(nc.vector.reciprocal(mx, ps[:, 2, :]))
            for c in range(2):
                nc.vector.tensor_tensor(lg[:, c, :], lg[:, c, :], mx, ALU.mult)
            nc.vector.tensor_tensor(ln[rows], ln[rows], mx[rows], ALU.mult).then_inc(s_pn, 1)
            def residual(t):
                r = rows_of(t)
                dve.wait_ge(s_mo, 2 * t + 2)
                dve.wait_ge(s_x2[t // NT], 16)
                src = (ps[0:r, 4:6, :] if t < NT else ps[0:r, 1:3, :]).rearrange("p a n -> p (a n)")
                nc.vector.tensor_tensor(hx[0:r, t, :], src, hx[0:r, t, :], ALU.add).then_inc(s_h, 1)

            def norm(t):
                r = rows_of(t)
                dve.wait_ge(s_root, TILES + t + 1)
                dve.wait_ge(s_hd, 16 * (t + 1))
                nc.vector.tensor_scalar(hx[0:r, t, :], hx[0:r, t, :], hr[0:r, t:t + 1], None, ALU.mult).then_inc(s_hn, 1)

            def gain2(t):
                r = rows_of(t)
                src = ps[:, 4 + 2 * (t % 2):6 + 2 * (t % 2), :].rearrange("p a (c t) -> p (a c) t", c=4)[:, :, 0:r]
                tok = slice(t * P, t * P + r)
                dve.wait_ge(s_hTr, t + 1)
                for c in range(KD):
                    ins = nc.vector.scalar_tensor_tensor(out=hT[1][c][:, tok], in0=src[:, c, :], scalar=g2[:, c:c + 1],
                                                         in1=hT[0][c][:, tok].bitcast(F32), op0=ALU.mult, op1=ALU.subtract)
                ins.then_inc(s_hT, 1)

            for t in range(NT):
                residual(t)
                if t:
                    norm(t - 1)
            norm(NT - 1)
            for t in range(NT // 2):
                gain2(t)
            dve.wait_ge(s_oh, 16)
            dve.wait_ge(s_nd, 1)
            nc.vector.tensor_tensor(sampled[rows], sampled[rows], ps[rows, 1, :], ALU.add).then_inc(s_os, 1)
            dve.wait_ge(s_oT, 1)
            nc.vector.tensor_copy(mixT[:, PAIRS:, SEQ:TOK], ps[:, 3, :].rearrange("p (c t) -> p c t", c=PAIRS)[:, :, 0:SROWS]).then_inc(s_oTe, 1)
            dve.wait_ge(s_stp, 1)
            nc.vector.tensor_copy(st, ps[:, 0, 0:NF * 2 * SB].rearrange("p (f s) -> p f s", f=NF)).then_inc(s_ste, 1)
            residual(NT)
            for t in range(NT // 2, NT):
                gain2(t)
            norm(NT)
            gain2(NT)

            def split_weights(f, w):
                dve.wait_ge(s_hi, f * 2 + (w + 1))
                nc.vector.tensor_tensor(w_parts[w][:, 1, :], raw[:, w, :], w_parts[w][:, 0, :].bitcast(F32), ALU.subtract).then_inc(s_sp, 1)

            split_weights(0, 0)
            split_weights(0, 1)

            def conv(f, last):
                dve.wait_ge(s_gc, f * 3 + 3)
                a = aT[:, bass.ds(f * TOK, SEQ)]
                a_s = aT[:, bass.ds(f * TOK + SEQ, SROWS)].rearrange("p (b t) -> p b t", b=SB)
                for j in (2, 1, 0):
                    w = cw[:, bass.ds(f + j * NF, 1)]
                    for out, src in ((a, gb_p[:, j:j + SEQ]), (a_s, gb_s[:, :, j:j + ST])):
                        if j == 2:
                            nc.vector.tensor_scalar(out, src, w, cb[:, bass.ds(f, 1)], ALU.mult, ALU.add)
                        else:
                            nc.vector.scalar_tensor_tensor(out=out, in0=src, scalar=w, in1=out, op0=ALU.mult, op1=ALU.add)
                    if j:
                        nc.vector.drain()
                nc.vector.drain().then_inc(s_cd2, 1)
                if not last:
                    split_weights(f + 1, 0)
                dve.wait_ge(s_si, f + 1)
                for g, (b, e) in enumerate(GROUPS):
                    dve.wait_ge(s_um, f * 3 + (g + 1))
                    o = aT[:, bass.ds(f * TOK + b, e - b)]
                    nc.vector.tensor_tensor(o, o, ps[:, 3 + g, 0:e - b], ALU.mult).then_inc(s_ag, 1)

                if not last:
                    split_weights(f + 1, 1)

            with dve.Fori(0, NF - 1) as f:
                conv(f, False)
            conv(NF - 1, True)

            def split_down(n, f, s, pieces, first=False, raw_slot=None, loads=0):
                dve.wait_ge(s_dh, n + 1)
                a, w = pieces
                nc.vector.tensor_tensor(d_parts[:, s, 1, :], d_raw[:, raw_slot, :], d_parts[:, s, 0, :].bitcast(F32), ALU.subtract)
                nc.vector.tensor_tensor(a_parts[:, s, 1, 0:w], aT[:, bass.ds(f * TOK + a, w)], a_parts[:, s, 0, 0:w].bitcast(F32),
                                        ALU.subtract).then_inc(s_ds, 1)

            def outputs(p):
                for t in range(3 * p, 3 * p + 3):
                    r = rows_of(t)
                    if t == 0:
                        dve.wait_ge(s_hl, 32)
                        dve.wait_ge(s_fg, 16)
                    dve.wait_ge(s_du, (p + 1) * NF)
                    for half in range(2):
                        o = y[0:r, t, half * 512:(half + 1) * 512]
                        nc.vector.tensor_tensor(o, o, ps[0:r, 2 * (t % 3) + half, :], ALU.add).then_inc(s_y, 1)
                for t in range(3 * p, 3 * p + 3):
                    r = rows_of(t)
                    dve.wait_ge(s_root, 2 * TILES + t + 1)
                    nc.vector.scalar_tensor_tensor(out=y[0:r, t, :], in0=y[0:r, t, :], scalar=yr[0:r, t:t + 1], in1=final_g[0:r, :],
                                                   op0=ALU.mult, op1=ALU.mult).then_inc(s_yn, 1)

            down_blocks(split_down, dve, outputs)

        @block.tensor
        def _(pe):
            pe.wait_ge(s_built, 1)
            pe.wait_ge(s_const, 16 * 7)
            nc.tensor.transpose(ps[:, 4, 0:112], rows_in[0:112, :], ident[0:112, 0:112]).then_inc(s_cps, 1)
            for t in range(TILES):
                r = rows_of(t)
                pe.wait_ge(s_xn, t + 1)
                if t >= 2:
                    pe.wait_ge(s_xT, t - 1)
                for c in range(KD):
                    o = ps[:, 2 * (t % 2) + c // 4, (c % 4) * P:(c % 4) * P + r]
                    ins = nc.tensor.transpose(o, xring[0:r, t % 3, c * P:(c + 1) * P], ident[0:r, 0:r])
                ins.then_inc(s_xTp, 1)

            def project_tile(c, t):
                n, r, width = n_of(c, t), rows_of(t), CHUNKS[c][2]
                pe.wait_ge(s_w[c % 2], 16 * (c // 2 + 1))
                pe.wait_ge(s_xT, t + 1)
                if n >= 2:
                    pe.wait_ge(s_z, n if FIRST_BETWEEN < n < AFTER else n - 1)
                if n == 0:
                    pe.wait_ge(s_col, 1)
                w = wring[:, c % 2, 0:KD * width].rearrange("p (k n) -> p k n", k=KD)
                for k in range(KD):
                    ins = nc.tensor.matmul(ps[0:r, bank_of(n), 0:width], xT[:, k, t * P:t * P + r], w[:, k, :],
                                           start=(k == 0), stop=(k == KD - 1))
                ins.then_inc(s_mm, 1)

            def transpose_z(job):
                c, t = job
                i = tjob_at[job]
                cc = 1 if c == "dup" else c
                n, r = n_of(cc, t), rows_of(t)
                pe.wait_ge(*((s_twice, 1) if c == "dup" else (s_z, n + 1)))
                if i >= 2:
                    pe.wait_ge(s_tev, i if i > 2 * TILES else i - 1)
                for b in range({0: 1, "dup": H}.get(c, PAIRS)):
                    if c == "dup":
                        src = twice[0:r, b * P:(b + 1) * P]
                        o = ps[:, turned_bank(i), b * SROWS:(b + 1) * SROWS]
                    else:
                        src = zr[0:r, n % 3, b * P:(b + 1) * P]
                        o = ps[:, turned_bank(i), b * P:b * P + r]
                    ins = nc.tensor.transpose(o, src, ident[0:r, 0:r])
                ins.then_inc(s_tz, 1)

            def index_dots(i):
                if i < 2:
                    return
                n, r, k0 = ((i + 1) * P, P, 0) if i < NT else (SROWS, SROWS, SEQ)
                pe.wait_ge(s_tev, tjob_at[(1, i)] + 1)
                for h in range(H):
                    m = (i - 2) * H + h
                    lo = (h % 2) * HD
                    if m >= 2:
                        pe.wait_ge(s_relu, m - 1)
                    for a in range(0, n, 512):
                        e = min(n, a + 512)
                        ins = nc.tensor.matmul(ps[0:r, 2 * (m % 2) + a // 512, 0:e - a],
                                               iqT[lo:lo + HD, h // 2, i * P:i * P + r],
                                               ikT[lo:lo + HD, k0 + a:k0 + e], start=True, stop=True)
                    ins.then_inc(s_dot, 1)

            run_items(range(TILES + 1), project_tile, transpose_z)
            nc.tensor.transpose(ps[0:H, 2, 0:SROWS], iw[0:SROWS, NT, :], ident[0:SROWS, 0:SROWS]).then_inc(s_iwp, 1)
            pe.wait_ge(s_iwT, 1)
            nc.tensor.matmul(ps[:, 2, SROWS:2 * SROWS], wrep[0:H, :], iwT[0:H, :], start=True, stop=True).then_inc(s_iwp, 1)
            pe.wait_ge(s_rel, 32)
            nc.tensor.matmul(ps[0:H, 3, 0:NEAR], relb[0:BUCKETS, :], hot[0:BUCKETS, :], start=True, stop=True).then_inc(s_toep, 1)
            pe.wait_ge(s_wd, 1)
            pe.wait_ge(s_toev, 1)
            run_items(range(TILES + 1, 2 * TILES), project_tile, transpose_z, index_dots)
            turn_last(2 * TILES - 1, transpose_z)
            index_dots(NT - 1)
            index_dots(NT)
            m = (NT - 1) * H
            pe.wait_ge(s_tev, 2 * TILES + 1)
            def turn_index_pages(un):
                slot = un % 2
                pe.wait_ge(s_ikc[slot], 16 * 16 * (un // 2 + 1))
                pe.wait_ge(*((s_cT, un) if un else (s_relu, m)))
                for j in range(8):
                    ins = nc.tensor.transpose(ps[:, j // 4, (j % 4) * P:(j % 4 + 1) * P],
                                              ikc[:, slot, j, :, :].rearrange("p e d -> p (e d)"), ident)
                ins.then_inc(s_ct, 1)

            turn_index_pages(0)
            for un in range(2 * SB):
                half, b = divmod(un, SB)
                if un == SB:
                    pe.wait_ge(s_cs, 1)
                if un + 1 < 2 * SB:
                    turn_index_pages(un + 1)
                pe.wait_ge(s_cT, un + 1)
                for r2 in range(2):
                    if un:
                        pe.wait_ge(s_cr, 2 * (un - 1) + r2 + 1)
                    for e in range(2):
                        r = slice(e * SROWS, (e + 1) * SROWS)
                        ins = nc.tensor.matmul(ps[r, 2 + r2, :], iqd[r, b, :], ikcT[r, un % 2, r2 * 512:(r2 + 1) * 512], start=True, stop=True)
                    ins.then_inc(s_cd, 1)
                for r2 in range(2):
                    pe.wait_ge(s_cr, 2 * un + r2 + 1)
                    nc.tensor.matmul(ps[:, 4 + r2, :], wd[:, b, :], rb4[:, r2, :], start=(b == 0), stop=(b == SB - 1),
                                     skip_group_check=True).then_inc(s_ch, 1)
                run_items(between[un], project_tile, transpose_z)
            pe.wait_ge(s_cs, 2)
            pe.wait_ge(s_ws, 16)
            for h in range(H):
                ins = nc.tensor.transpose(ps[:, h // 4, (h % 4) * P:(h % 4 + 1) * P], ws_in[:, h, :], ident)
            ins.then_inc(s_wsp, 1)
            run_items(range(AFTER, len(order)), project_tile, transpose_z)

            pe.wait_ge(s_vn, TILES)
            pe.wait_ge(s_wsd, 16 * 2 * SB)
            for h in range(H):
                c = slice(h * HD, (h + 1) * HD)
                pe.wait_ge(*((s_sb, h - 1) if h >= 2 else (s_wse, 1)))
                nc.tensor.matmul(ps[:, h % 2, :], wsT[:, h, :], vn[:, 0:NT, c], start=True, stop=True)
                nc.tensor.matmul(ps[0:SROWS, 2 + h % 2, 0:HD], wsd[0:SROWS, h, :], vn[0:SROWS, NT, c], start=True, stop=True).then_inc(s_sg, 1)
            pe.wait_ge(s_qbd, 2)
            for c in range(PAIRS):
                ins = nc.tensor.matmul(ps[0:SROWS, 5, :].rearrange("p (b c n) -> p b c n", b=SB, c=PAIRS)[:, :, c, :],
                                       kT[:, c, SEQ:TOK], qbd[:, :, c, :], start=True, stop=True)
            ins.then_inc(s_kn, 1)
            pe.wait_ge(s_au, H)
            for t in range(TILES):
                r = rows_of(t)
                if t >= 2:
                    pe.wait_ge(s_am, t - 1)
                for c in range(PAIRS):
                    ins = nc.tensor.transpose(ps[:, 6 + t % 2, c * P:c * P + r], u[0:r, t, c * P:(c + 1) * P], ident[0:r, 0:r])
                ins.then_inc(s_at, 1)

            pe.wait_ge(s_pick, 2)
            pe.wait_ge(s_am, TILES)
            for k, src in enumerate((rows_f, turn_f)):
                for c in range(2):
                    nc.tensor.transpose(ps[:, 0, k * P + c * SROWS:k * P + (c + 1) * SROWS], src[0:SROWS, c * P:(c + 1) * P],
                                        ident[0:SROWS, 0:SROWS])
            nc.tensor.transpose(ps[0:SROWS, 0, 2 * P:2 * P + SROWS], new_mask[0:SROWS, :], ident[0:SROWS, 0:SROWS]).then_inc(s_pickT, 1)
            pe.wait_ge(s_nmT, 1)
            pe.wait_ge(s_ind, 1)
            for a in range(SROWS // 4):
                for c in range(2):
                    ins = nc.tensor.matmul(ps[:, c, :].rearrange("p (g a h) -> p g a h", g=4, h=H)[:, :, a, :],
                                           reached[:, a * TOPK + c * P:a * TOPK + (c + 1) * P], step_k, start=True, stop=True)
            ins.then_inc(s_sbT, 1)
            pe.wait_ge(s_sbe, 1)

            def logits(m):
                h, i = divmod(m, NT)
                n, lo = (i + 1) * P, (h % 2) * HD
                if m >= 2:
                    pe.wait_ge(s_L, m - 1)
                near = max(n - 2 * P, 0)
                for a in range(0, n, 512):
                    e = min(n, a + 512)
                    o = ps[:, 2 * (m % 2) + a // 512, :]
                    nc.tensor.matmul(o[:, 0:e - a], qT[lo:lo + HD, h // 2, i * P:(i + 1) * P], kT[lo:lo + HD, h // 2, a:e],
                                     start=True, stop=True)
                for a in range(0, n, 512):
                    c, e = max(a, near), min(n, a + 512)
                    if c < e:
                        first = c - (n - 2 * P)
                        ins = nc.tensor.matmul(ps[:, 2 * (m % 2) + a // 512, c - a:e - a], ident, bn[:, h, first:first + e - c],
                                               start=False, stop=True, skip_group_check=True)
                ins.then_inc(s_S, 1)

            def head_values(h, i):
                if i == 1:
                    pe.wait_ge(s_vo[h % 2], 16 * (h // 2 + 1))
                    if h:
                        pe.wait_ge(s_po, h)
                pe.wait_ge(s_Te, turned_after(h * NT + i))
                for k in range(i + 1):
                    a, e = max(i - 1, k) * P, (i + 1) * P
                    ins = nc.tensor.matmul(ps[:, 6 + a // 512, a % 512:a % 512 + e - a], vone[:, h % 2, k, :], pT[:, k, a:e],
                                           start=(k == 0), stop=(k == i), skip_group_check=True)
                ins.then_inc(s_pv, 1)

            g = 0
            pe.wait_ge(s_bn, 16)
            pe.wait_ge(s_built, 5)
            logits(0)
            for m in range(H * NT):
                h, i = divmod(m, NT)
                if m + 1 < H * NT:
                    logits(m + 1)
                pe.wait_ge(s_E, m + 1)
                for blocks in probs_groups(i):
                    if g >= 2:
                        pe.wait_ge(s_Te, g - 1)
                    for k in blocks:
                        ins = nc.tensor.transpose(ps[:, 4 + g % 2, (k % 4) * P:(k % 4 + 1) * P], rb[:, m % 2, k * P:(k + 1) * P], ident)
                    ins.then_inc(s_T, 1)
                    g += 1
                if m and i % 2 == 0:
                    head_values(*((h, i - 1) if i else (h - 1, NT - 1)))
            head_values(H - 1, NT - 1)

            pe.wait_ge(s_nbs, 1)
            for h in range(H):
                ins = nc.tensor.transpose(ps[0:SROWS, 1, h * ST:(h + 1) * ST], own_near(h), ident[0:ST, 0:ST])
            ins.then_inc(s_nbT, 1)
            pe.wait_ge(s_dg, 1)
            for k in range(4):
                ins = nc.tensor.transpose(ps[:, 2, k * P:(k + 1) * P], mx[:, k * P:(k + 1) * P], ident)
            ins.then_inc(s_mxT, 1)
            pe.wait_ge(s_dg, 2)
            nc.tensor.matmul(ps[:, 3, :], ones, diag, start=True, stop=True).then_inc(s_mb, 1)
            pe.wait_ge(s_ls, 1)
            nc.tensor.matmul(ps[:, 2, :], ones, mx, start=True, stop=True).then_inc(s_lb, 1)
            pe.wait_ge(s_pn, 1)
            pe.wait_ge(s_vnl, 16)
            for h in range(H):
                ins = nc.tensor.matmul(ps[0:SROWS, 1, h * HD:(h + 1) * HD], ln[0:SROWS, :].rearrange("p (r h) -> p r h", h=H)[:, :, h],
                                       own_v[0:SROWS, h * HD:(h + 1) * HD], start=True, stop=True)
            ins.then_inc(s_nd, 1)
            def out_products(t, half, bank):
                r = rows_of(t)
                if 0 < t < NT and half == 0:
                    pe.wait_ge(s_h, t)
                pe.wait_ge(s_wo[half], 16)
                for k in range(KD):
                    ins = nc.tensor.matmul(ps[0:r, bank + half, :], mixT[:, k, t * P:t * P + r],
                                           wo[:, k, half * 512:(half + 1) * 512], start=(k == 0), stop=(k == KD - 1))
                ins.then_inc(s_mo, 1)

            def turn_residual(t):
                r = rows_of(t)
                pe.wait_ge(s_hn, t + 1)
                pe.wait_ge(*((s_hT, t - 1) if t >= 2 else (s_h, NT)))
                for c in range(KD):
                    ins = nc.tensor.transpose(ps[:, 4 + 2 * (t % 2) + c // 4, (c % 4) * P:(c % 4) * P + r], hx[0:r, t, c * P:(c + 1) * P],
                                              ident[0:r, 0:r])
                ins.then_inc(s_hp, 1)

            pe.wait_ge(s_po, H)
            for g in range(SROWS // 4):
                pe.wait_ge(s_kg[g % 2], 32 * SROWS // 4 + 128 * (g // 2 + 1))
                if g >= 2:
                    pe.wait_ge(s_ve, g - 1)
                for c in range(2):
                    for j in range(4):
                        r = 4 * g + j
                        ins = nc.tensor.matmul(ps[32 * j:32 * j + H, 2 * (g % 2), :], lg[:, c, r * H:(r + 1) * H],
                                               v_rows[4 * (g % 2) + j][:, c * W:(c + 1) * W], start=(c == 0), stop=(c == 1))
                ins.then_inc(s_vd, 1)
                out_products(g // 2, g % 2, 4)
            for t in range(NT // 2):
                turn_residual(t)
            pe.wait_ge(s_os, 1)
            for c in range(PAIRS):
                ins = nc.tensor.transpose(ps[:, 3, c * P:c * P + SROWS], sampled[0:SROWS, c * P:(c + 1) * P], ident[0:SROWS, 0:SROWS])
            ins.then_inc(s_oT, 1)
            pe.wait_ge(s_st, 16)
            pe.wait_ge(s_ve, SROWS // 4)
            for f in range(NF):
                ins = nc.tensor.transpose(ps[:, 0, f * 2 * SB:(f + 1) * 2 * SB], state_rows[0:2 * SB, f * P:(f + 1) * P],
                                          ident[0:2 * SB, 0:2 * SB])
            ins.then_inc(s_stp, 1)
            pe.wait_ge(s_oTe, 1)
            out_products(NT, 0, 1)
            out_products(NT, 1, 1)
            for t in range(NT // 2, TILES):
                turn_residual(t)
            def ffn_block(f, first=False):
                for w, done in ((0, s_gm), (1, s_um)):
                    pe.wait_ge(s_sp, f * 2 + (w + 1))
                    for g, (a, e) in enumerate(GROUPS):
                        if not first:
                            pe.wait_ge((s_gc, s_ag)[w], f * 3 + (g - 2))
                        for k in range(KD):
                            for n, (i, j) in enumerate(((0, 0), (0, 1), (1, 0))):
                                ins = nc.tensor.matmul(ps[:, 3 * w + g, 0:e - a], w_parts[w][:, i, k * P:(k + 1) * P], hT[j][k][:, a:e],
                                                       start=(k + n == 0), stop=(k + n == KD + 1))
                        ins.then_inc(done, 1)

            pe.wait_ge(s_hT, TILES)
            ffn_block(0, True)
            with pe.Fori(1, NF) as f:
                ffn_block(f)

            pe.wait_ge(s_gst, NF + 1)
            pe.wait_ge(s_ag, 3 * NF)
            for f in range(NF):
                bank, c = divmod(f, 4) if f < 14 else (4 + (f - 14) // 4, (f - 14) % 4)
                ins = nc.tensor.transpose(ps[0:2 + 2 * SB, bank, c * P:(c + 1) * P], cs[:, f, :], ident)
            ins.then_inc(s_cst, 1)

            pe.wait_ge(s_cse, 2)

            def down(n, f, s, pieces, first=False, raw_slot=None, loads=0):
                p = pieces[0] // (3 * P)
                pe.wait_ge(s_ds, n + 1)
                start, stop = isinstance(f, int) and f == 0, isinstance(f, int) and f == NF - 1
                for j in range(3):
                    t = 3 * p + j
                    r = rows_of(t)
                    if start and p:
                        pe.wait_ge(s_y, 6 * (p - 1) + 2 * j + 2)
                    for half in range(2):
                        for q, (x, y) in enumerate(((0, 0), (0, 1), (1, 0))):
                            ins = nc.tensor.matmul(ps[0:r, 2 * j + half, :], a_parts[:, s, x, j * P:j * P + r],
                                                   d_parts[:, s, y, half * 512:(half + 1) * 512],
                                                   start=start and q == 0, stop=stop and q == 2)
                ins.then_inc(s_du, 1)

            down_blocks(down, pe, lambda p: None)


OUTS = [("y_p", (1, SEQ, D)), ("y_s", (SB, ST, D)), ("k_p", (1, 1, SEQ, H, HD)), ("v_p", (1, 1, SEQ, H, HD)),
        ("idx_k_p", (1, 1, SEQ, HD)), ("conv_p", (1, 1, 2, DFF)), ("k_s", (1, SB, ST, H, HD)),
        ("v_s", (1, SB, ST, H, HD)), ("idx_k_s", (1, SB, ST, HD)), ("conv_s", (1, SB, 2, DFF)),
        ("chunk_v_s", (1, SB, ST, H, HD))]


def constants():
    rep = np.zeros((H, P), np.float32)
    sel = np.zeros((P, ST), np.float32)
    for c in range(P):
        rep[(c // ST) % H, c] = 1.0
        sel[c, c % ST] = 1.0
    hot = np.zeros((BUCKETS, NEAR), np.float32)
    for y in range(NEAR):
        hot[BUCKET_OF[max(2 * P - 1 - y, 0)], y] = 1.0
    first = np.array([[FIRST_OF[k]] for _ in range(P // BUCKETS) for k in range(BUCKETS)], np.float32)
    rows = np.zeros((SROWS, 2), np.float32)
    for r in range(SROWS):
        rows[r] = (PAST + r % ST, PAST + r // ST * ST)
    return {"c_rep": rep, "c_sel": sel, "c_hot": hot, "c_rows": rows, "c_first": first}


def kernel(**inputs):
    import concourse.bacc as bacc
    from concourse.bass_utils import run_bass_kernel_spmd as run

    nc = bacc.Bacc("TRN2", target_bir_lowering=False, num_devices=1)
    arrays, io = {}, {}
    for name, a in list(inputs.items()) + list(constants().items()):
        a = np.ascontiguousarray(a)
        arrays["in_" + name] = a
        io[name] = nc.dram_tensor("in_" + name, a.shape, mybir.dt.from_np(a.dtype), kind="ExternalInput").ap()
    for name, shape in OUTS:
        io[name] = nc.dram_tensor("out_" + name, shape, F32, kind="ExternalOutput").ap()
    io["pool"] = inputs["cache_k"].shape[1]
    program(nc, io)
    r = run(nc, [arrays], core_ids=[0])
    return tuple(r.results[0]["out_" + name] for name, _ in OUTS)
```
